# Optimizing a Trainium2 kernel written in Bass

```python
import jax
import jax.numpy as jnp
from jax import lax
import numpy as np

D_MODEL = 1024
BATCH = 1
SEQ = 512
DEPTH = 1

MEM_LEN = 256
N_ATT_HEADS = 8
ATT_HEAD_DIM = 64
ATT_WIDTH = N_ATT_HEADS * ATT_HEAD_DIM
N_RWKV_HEADS = 8
RWKV_HEAD_DIM = 64
RWKV_WIDTH = N_RWKV_HEADS * RWKV_HEAD_DIM
MIX_WIDTH = ATT_WIDTH + RWKV_WIDTH
MOBA_BLOCK = 256
MOBA_TOP_BLOCKS = 3
MOBA_Q_CHUNK = 16
DECAY_LORA = 64
ICLR_LORA = 64
VRES_LORA = 32
GATE_LORA = 128
RWKV_GN_EPS = 64e-5
N_MEM_HEADS = 4
MEM_HEAD_DIM = D_MODEL // N_MEM_HEADS
N_EXPERTS = 32
N_EXPERT_GROUPS = 8
EXPERTS_PER_GROUP = N_EXPERTS // N_EXPERT_GROUPS
TOP_K = 2
D_EXPERT = 512
MOE_ROW_BLOCK = 128
LN_EPS = 1e-5
RMS_EPS = 1e-6
NEG_INF = -1e30
DEEPNORM_ALPHA = (2 * DEPTH) ** 0.25
DEEPNORM_BETA = (8 * DEPTH) ** -0.25
SHIFT_COLS = 3 * RWKV_WIDTH + DECAY_LORA + ICLR_LORA + GATE_LORA
IN_COLS = 3 * ATT_WIDTH + SHIFT_COLS
RWKV_SPLITS = (RWKV_WIDTH, 2 * RWKV_WIDTH, 3 * RWKV_WIDTH, 3 * RWKV_WIDTH + DECAY_LORA, 3 * RWKV_WIDTH + DECAY_LORA + ICLR_LORA)

kernel_name = 'hybrid_moba_rwkv7_moe_deepnorm'

def layer_norm(x, g, b):
    xf = x.astype(jnp.float32)
    mu = jnp.mean(xf, -1, keepdims=True)
    var = jnp.mean(jnp.square(xf - mu), -1, keepdims=True)
    return ((xf - mu) * lax.rsqrt(var + LN_EPS) * g + b).astype(x.dtype)

def alibi_slopes(n_heads):
    return 2.0 ** (-8.0 * jnp.arange(1, n_heads + 1, dtype=jnp.float32) / n_heads)

def token_shift(z):
    return jnp.pad(z, ((0, 0), (1, 0), (0, 0)))[:, :-1]

def moba_attention(q, k, v):
    B, S, H, hd = q.shape
    nb = -(-S // MOBA_BLOCK)
    s_pad = nb * MOBA_BLOCK
    ksel = max(1, min(MOBA_TOP_BLOCKS, nb - 1))
    pad = ((0, 0), (0, 0), (0, s_pad - S), (0, 0))
    qh = jnp.pad(q.transpose(0, 2, 1, 3), pad) * hd ** -0.5
    kh = jnp.pad(k.transpose(0, 2, 1, 3), pad)
    vh = jnp.pad(v.transpose(0, 2, 1, 3), pad)
    kb = kh.reshape(B, H, nb, MOBA_BLOCK, hd)
    vb = vh.reshape(B, H, nb, MOBA_BLOCK, hd)
    kmean = jnp.mean(kb, axis=3)
    slopes = alibi_slopes(H)[None, :, None, None]
    bi = jnp.arange(B)[:, None, None, None]
    hi = jnp.arange(H)[None, :, None, None]
    blk_ids = jnp.arange(nb)
    offs = jnp.arange(MOBA_BLOCK)
    n_sel = ksel * MOBA_BLOCK

    def chunk(start):
        cur = start // MOBA_BLOCK
        pos_q = start + jnp.arange(MOBA_Q_CHUNK)
        qc = lax.dynamic_slice(qh, (0, 0, start, 0), (B, H, MOBA_Q_CHUNK, hd))
        gate = jnp.einsum('bhqd,bhnd->bhqn', qc, kmean)
        gate = jnp.where(blk_ids < cur, gate, NEG_INF)
        _, idx = lax.top_k(gate, ksel)
        valid = jnp.arange(ksel) < cur
        k_sel = kb[bi, hi, idx]
        v_sel = vb[bi, hi, idx]
        s_sel = jnp.einsum('bhqd,bhqnld->bhqnl', qc, k_sel)
        dist_sel = pos_q[:, None, None] - (idx[..., None] * MOBA_BLOCK + offs)
        s_sel = jnp.where(valid[:, None], s_sel - slopes[..., None] * dist_sel, NEG_INF)
        k_own = lax.dynamic_slice(kh, (0, 0, cur * MOBA_BLOCK, 0), (B, H, MOBA_BLOCK, hd))
        v_own = lax.dynamic_slice(vh, (0, 0, cur * MOBA_BLOCK, 0), (B, H, MOBA_BLOCK, hd))
        dist_own = pos_q[:, None] - (cur * MOBA_BLOCK + offs)[None, :]
        s_own = jnp.einsum('bhqd,bhld->bhql', qc, k_own)
        s_own = jnp.where(dist_own >= 0, s_own - slopes * dist_own, NEG_INF)
        logits = jnp.concatenate([s_sel.reshape(B, H, MOBA_Q_CHUNK, n_sel), s_own], axis=-1)
        p = jax.nn.softmax(logits, axis=-1)
        p_sel = p[..., :n_sel].reshape(B, H, MOBA_Q_CHUNK, ksel, MOBA_BLOCK)
        p_own = p[..., n_sel:]
        return (jnp.einsum('bhqnl,bhqnld->bhqd', p_sel, v_sel)
                + jnp.einsum('bhql,bhld->bhqd', p_own, v_own))

    starts = jnp.arange(0, s_pad, MOBA_Q_CHUNK)
    out = lax.map(chunk, starts)
    out = out.transpose(1, 2, 0, 3, 4).reshape(B, H, s_pad, hd)[:, :, :S]
    return out.transpose(0, 2, 1, 3)

def rwkv7_recurrence(r, w, k, v, a, b):
    B, S, H, hd = r.shape

    def step(state, inp):
        r_t, w_t, k_t, v_t, a_t, b_t = inp
        sa = jnp.einsum('bhij,bhj->bhi', state, a_t)
        state = (state * w_t[:, :, None, :] + sa[..., None] * b_t[:, :, None, :]
                 + v_t[..., None] * k_t[:, :, None, :])
        return state, jnp.einsum('bhij,bhj->bhi', state, r_t)

    xs = tuple(t.transpose(1, 0, 2, 3) for t in (r, w, k, v, a, b))
    _, y = lax.scan(step, jnp.zeros((B, H, hd, hd), jnp.float32), xs)
    return y.transpose(1, 0, 2, 3)

def rwkv7_time_mix(r, k, v, zw, za, zg, w0, w_decay_up, a0, w_iclr_up, w_gate_up,
                   k_k, k_a, r_k, lnx_g, lnx_b):
    B, S, _ = r.shape
    H, hd = N_RWKV_HEADS, RWKV_HEAD_DIM
    log_w = -jax.nn.softplus(-(w0 + jnp.tanh(zw) @ w_decay_up)) - 0.5
    decay = jnp.exp(-jnp.exp(log_w))
    a = jax.nn.sigmoid(a0 + za @ w_iclr_up)
    g = jax.nn.sigmoid(zg) @ w_gate_up
    heads = lambda t: t.reshape(B, S, H, hd)
    kk = heads(k * k_k)
    kk = kk * lax.rsqrt(jnp.maximum(jnp.sum(kk * kk, -1, keepdims=True), 1e-24))
    k = heads(k * (1.0 + (a - 1.0) * k_a))
    r, v, a = heads(r), heads(v), heads(a)
    y = rwkv7_recurrence(r, heads(decay), k, v, -kk, kk * a)
    mu = jnp.mean(y, -1, keepdims=True)
    var = jnp.mean(jnp.square(y - mu), -1, keepdims=True)
    y = ((y - mu) * lax.rsqrt(var + RWKV_GN_EPS)).reshape(B, S, RWKV_WIDTH) * lnx_g + lnx_b
    bonus = (jnp.sum(r * k * r_k, -1, keepdims=True) * v).reshape(B, S, RWKV_WIDTH)
    return (y + bonus) * g

def memory_cross_attention(x, mem, w_q, w_kv, w_o):
    B, S, D = x.shape
    q = (x @ w_q).reshape(B, S, N_MEM_HEADS, MEM_HEAD_DIM).astype(jnp.float32)
    kv = (mem @ w_kv).reshape(B, mem.shape[1], 2, N_MEM_HEADS, MEM_HEAD_DIM).astype(jnp.float32)
    s = jnp.einsum('bshd,bmhd->bhsm', q, kv[:, :, 0]) * MEM_HEAD_DIM ** -0.5
    p = jax.nn.softmax(s, axis=-1)
    o = jnp.einsum('bhsm,bmhd->bshd', p, kv[:, :, 1]).reshape(B, S, D).astype(x.dtype)
    return o @ w_o

def route(xf, w_router, b_router):
    s = jax.nn.sigmoid((xf @ w_router).astype(jnp.float32))
    sel = s + b_router.astype(jnp.float32)
    grp = jnp.sum(lax.top_k(sel.reshape(-1, N_EXPERT_GROUPS, EXPERTS_PER_GROUP), 2)[0], -1)
    g_best = jnp.argmax(grp, axis=-1)
    in_grp = (jnp.arange(N_EXPERTS) // EXPERTS_PER_GROUP)[None, :] == g_best[:, None]
    _, e_idx = lax.top_k(jnp.where(in_grp, sel, NEG_INF), TOP_K)
    w = jnp.take_along_axis(s, e_idx, axis=-1)
    return e_idx, w / jnp.sum(w, -1, keepdims=True)

def moe_ffn(xf, e_idx, gate, w_gate, w_up, w_down):
    N, D = xf.shape
    A = N * TOP_K
    eid = e_idx.reshape(-1)
    tok = jnp.repeat(jnp.arange(N), TOP_K)
    gt = gate.reshape(-1)
    order = jnp.argsort(eid)
    eid_s, tok_s, gt_s = eid[order], tok[order], gt[order]
    counts = jnp.bincount(eid, length=N_EXPERTS)
    off = jnp.cumsum(counts) - counts
    pcounts = (counts + MOE_ROW_BLOCK - 1) // MOE_ROW_BLOCK * MOE_ROW_BLOCK
    pend = jnp.cumsum(pcounts)
    poff = pend - pcounts
    dest = poff[eid_s] + (jnp.arange(A) - off[eid_s])
    M = A + N_EXPERTS * MOE_ROW_BLOCK
    n_blk = M // MOE_ROW_BLOCK
    row_tok = jnp.full((M,), N, jnp.int32).at[dest].set(tok_s.astype(jnp.int32))
    row_gate = jnp.zeros((M,), xf.dtype).at[dest].set(gt_s)
    blk_expert = jnp.minimum(jnp.searchsorted(pend, jnp.arange(n_blk) * MOE_ROW_BLOCK, side='right'), N_EXPERTS - 1)
    x_rows = jnp.concatenate([xf, jnp.zeros((1, D), xf.dtype)], 0)[row_tok]
    x_rows = x_rows.reshape(n_blk, MOE_ROW_BLOCK, D)

    def expert_block(args):
        xb, e = args
        h = jax.nn.silu(xb @ w_gate[e]) * (xb @ w_up[e])
        return h @ w_down[e]

    y = lax.map(expert_block, (x_rows, blk_expert)).reshape(M, D)
    return jax.ops.segment_sum(y * row_gate[:, None], row_tok, num_segments=N + 1)[:N]

def setup_inputs(seed: int = 0) -> dict:
    key = jax.random.key(seed)
    ks = iter(jax.random.split(key, 40))
    f32 = jnp.float32

    def nrm(shape, scale):
        return jax.random.normal(next(ks), shape, f32) * scale

    def unif(shape, lo, hi):
        return jax.random.uniform(next(ks), shape, f32, lo, hi)

    beta = DEEPNORM_BETA
    rv = 3 * ATT_WIDTH + 2 * RWKV_WIDTH
    col_scale = (jnp.ones((IN_COLS,), f32).at[2 * ATT_WIDTH:3 * ATT_WIDTH].set(beta)
                 .at[rv:rv + RWKV_WIDTH].set(beta))
    kv_scale = jnp.concatenate([jnp.ones((D_MODEL,), f32), jnp.full((D_MODEL,), beta, f32)])
    dm1 = max(DEPTH - 1, 0)
    return {
        'x': nrm((BATCH, SEQ, D_MODEL), 1.0),
        'mem': nrm((BATCH, MEM_LEN, D_MODEL), 1.0),
        'w_in': nrm((DEPTH, D_MODEL, IN_COLS), D_MODEL ** -0.5) * col_scale,
        'w_in_vres': nrm((dm1, D_MODEL, VRES_LORA), D_MODEL ** -0.5),
        'mu_shift': unif((DEPTH, SHIFT_COLS), 0.0, 1.0),
        'mu_vres': unif((dm1, VRES_LORA), 0.0, 1.0),
        'w0': unif((DEPTH, RWKV_WIDTH), -3.0, 0.0),
        'w_decay_up': nrm((DEPTH, DECAY_LORA, RWKV_WIDTH), 0.5 * DECAY_LORA ** -0.5),
        'a0': nrm((DEPTH, RWKV_WIDTH), 0.1),
        'w_iclr_up': nrm((DEPTH, ICLR_LORA, RWKV_WIDTH), ICLR_LORA ** -0.5),
        'v0': nrm((dm1, RWKV_WIDTH), 0.1),
        'w_vres_up': nrm((dm1, VRES_LORA, RWKV_WIDTH), VRES_LORA ** -0.5),
        'w_gate_up': nrm((DEPTH, GATE_LORA, RWKV_WIDTH), GATE_LORA ** -0.5),
        'k_k': 0.85 + nrm((DEPTH, RWKV_WIDTH), 0.05),
        'k_a': 1.0 + nrm((DEPTH, RWKV_WIDTH), 0.05),
        'r_k': nrm((DEPTH, N_RWKV_HEADS, RWKV_HEAD_DIM), 0.1),
        'lnx_g': 1.0 + nrm((DEPTH, RWKV_WIDTH), 0.05),
        'lnx_b': nrm((DEPTH, RWKV_WIDTH), 0.02),
        'attn_out_g': 1.0 + nrm((DEPTH, ATT_WIDTH), 0.05),
        'w_out': nrm((DEPTH, MIX_WIDTH, D_MODEL), beta * MIX_WIDTH ** -0.5),
        'w_mem_q': nrm((DEPTH, D_MODEL, D_MODEL), D_MODEL ** -0.5),
        'w_mem_kv': nrm((DEPTH, D_MODEL, 2 * D_MODEL), D_MODEL ** -0.5) * kv_scale,
        'w_mem_o': nrm((DEPTH, D_MODEL, D_MODEL), beta * D_MODEL ** -0.5),
        'w_router': nrm((D_MODEL, N_EXPERTS), D_MODEL ** -0.5),
        'b_router': nrm((N_EXPERTS,), 0.01),
        'w_exp_gate': nrm((DEPTH, N_EXPERTS, D_MODEL, D_EXPERT), D_MODEL ** -0.5),
        'w_exp_up': nrm((DEPTH, N_EXPERTS, D_MODEL, D_EXPERT), D_MODEL ** -0.5),
        'w_exp_down': nrm((DEPTH, N_EXPERTS, D_EXPERT, D_MODEL), beta * D_EXPERT ** -0.5),
        'ln_g': 1.0 + nrm((DEPTH, 3, D_MODEL), 0.05),
        'ln_b': nrm((DEPTH, 3, D_MODEL), 0.02),
    }

def reference(x, mem, w_in, w_in_vres, mu_shift, mu_vres, w0, w_decay_up, a0, w_iclr_up,
              v0, w_vres_up, w_gate_up, k_k, k_a, r_k, lnx_g, lnx_b, attn_out_g, w_out,
              w_mem_q, w_mem_kv, w_mem_o, w_router, b_router, w_exp_gate, w_exp_up,
              w_exp_down, ln_g, ln_b):
    B, S, D = x.shape
    f32 = jnp.float32
    v_first = None
    for l in range(DEPTH):
        w_comb = w_in[l] if l == 0 else jnp.concatenate([w_in[l], w_in_vres[l - 1]], axis=1)
        z = x @ w_comb
        att = z[..., :3 * ATT_WIDTH].astype(f32).reshape(B, S, 3, N_ATT_HEADS, ATT_HEAD_DIM)
        o_att = moba_attention(att[:, :, 0], att[:, :, 1], att[:, :, 2])
        o_att = (o_att * lax.rsqrt(jnp.mean(o_att * o_att, -1, keepdims=True) + RMS_EPS)
                 * attn_out_g[l].reshape(N_ATT_HEADS, ATT_HEAD_DIM)).reshape(B, S, ATT_WIDTH)
        zs = z[..., 3 * ATT_WIDTH:3 * ATT_WIDTH + SHIFT_COLS].astype(f32)
        zs = zs + (token_shift(zs) - zs) * mu_shift[l]
        r, kr, vr, zw, za, zg = jnp.split(zs, RWKV_SPLITS, axis=-1)
        if l == 0:
            v_first = vr
        else:
            zv = z[..., 3 * ATT_WIDTH + SHIFT_COLS:].astype(f32)
            zv = zv + (token_shift(zv) - zv) * mu_vres[l - 1]
            vr = vr + (v_first - vr) * jax.nn.sigmoid(v0[l - 1] + zv @ w_vres_up[l - 1])
        o_rwkv = rwkv7_time_mix(r, kr, vr, zw, za, zg, w0[l], w_decay_up[l], a0[l], w_iclr_up[l],
                                w_gate_up[l], k_k[l], k_a[l], r_k[l], lnx_g[l], lnx_b[l])
        mix = jnp.concatenate([o_att, o_rwkv], axis=-1).astype(x.dtype)
        x = layer_norm(DEEPNORM_ALPHA * x + mix @ w_out[l], ln_g[l, 0], ln_b[l, 0])
        x = layer_norm(DEEPNORM_ALPHA * x + memory_cross_attention(x, mem, w_mem_q[l], w_mem_kv[l], w_mem_o[l]),
                       ln_g[l, 1], ln_b[l, 1])
        xf = x.reshape(B * S, D)
        e_idx, gate = route(xf, w_router, b_router)
        y = moe_ffn(xf, e_idx, gate.astype(x.dtype), w_exp_gate[l], w_exp_up[l], w_exp_down[l])
        x = layer_norm(DEEPNORM_ALPHA * x + y.reshape(B, S, D), ln_g[l, 2], ln_b[l, 2])
    return x


_drawn_inputs = setup_inputs


def setup_inputs(seed=0):
    import zlib

    import numpy as np

    out = dict(_drawn_inputs(seed))
    spreads = {}
    factors = {'lnx_b': 3.293, 'a0': 3.931, 'k_k': 2.723, 'lnx_g': 2.779}
    for name, (base, spread) in spreads.items():
        noise = np.random.default_rng([zlib.crc32(name.encode()), seed]).standard_normal(out[name].shape)
        drawn = base * np.exp(spread * noise) if base else spread * noise
        out[name] = jnp.asarray(drawn.astype(out[name].dtype))
    for name, factor in factors.items():
        out[name] = (out[name] * factor).astype(out[name].dtype)
    return out
```

```python
from contextlib import ExitStack

import concourse.bass as bass
from concourse import mybir

ALU = mybir.AluOpType
ACT = mybir.ActivationFunctionType
F32 = mybir.dt.float32
I32 = mybir.dt.int32
U32 = mybir.dt.uint32
AX_X = mybir.AxisListType.X

P = 128
S = 512
D = 1024
KT = D // P
NT = S // P
MEM = 256
MT = MEM // P
H = 8
HD = 64
W = H * HD
NJ = W // P
CH = 64
NC = S // CH
MH = 4
MHD = D // MH
NE = 32
NGRP = 8
EPG = NE // NGRP
DE = 512
FT = DE // P
CAP = 64
TOP_K = 2
OFF = 1 << 20
NEG = -1e30
LN_EPS = 1e-5
RMS_EPS = 1e-6
GN_EPS = 64e-5
ALPHA = 2.0 ** 0.25
DECAY = 0.6065306597126334
ATT0 = 3 * W
SLOT = KT * 512

ROWS = {}
_n = 0
for _name, _k in (("mu", 14), ("w0", 4), ("a0", 4), ("k_k", 4), ("k_a", 4), ("r_k", 4),
                  ("lnx_g", 4), ("lnx_b", 4), ("attn_out_g", 4)):
    ROWS[_name] = (_n, _k)
    _n += _k
NROWS = _n


def hybrid_decoder_trunk(nc, x, mem, w_in, mu_shift, w0, w_decay_up, a0, w_iclr_up, w_gate_up, k_k, k_a,
                         r_k, lnx_g, lnx_b, attn_out_g, w_out, w_mem_q, w_mem_kv, w_mem_o, w_router,
                         b_router, w_exp_gate, w_exp_up, w_exp_down, ln_g, ln_b, out, stop=99):
    ctx = ExitStack()
    with ctx:
        def sb(name, shape, dt=F32):
            return ctx.enter_context(nc.sbuf_tensor(name, shape, dt))

        def sem(name):
            return ctx.enter_context(nc.semaphore(name))

        part_sems = []

        def part_sem(name):
            part_sems.append(nc.alloc_semaphore(name=name))
            return part_sems[-1]

        dve_step, act_step, pool_step = sem("dve_step"), sem("act_step"), sem("pool_step")
        steps = {"dve": 0, "act": 0, "pool": 0}

        def link(eng, ins):
            name, step = {id(nc.vector): ("dve", dve_step), id(nc.scalar): ("act", act_step),
                          id(nc.gpsimd): ("pool", pool_step)}[id(eng)]
            steps[name] += 1
            ins.then_inc(step, 1)
            eng.wait_ge(step, steps[name])

        bank = [ctx.enter_context(nc.psum_tensor(f"bank{i}", [P, 512], F32)) for i in range(8)]

        ident = sb("ident", [P, P])
        blkones = sb("blkones", [P, P])
        cols = sb("cols", [P, NROWS])
        omm = sb("omm", [P, 14])
        xT = sb("xT", [P, KT, S])
        mixT = sb("mixT", [P, 2 * NJ, S])
        ring = sb("ring", [P, 3 * SLOT])
        ar = sb("ar", [P, 2, NJ, S])
        kmT = ar[:, 0, :, :].rearrange("p j s -> p (j s)").rearrange("p (k m) -> p k m", k=KT)
        vm = ar[:, 1, :, :].rearrange("p j s -> p (j s)").rearrange("p (t d) -> p t d", t=MT)

        def col(name, i):
            return cols[:, ROWS[name][0] + i:ROWS[name][0] + i + 1]

        def slot(g, width):
            o = (g % 3) * SLOT
            return ring[:, o:o + KT * width].rearrange("p (k n) -> p k n", k=KT)

        def finish_early(t):
            out_done = sem("out_done")
            with nc.Block() as block:
                @block.sync
                def _(sp):
                    sp.dma_start(out[0, 0:P, 0:512], t[:, :]).then_inc(out_done, 16)
                    sp.wait_ge(out_done, 16)

        wv = w_in[0].rearrange("(p k) n -> p k n", k=KT)
        kvv = w_mem_kv[0].rearrange("(p k) n -> p k n", k=KT)
        outv = w_out[0].rearrange("(k p) n -> p k n", p=P)
        qv = w_mem_q[0].rearrange("(p k) n -> p k n", k=KT)
        ov = w_mem_o[0].rearrange("(k p) n -> p k n", p=P)
        groups = ([wv[:, :, ATT0 + 3 * W:ATT0 + 3 * W + 2 * P]]
                  + [wv[:, :, c:c + W] for c in (ATT0 + W, ATT0, ATT0 + 2 * W, 2 * W, 0, W)]
                  + [kvv[:, :, c:c + 512] for c in range(0, 2 * D, 512)]
                  + [v[:, :, c:c + 512] for v in (outv, qv, ov) for c in (0, 512)])
        GL, GK, GR, GV, GAV, GAQ, GAK, GKV, GO, GQ, GMO = 0, 1, 2, 3, 4, 5, 6, 7, 11, 13, 15
        w_here = [sem(f"w_here{i}") for i in range(3)]

        def load_group(eng, g, held=None):
            if held:
                eng.wait_ge(*held)
            n = groups[g].shape[2]
            eng.dma_start(slot(g, n), groups[g]).then_inc(w_here[g % 3], 16)

        def group_here(eng, g):
            eng.wait_ge(w_here[g % 3], 16 * (g // 3 + 1))


        A = ExitStack()
        with A:
            def sa(name, shape, dt=F32):
                return A.enter_context(nc.sbuf_tensor(name, shape, dt))

            bt = sa("bt", [P, NJ, S])
            kt_ = sa("kt_", [P, NJ, S])
            vf = sa("vf", [P, NJ, S])
            rf = sa("rf", [P, NJ, S])
            sgz = sa("sgz", [P, S])
            wc = sa("wc", [P, NJ, NC])
            wg = sa("wg", [P, W])
            av = sa("av", [P, NT, W])
            mask = sa("mask", [P, 2, 2, 2, CH])
            maskT = sa("maskT", [P, 4, CH])
            id64 = sa("id64", [P, CH])

            A1 = ExitStack()
            with A1:
                def s1(name, shape, dt=F32):
                    return A1.enter_context(nc.sbuf_tensor(name, shape, dt))

                kf = s1("kf", [P, NJ, S])
                af = s1("af", [P, NJ, S])
                wf = s1("wf", [P, NJ, S])
                lf = s1("lf", [P, S])
                sq = s1("sq", [P, NJ, S])
                tmp = s1("tmp", [P, 4, S])
                zb = s1("zb", [P, 2, S + 1])
                wup = s1("wup", [P, W])
                rows = s1("rows", [NROWS, P])
                starts = s1("starts", [P, S])
                xtm = mixT[:, :, :].rearrange("p a s -> p (a s)").rearrange("p (t d) -> p t d", t=NT)

                x_here = [part_sem(f"x_here{i}") for i in range(NT)]
                rows_here, up_here = part_sem("rows_here"), part_sem("up_here")
                ident_done, consts_done = part_sem("ident_done"), part_sem("consts_done")
                xt_full, xt_dve, xt_act = part_sem("xt_full"), part_sem("xt_dve"), part_sem("xt_act")
                cols_full, cols_done, omm_done = part_sem("cols_full"), part_sem("cols_done"), part_sem("omm_done")
                job_full = part_sem("job_full")
                z_read, dec_read, icl_read, nrm_read = part_sem("z_read"), part_sem("dec_read"), part_sem("icl_read"), part_sem("nrm_read")
                shifted, tanh_done, sgz_done, w_done = part_sem("shifted"), part_sem("tanh_done"), part_sem("sgz_done"), part_sem("w_done")
                sq_done, rt_done, scanned = part_sem("sq_done"), part_sem("rt_done"), part_sem("scanned")

                AV_EARLY = 2
                jobs = [("L", 0), ("L", 1), ("K", 0), ("K", 1)]
                for j in range(NJ):
                    jobs += [("dec", j), ("icl", j)]
                jobs += [("K", 2), ("K", 3), ("R", 0)] + [("nrm", j) for j in range(NJ)]
                jobs += [("R", j) for j in range(1, NJ)]
                jobs += [("V", j) for j in range(NJ)]
                jobs += [("AV", t) for t in range(AV_EARLY)]
                shift_order = [job for job in jobs if job[0] in ("L", "K", "R", "V")]
                mu_col = {"R": 0, "K": 4, "V": 8, "L": 12}

                def nth(job):
                    return shift_order.index(job) + 1

                def shift_dest(kind, j):
                    if kind == "L":
                        return (lf, sgz)[j][:, :]
                    return {"K": kf, "R": rf, "V": vf}[kind][:, j, :]

                def wait_bank_free(eng, n):
                    if n >= 8:
                        kind, j = jobs[n - 8]
                        if kind in ("L", "K", "R", "V"):
                            eng.wait_ge(z_read, nth((kind, j)))
                        else:
                            eng.wait_ge({"dec": dec_read, "icl": icl_read, "nrm": nrm_read}[kind], j + 1)

                with nc.Block() as block:
                    @block.sync
                    def _(sp):
                        for t in range(NT):
                            sp.dma_start(xtm[:, t, :], x[0, t * P:(t + 1) * P, :]).then_inc(x_here[t], 16)
                        load_group(sp, GL)
                        sp.wait_ge(rows_here, 16 * len(ROWS))
                        load_group(sp, GK)
                        load_group(sp, GR)
                        sp.dma_start(wup[0:64, :], w_decay_up[0]).then_inc(up_here, 16)
                        sp.dma_start(wup[64:128, :], w_iclr_up[0]).then_inc(up_here, 16)
                        sp.dma_start(wg[:, :], w_gate_up[0]).then_inc(up_here, 16)
                        for g, last in ((3, ("L", 1)), (4, ("K", 3)), (5, ("R", 3)), (6, ("V", 3))):
                            load_group(sp, g, (job_full, jobs.index(last) + 1))

                    @block.gpsimd
                    def _(pool):
                        link(pool, pool.memset(ident[:, :], 0.0))
                        pool.affine_select(out=ident[:, :], in_=ident[:, :], compare_op=ALU.not_equal,
                                           fill=1.0, base=0, pattern=[[-1, P]], channel_multiplier=1)\
                            .then_inc(ident_done, 1)
                        pool.wait_ge(ident_done, 1)
                        link(pool, pool.memset(id64[:, :], 0.0))
                        link(pool, pool.memset(blkones[:, :], 0.0))
                        link(pool, pool.memset(mask[:, :, :, :, :], 1.0))
                        link(pool, pool.memset(maskT[:, :, :], 1.0))
                        link(pool, pool.memset(starts[:, :], 0.0))
                        link(pool, pool.memset(zb[:, :, 0:1], 0.0))
                        for h in range(2):
                            rs = slice(64 * h, 64 * h + 64)
                            link(pool, pool.memset(blkones[rs, 64 * h:64 * h + 64], 1.0))
                            link(pool, pool.affine_select(out=id64[rs, :], in_=id64[rs, :],
                                                          compare_op=ALU.not_equal, fill=1.0, base=0,
                                                          pattern=[[-1, CH]], channel_multiplier=1))
                            m = mask[rs, :, :, :, :].rearrange("p u b a t -> p (u b) a t")
                            link(pool, pool.affine_select(out=m, in_=m, compare_op=ALU.is_gt, fill=0.0, base=0,
                                                          pattern=[[0, 4], [1, 2], [1, CH]],
                                                          channel_multiplier=-1))
                            pool.affine_select(out=maskT[rs, :, :], in_=maskT[rs, :, :],
                                               compare_op=ALU.is_gt, fill=0.0, base=0,
                                               pattern=[[0, 4], [-1, CH]], channel_multiplier=1)\
                                .then_inc(consts_done, 1)
                            pool.wait_ge(consts_done, h + 1)

                    @block.tensor
                    def _(pe):
                        pe.wait_ge(ident_done, 1)
                        for t in range(NT):
                            pe.wait_ge(x_here[t], 16)
                            for hf in range(2):
                                for k in range(4):
                                    c = 4 * hf + k
                                    last = nc.tensor.transpose(bank[2 * t + hf][:, k * P:(k + 1) * P],
                                                               xtm[:, t, c:D:KT], ident[:, :])
                                last.then_inc(xt_full, 1)
                        pe.wait_ge(rows_here, 16 * len(ROWS))
                        pe.wait_ge(xt_dve, 1)
                        nc.tensor.transpose(bank[0][:, 0:NROWS], rows[:, :], ident[0:NROWS, 0:NROWS])\
                            .then_inc(cols_full, 1)
                        pe.wait_ge(xt_dve, 4)
                        pe.wait_ge(xt_act, 4)
                        pe.wait_ge(cols_done, 1)
                        for n, (kind, j) in enumerate(jobs):
                            dst = bank[n % 8]
                            wait_bank_free(pe, n)
                            if kind in ("L", "K", "R", "V"):
                                g = {"L": GL, "K": GK, "R": GR, "V": GV}[kind]
                                w = slot(g, 256 if kind == "L" else 512)
                                group_here(pe, g)
                                for k in range(KT):
                                    last = nc.tensor.matmul(dst[:, :], w[:, k, j * P:(j + 1) * P], xT[:, k, :],
                                                            start=(k == 0), stop=(k == KT - 1))
                                last.then_inc(job_full, 1)
                            elif kind == "AV":
                                group_here(pe, GAV)
                                for k in range(KT):
                                    last = nc.tensor.matmul(dst[:, :], xT[:, k, j * P:(j + 1) * P], slot(GAV, 512)[:, k, :],
                                                            start=(k == 0), stop=(k == KT - 1))
                                last.then_inc(job_full, 1)
                            elif kind == "dec":
                                pe.wait_ge(up_here, 48)
                                pe.wait_ge(tanh_done, 1)
                                nc.tensor.matmul(dst[:, :], wup[0:64, j * P:(j + 1) * P], lf[0:64, :],
                                                 start=True, stop=True).then_inc(job_full, 1)
                            elif kind == "icl":
                                pe.wait_ge(shifted, 1)
                                nc.tensor.matmul(dst[:, :], wup[64:128, j * P:(j + 1) * P], lf[64:128, :],
                                                 start=True, stop=True).then_inc(job_full, 1)
                            else:
                                pe.wait_ge(consts_done, 2)
                                pe.wait_ge(sq_done, j + 1)
                                nc.tensor.matmul(dst[:, :], blkones[:, :], sq[:, j, :],
                                                 start=True, stop=True).then_inc(job_full, 1)

                    @block.scalar
                    def _(act):
                        for name, src in (("mu", mu_shift[0]), ("w0", w0[0]), ("a0", a0[0]), ("k_k", k_k[0]),
                                          ("k_a", k_a[0]), ("r_k", r_k[0].rearrange("h d -> (h d)")),
                                          ("lnx_g", lnx_g[0]), ("lnx_b", lnx_b[0]),
                                          ("attn_out_g", attn_out_g[0])):
                            r, k = ROWS[name]
                            act.dma_start(rows[r:r + k, :], src.rearrange("(c p) -> c p", p=P))\
                                .then_inc(rows_here, 16)
                        for b in range(1, 8, 2):
                            act.wait_ge(xt_full, b + 1)
                            t, hf = divmod(b, 2)
                            nc.scalar.activation(xT[:, 4 * hf:4 * hf + 4, t * P:(t + 1) * P],
                                                 bank[b][:, :].rearrange("p (k s) -> p k s", k=4),
                                                 ACT.Copy).then_inc(xt_act, 1)
                        act.wait_ge(omm_done, 1)
                        act.wait_ge(consts_done, 2)
                        for n, (kind, j) in enumerate(jobs):
                            if kind in ("L", "K", "R", "V"):
                                i = mu_col[kind] + j
                                m = nth((kind, j))
                                act.wait_ge(job_full, n + 1)
                                if m > 2:
                                    act.wait_ge(shifted, m - 2)
                                nc.scalar.activation(zb[:, (m - 1) % 2, 1:S + 1], bank[n % 8][:, :], ACT.Copy)
                                nc.scalar.activation(shift_dest(kind, j), bank[n % 8][:, :], ACT.Copy,
                                                     scale=omm[:, i:i + 1]).then_inc(z_read, 1)
                            if kind == "AV":
                                act.wait_ge(job_full, n + 1)
                                nc.scalar.activation(av[:, j, :], bank[n % 8][:, :], ACT.Copy)
                            if (kind, j) == ("L", 1):
                                act.wait_ge(shifted, 1)
                                nc.scalar.activation(lf[0:64, :], lf[0:64, :], ACT.Tanh).then_inc(tanh_done, 1)
                                act.wait_ge(shifted, 2)
                                nc.scalar.activation(sgz[:, :], sgz[:, :], ACT.Sigmoid).then_inc(sgz_done, 1)
                            if kind == "dec":
                                act.wait_ge(job_full, n + 1)
                                nc.scalar.activation(wf[:, j, :], bank[n % 8][:, :], ACT.Sigmoid,
                                                     bias=col("w0", j)).then_inc(dec_read, 1)
                            if kind == "icl":
                                act.wait_ge(job_full, n + 1)
                                nc.scalar.activation(af[:, j, :], bank[n % 8][:, :], ACT.Sigmoid,
                                                     bias=col("a0", j)).then_inc(icl_read, 1)
                            if (kind, j) == ("K", 3):
                                for q in range(NJ):
                                    act.wait_ge(dec_read, q + 1)
                                    nc.scalar.activation(wf[:, q, :], wf[:, q, :], ACT.Exp, scale=-DECAY)\
                                        .then_inc(w_done, 1)
                                for q in range(NJ):
                                    act.wait_ge(shifted, nth(("K", q)))
                                    nc.scalar.activation(sq[:, q, :], kf[:, q, :], ACT.Square,
                                                         scale=col("k_k", q)).then_inc(sq_done, 1)
                            if kind == "nrm":
                                act.wait_ge(nrm_read, j + 1)
                                nc.scalar.activation(sq[:, j, :], sq[:, j, :], ACT.Sqrt).then_inc(rt_done, 1)

                    @block.vector
                    def _(dve):
                        for b in range(0, 8, 2):
                            dve.wait_ge(xt_full, b + 1)
                            t, hf = divmod(b, 2)
                            nc.vector.tensor_copy(xT[:, 4 * hf:4 * hf + 4, t * P:(t + 1) * P],
                                                  bank[b][:, :].rearrange("p (k s) -> p k s", k=4))\
                                .then_inc(xt_dve, 1)
                        dve.wait_ge(cols_full, 1)
                        nc.vector.tensor_copy(cols[:, :], bank[0][:, 0:NROWS]).then_inc(cols_done, 1)
                        dve.wait_ge(cols_done, 1)
                        nc.vector.tensor_scalar(omm[:, :], cols[:, 0:14], -1.0, 1.0, ALU.mult, ALU.add)\
                            .then_inc(omm_done, 1)
                        dve.wait_ge(consts_done, 2)

                        def decay_products(j):
                            dve.wait_ge(w_done, j + 1)
                            if j > 0:
                                dve.wait_ge(scanned, j)
                            link(dve, nc.vector.tensor_copy(starts[:, 0:S:CH], wf[:, j, 0:S:CH]))
                            link(dve, nc.vector.memset(wf[:, j, 0:S:CH], 0.0))
                            nc.vector.tensor_tensor_scan(wf[:, j, :], wf[:, j, :], starts[:, :], 0.0,
                                                         ALU.mult, ALU.add).then_inc(scanned, 1)

                        def key_side(j):
                            dve.wait_ge(rt_done, j + 1)
                            dve.wait_ge(scanned, j + 1)
                            dve.wait_ge(icl_read, j + 1)
                            rn, kk, b, rw, am = sq[:, j, :], tmp[:, 0, :], tmp[:, 1, :], tmp[:, 2, :], tmp[:, 3, :]
                            nc.vector.reciprocal(rw, wf[:, j, :])
                            nc.vector.tensor_copy(wc[:, j, :], wf[:, j, CH - 1:S:CH])
                            link(dve, nc.vector.reciprocal(rn, rn))
                            nc.vector.tensor_scalar(am, af[:, j, :], -1.0, col("k_a", j), ALU.add, ALU.mult)
                            link(dve, nc.vector.scalar_tensor_tensor(kk, kf[:, j, :], col("k_k", j), rn,
                                                                     ALU.mult, ALU.mult))
                            kkc, wfc = (v.rearrange("p (c t) -> p c t", t=CH) for v in (kk, wf[:, j, :]))
                            at = ar[:, 0, j, :].rearrange("p (c t) -> p c t", t=CH)
                            nc.vector.scalar_tensor_tensor(at[:, :, 1:CH], kkc[:, :, 1:CH], -1.0,
                                                           wfc[:, :, 0:CH - 1], ALU.mult, ALU.mult)
                            nc.vector.tensor_scalar(at[:, :, 0:1], kkc[:, :, 0:1], -1.0, None, ALU.mult)
                            nc.vector.tensor_tensor(b, kk, af[:, j, :], ALU.mult)
                            link(dve, nc.vector.scalar_tensor_tensor(kf[:, j, :], am, 1.0, kf[:, j, :],
                                                                     ALU.add, ALU.mult))
                            nc.vector.tensor_tensor(bt[:, j, :], b, rw, ALU.mult)
                            link(dve, nc.vector.tensor_tensor(kt_[:, j, :], kf[:, j, :], rw, ALU.mult))

                        def receptance_side(j):
                            dve.wait_ge(shifted, nth(("R", j)))
                            nc.vector.tensor_tensor(ar[:, 1, j, :], rf[:, j, :], wf[:, j, :], ALU.mult)
                            nc.vector.scalar_tensor_tensor(rf[:, j, :], rf[:, j, :], col("r_k", j), kf[:, j, :],
                                                           ALU.mult, ALU.mult)

                        for n, (kind, j) in enumerate(jobs):
                            if kind in ("L", "K", "R", "V"):
                                m = nth((kind, j))
                                i = mu_col[kind] + j
                                d = shift_dest(kind, j)
                                dve.wait_ge(z_read, m)
                                nc.vector.scalar_tensor_tensor(d, zb[:, (m - 1) % 2, 0:S], cols[:, i:i + 1], d,
                                                               ALU.mult, ALU.add).then_inc(shifted, 1)
                            if (kind, j) == ("R", 0):
                                for q in range(NJ):
                                    decay_products(q)
                            if kind == "nrm":
                                dve.wait_ge(job_full, n + 1)
                                nc.vector.tensor_scalar(sq[:, j, :], bank[n % 8][:, :], 1e-24, None, ALU.max)\
                                    .then_inc(nrm_read, 1)
                            if kind == "R" and j > 0:
                                key_side(j - 1)
                            if (kind, j) == ("V", 0):
                                key_side(NJ - 1)
                            if kind == "V":
                                receptance_side(j)
            if stop == 1:
                return finish_early(sgz)

            qT = sa("qT", [P, NJ, S])
            kT = sa("kT", [P, NJ, S])
            A2 = ExitStack()
            with A2:
                def s2(name, shape, dt=F32):
                    return A2.enter_context(nc.sbuf_tensor(name, shape, dt))

                NG = (NC // 2) * 2
                tm = s2("tm", [P, 2, 2, 3, P])
                gg = s2("gg", [P, 2, 2, 2, 2, 2, CH])
                ntb = s2("ntb", [P, 2, 2, 2, CH])
                pw = s2("pw", [P, 2, 2, 4, CH])
                pd = s2("pd", [P, 2, 2, 4, 2, CH])
                ux = s2("ux", [P, 2, 4, 2, CH])
                rr = s2("rr", [P, 2, 2, CH])
                ft = s2("ft", [P, 2, 2, CH])
                hs = s2("hs", [P, 2, 2, CH])
                yi = s2("yi", [P, 2, 2, CH])
                st = s2("st", [P, NJ, 2, CH])

                tm_full, tm_read = part_sem("tm_full"), part_sem("tm_read")
                g_full, g_masked = part_sem("g_full"), part_sem("g_masked")
                nt_full, nt_masked = part_sem("nt_full"), part_sem("nt_masked")
                akv_full, akv_read = part_sem("akv_full"), part_sem("akv_read")
                sq_full, sq_act, sq_dve = part_sem("sqr_full"), part_sem("sq_act"), part_sem("sq_dve")
                ax_full, ax_added = part_sem("ax_full"), part_sem("ax_added")
                re_full, re_read = part_sem("re_full"), part_sem("re_read")
                sy_full, st_done, y_done = part_sem("sy_full"), part_sem("st_done"), part_sem("y_done")
                st_zero = part_sem("st_zero")
                fill_full, fill_read = part_sem("fill_full"), part_sem("fill_read")
                half = [slice(0, 64), slice(64, 128)]

                fills = ([(GAV, t, av[:, t, :]) for t in range(AV_EARLY, NT)]
                         + [(GAQ, j, qT[:, j, :]) for j in range(NJ)] + [(GAK, j, kT[:, j, :]) for j in range(NJ)])
                STEPS = 4
                share = (0, 1, 0, 0, 0, 0, 0, 1, 1, 1, 1, 0)
                fill_at = [0]
                for place in range(NG * len(share)):
                    fill_at.append(min(STEPS * len(fills), fill_at[-1] + share[place % len(share)]))
                fill_at[-1] = STEPS * len(fills)

                def scalar_copy(dst, src):
                    return nc.scalar.activation(dst, src, ACT.Copy)

                def first_powers(copy, cp):
                    src = bank[cp][half[cp], :].rearrange("p (w u c) -> p w u c", w=2, u=4)
                    copy(pw[half[cp], 0, :, :, :], src)
                    return copy(pd[half[cp], 0, :, :, cp, :], src)

                def powers(copy, m, which):
                    src = bank[which][:, 0:4 * CH].rearrange("p (u c) -> p u c", u=4)
                    if m < 4 - which:
                        copy(pw[:, m % 2, which, :, :], src)
                    copy(pd[half[0], m % 2, which, :, 0, :], src[half[0]])
                    return copy(pd[half[1], m % 2, which, :, 1, :], src[half[1]])

                with nc.Block() as block:
                    @block.sync
                    def _(sp):
                        for i in range(3):
                            load_group(sp, GKV + i, (fill_full, 4 * (i + 1) - AV_EARLY))

                    @block.gpsimd
                    def _(pool):
                        pool.memset(pd[:, :, :, :, :, :], 0.0).then_inc(st_zero, 1)
                        pool.wait_ge(st_zero, 1)
                        pool.memset(st[:, :, 0, :], 0.0).then_inc(st_zero, 1)

                    @block.tensor
                    def _(pe):
                        def fill(n, place):
                            place += n * len(share)
                            for step in range(fill_at[place], fill_at[place + 1]):
                                f, part = divmod(step, STEPS)
                                g, i, _ = fills[f]
                                if part == 0:
                                    group_here(pe, g)
                                    if f >= 2:
                                        pe.wait_ge(fill_read, f - 1)
                                w = slot(g, 512)
                                for k in range(2 * part, 2 * part + 2):
                                    sl = slice(i * P, (i + 1) * P)
                                    lhs, rhs = (xT[:, k, sl], w[:, k, :]) if g == GAV else (w[:, k, sl], xT[:, k, :])
                                    last = nc.tensor.matmul(bank[6 + f % 2][:, :], lhs, rhs, start=(k == 0),
                                                            stop=(k == KT - 1))
                                if part == STEPS - 1:
                                    last.then_inc(fill_full, 1)

                        pe.wait_ge(st_zero, 2)
                        for n in range(NG):
                            cpair, quad = divmod(n, 2)
                            b = n % 2
                            units = [(p, hp) for p in range(2) for hp in range(2)]
                            ts = slice(cpair * P, (cpair + 1) * P)
                            fill(n, 0)
                            if n:
                                pe.wait_ge(y_done, 2 * n - 1)
                            for p in range(2):
                                j = 2 * quad + p
                                srcs = (ar[:, 0, j, ts], bt[:, j, ts], kt_[:, j, ts],
                                        vf[:, j, ts])
                                for i, src in enumerate(srcs):
                                    last = nc.tensor.transpose(bank[4 + p][:, i * P:(i + 1) * P], src, ident[:, :])
                                last.then_inc(tm_full, 1)
                            if n:
                                pe.wait_ge(re_read, 2 * n)
                            for p in range(2):
                                for cp in range(2):
                                    c = 2 * cpair + cp
                                    cs = slice(c * CH, (c + 1) * CH)
                                    for i, left in enumerate((bt, kt_)):
                                        for hp in range(2):
                                            j = 2 * quad + p
                                            o = (2 * p + i) * 2 * CH
                                            ins = nc.tensor.matmul(bank[hp][half[cp], o:o + 2 * CH],
                                                                   left[half[hp], j, cs], ar[half[hp], :, j, cs],
                                                                   start=True, stop=True)
                                            if (p, cp, i) == (1, 1, 1):
                                                ins.then_inc(g_full, 1)
                            if n:
                                pe.wait_ge(y_done, 2 * n)
                            for p in range(2):
                                for cp in range(2):
                                    c = 2 * cpair + cp
                                    cs = slice(c * CH, (c + 1) * CH)
                                    for hp in range(2):
                                        j = 2 * quad + p
                                        ins = nc.tensor.matmul(bank[2 + hp][half[cp], p * CH:(p + 1) * CH],
                                                               ar[half[hp], 0, j, cs], bt[half[hp], j, cs],
                                                               start=True, stop=True)
                                        if (p, cp) == (1, 1):
                                            ins.then_inc(nt_full, 1)
                            fill(n, 1)
                            pe.wait_ge(tm_read, 2 * n + 2)
                            pe.wait_ge(g_masked, 2 * n + 2)
                            for u, (p, hp) in enumerate(units):
                                for cp in range(2):
                                    ins = nc.tensor.matmul(bank[4 + cp][half[cp], u * CH:(u + 1) * CH],
                                                           gg[half[cp], b, hp, p, 1, 0, :],
                                                           tm[half[cp], b, p, 2, hp * CH:(hp + 1) * CH],
                                                           start=True, stop=True)
                                    if u == 3:
                                        ins.then_inc(akv_full, 1)
                            fill(n, 2)
                            pe.wait_ge(nt_masked, 2 * n + 2)
                            for which in range(2):
                                for u, (p, hp) in enumerate(units):
                                    for cp in range(2):
                                        at, a = gg[half[cp], b, hp, p, 0, 0, :], ntb[half[cp], b, hp, p, :]
                                        o = (4 * which + u) * CH
                                        ins = nc.tensor.matmul(bank[cp][half[cp], o:o + CH], (a, at)[which],
                                                               (at, a)[which], start=True, stop=True)
                                        if (which, u) == (1, 3):
                                            ins.then_inc(sq_full, 1)
                            pe.wait_ge(akv_read, 2 * n + 2)
                            for u, (p, hp) in enumerate(units):
                                for cp in range(2):
                                    ins = nc.tensor.matmul(bank[2 + cp][half[cp], 2 * u * CH:2 * (u + 1) * CH],
                                                           gg[half[cp], b, hp, p, 0, 0, :],
                                                           ux[half[cp], b, u, :, :], start=True, stop=True)
                                    if u == 3:
                                        ins.then_inc(ax_full, 1)
                            for m in range(1, 6):
                                fill(n, 2 + m)
                                q = (m - 1) % 2
                                pe.wait_ge(sq_act, 5 * n + m)
                                if m < 5:
                                    pe.wait_ge(sq_dve, 4 * n + m)
                                    for which in ((0, 1) if m < 4 else (0,)):
                                        for u in range(4):
                                            last = nc.tensor.matmul(bank[which][:, u * CH:(u + 1) * CH],
                                                                    pd[:, q, 1 - which, u, :, :]
                                                                    .rearrange("p c t -> p (c t)"),
                                                                    pw[:, q, which, u, :], start=True, stop=True)
                                        last.then_inc(sq_full, 1)
                                pe.wait_ge(ax_added, 7 * n + (2 if m == 1 else m + 1))
                                for u in range(4):
                                    last = nc.tensor.matmul(bank[2][:, 2 * u * CH:2 * (u + 1) * CH],
                                                            pd[:, q, 0, u, :, :].rearrange("p c t -> p (c t)"),
                                                            ux[:, b, u, :, :].rearrange("p w c -> p (w c)"),
                                                            start=True, stop=True)
                                last.then_inc(ax_full, 1)
                            fill(n, 8)
                            pe.wait_ge(ax_added, 7 * n + 7)
                            for u, (p, hp) in enumerate(units):
                                hs_ = slice(hp * CH, (hp + 1) * CH)
                                for kind in range(4):
                                    for cp in range(2):
                                        r, o = half[cp], (4 * p + kind) * CH
                                        dst = bank[cp][half[hp], o:o + CH]
                                        M, U = ux[r, b, u, 0, :], ux[r, b, u, 1, :]
                                        bm, km, vm = (tm[r, b, p, i, hs_] for i in range(3))
                                        br, kr = gg[r, b, hp, p, 0, 1, :], gg[r, b, hp, p, 1, 1, :]
                                        terms = (((M, br),), ((M, bm),), ((bm, U), (km, vm)), ((U, br), (vm, kr)))[kind]
                                        for i, (lhs, rhs) in enumerate(terms):
                                            ins = nc.tensor.matmul(dst, lhs, rhs, start=(i == 0),
                                                                   stop=(i == len(terms) - 1))
                                        if u == 3 and kind == 3:
                                            ins.then_inc(re_full, 1)
                            for cp in range(2):
                                c = 2 * cpair + cp
                                fill(n, 9 + cp)
                                pe.wait_ge(re_read, 2 * n + cp + 1)
                                pe.wait_ge(st_done, 2 * n + cp) if 2 * n + cp else None
                                base = 4 if cp == 0 else 2
                                for p in range(2):
                                    for hp in range(2):
                                        j = 2 * quad + p
                                        s_in = st[half[hp], j, c % 2, :]
                                        nc.tensor.matmul(bank[base + hp][half[hp], p * CH:(p + 1) * CH],
                                                         ft[half[hp], cp, p, :], s_in, start=True, stop=True)
                                for p in range(2):
                                    for hp in range(2):
                                        j = 2 * quad + p
                                        s_in = st[half[hp], j, c % 2, :]
                                        ins = nc.tensor.matmul(bank[base + hp][half[hp], (2 + p) * CH:(3 + p) * CH],
                                                               s_in, rr[half[hp], cp, p, :], start=True, stop=True)
                                ins.then_inc(sy_full, 1)
                            fill(n, 11)

                    @block.scalar
                    def _(act):
                        done = [0]

                        def fill(n, place):
                            place += n * len(share)
                            while done[0] < fill_at[place + 1] // STEPS:
                                f = done[0]
                                act.wait_ge(fill_full, f + 1)
                                nc.scalar.activation(fills[f][2], bank[6 + f % 2][:, :], ACT.Copy)\
                                    .then_inc(fill_read, 1)
                                done[0] += 1

                        for n in range(NG):
                            b = n % 2
                            for p in range(2):
                                act.wait_ge(tm_full, 2 * n + p + 1)
                                if n >= 2 and p == 0:
                                    act.wait_ge(sy_full, 2 * n - 2)
                                nc.scalar.activation(ux[:, b, 2 * p:2 * p + 2, 0, :],
                                                     bank[4 + p][:, 0:P].rearrange("p (h c) -> p h c", h=2), ACT.Copy)
                                nc.scalar.activation(tm[:, b, p, :, :],
                                                     bank[4 + p][:, P:4 * P].rearrange("p (k c) -> p k c", k=3),
                                                     ACT.Copy).then_inc(tm_read, 1)
                            fill(n, 1)
                            act.wait_ge(sq_full, 9 * n + 1)
                            first_powers(scalar_copy, 0).then_inc(sq_act, 1)
                            for m in range(1, 5):
                                act.wait_ge(sq_full, 9 * n + 2 * m + 1)
                                powers(scalar_copy, m, 0).then_inc(sq_act, 1)
                            fill(n, 7)
                            fill(n, 11)

                    @block.vector
                    def _(dve):
                        for n in range(NG):
                            cpair, quad = divmod(n, 2)
                            b = n % 2
                            if n >= 2:
                                dve.wait_ge(sy_full, 2 * n - 2)
                            for hp in range(2):
                                dve.wait_ge(g_full, 2 * n + hp + 1)
                                nc.vector.tensor_tensor(gg[:, b, hp, :, :, :, :].rearrange("p a b c t -> p (a b c t)"),
                                                        bank[hp][:, :],
                                                        mask[:, :, :, :, :].rearrange("p a b c t -> p (a b c t)"),
                                                        ALU.mult).then_inc(g_masked, 1)
                            for hp in range(2):
                                dve.wait_ge(nt_full, 2 * n + hp + 1)
                                nc.vector.tensor_tensor(ntb[:, b, hp, :, :], bank[2 + hp][:, 0:2 * CH]
                                                        .rearrange("p (a t) -> p a t", a=2), maskT[:, 0:2, :],
                                                        ALU.mult).then_inc(nt_masked, 1)
                            for cp in range(2):
                                dve.wait_ge(akv_full, 2 * n + cp + 1)
                                nc.vector.tensor_copy(ux[half[cp], b, :, 1, :],
                                                      bank[4 + cp][half[cp], 0:4 * CH]
                                                      .rearrange("p (u c) -> p u c", u=4)).then_inc(akv_read, 1)
                            dve.wait_ge(sq_full, 9 * n + 2)
                            first_powers(nc.vector.tensor_copy, 1).then_inc(sq_dve, 1)
                            for cp in range(2):
                                dve.wait_ge(ax_full, 7 * n + cp + 1)
                                v = ux[half[cp], b, :, :, :].rearrange("p u w c -> p (u w c)")
                                nc.vector.tensor_tensor(v, bank[2 + cp][half[cp], :], v, ALU.add)\
                                    .then_inc(ax_added, 1)
                            for m in range(1, 6):
                                if m < 4:
                                    dve.wait_ge(sq_full, 9 * n + 2 * m + 2)
                                    powers(nc.vector.tensor_copy, m, 1).then_inc(sq_dve, 1)
                                dve.wait_ge(ax_full, 7 * n + m + 2)
                                v = ux[:, b, :, :, :].rearrange("p u w c -> p (u w c)")
                                nc.vector.tensor_tensor(v, bank[2][:, :], v, ALU.add).then_inc(ax_added, 1)
                            js = slice(2 * quad, 2 * quad + 2)
                            for cp in range(2):
                                c = 2 * cpair + cp
                                dve.wait_ge(re_full, 2 * n + cp + 1)
                                if n:
                                    dve.wait_ge(sy_full, 2 * n)
                                    dve.wait_ge(st_done, 2 * n)
                                    dve.wait_ge(y_done, 2 * n)
                                src = bank[cp][:, :].rearrange("p (a k t) -> p a k t", a=2, k=4)
                                nc.vector.tensor_tensor(rr[:, cp, :, :], src[:, :, 0, :], ar[:, 1, js, c * CH:(c + 1) * CH],
                                                        ALU.add)
                                nc.vector.tensor_tensor(ft[:, cp, :, :], src[:, :, 1, :],
                                                        id64[:, :].unsqueeze(1).to_broadcast([P, 2, CH]), ALU.add)
                                nc.vector.tensor_tensor(hs[:, cp, :, :], src[:, :, 2, :],
                                                        wc[:, js, c:c + 1].to_broadcast([P, 2, CH]), ALU.mult)
                                nc.vector.tensor_copy(yi[:, cp, :, :], src[:, :, 3, :]).then_inc(re_read, 1)
                            for cp in range(2):
                                c = 2 * cpair + cp
                                base = 4 if cp == 0 else 2
                                dve.wait_ge(sy_full, 2 * n + cp + 1)
                                dve.wait_ge(re_read, 2 * n + cp + 1)
                                for p in range(2):
                                    for hp in range(2):
                                        j = 2 * quad + p
                                        ins = nc.vector.scalar_tensor_tensor(
                                            st[half[hp], j, (c + 1) % 2, :],
                                            bank[base + hp][half[hp], p * CH:(p + 1) * CH], wc[half[hp], j, c:c + 1],
                                            hs[half[hp], cp, p, :], ALU.mult, ALU.add)
                                ins.then_inc(st_done, 1)
                                for hp in range(2):
                                    ins = nc.vector.tensor_tensor(
                                        bt[half[hp], js, c * CH:(c + 1) * CH],
                                        bank[base + hp][half[hp], 2 * CH:4 * CH].rearrange("p (a t) -> p a t", a=2),
                                        yi[half[hp], cp, :, :], ALU.add)
                                ins.then_inc(y_done, 1)
            if stop == 2:
                return finish_early(sgz)

            A3 = ExitStack()
            with A3:
                def s3(name, shape, dt=F32):
                    return A3.enter_context(nc.sbuf_tensor(name, shape, dt))

                dist = s3("dist", [P, 512])
                ysq = s3("ysq", [P, 2, S])
                sc = s3("sc", [P, 3, S])
                pr = s3("pr", [P, 3, S])
                prT = s3("prT", [P, 3, S])
                mx = s3("mx", [P, H, NT])
                nmx = s3("nmx", [P, H, NT])
                rs = s3("rs", [P, H, NT])
                ri = s3("ri", [P, H, NT])
                oa = s3("oa", [P, NT, H, HD])
                osq = s3("osq", [P, NT, H, HD])
                oss = s3("oss", [P, NT, H])
                memtm = mixT[:, 0:NJ, :].rearrange("p a s -> p (a s)").rearrange("p (t d) -> p t d", t=MT)
                memT = mixT[:, NJ:2 * NJ, :].rearrange("p a s -> p (a s)").rearrange("p (k s) -> p k s", k=KT)

                mem_here, dist_done = part_sem("mem_here"), part_sem("dist_done")
                mt_full, mt_read = part_sem("mt_full"), part_sem("mt_read")
                mu_full, yc_done, ysq_done = part_sem("mu_full"), part_sem("yc_done"), part_sem("ysq_done")
                var_full, var_read, rstd_root = part_sem("var_full"), part_sem("var_read"), part_sem("rstd_root")
                bon_full, gate_full, bon_read, gate_read = part_sem("bon_full"), part_sem("gate_full"), part_sem("bon_read"), part_sem("gate_read")
                mfill_full, mfill_read = part_sem("mfill_full"), part_sem("mfill_read")
                s_full, s_read, s_max, p_done, p_norm = part_sem("s_full"), part_sem("s_read"), part_sem("s_max"), part_sem("p_done"), part_sem("p_norm")
                pt_full, pt_read, o_full, o_read = part_sem("pt_full"), part_sem("pt_read"), part_sem("o_full"), part_sem("o_read")
                osq_done, oms_done, ort_done, on_done = part_sem("osq_done"), part_sem("oms_done"), part_sem("ort_done"), part_sem("on_done")
                ot_full, ot_read = part_sem("ot_full"), part_sem("ot_read")

                mfills = [("k", i) for i in range(KT // 2)] + [("v", i) for i in range(2 * MT)]
                mplaces = (2, 4, 2, 2, 2, 0) + (1, 0, 1, 1) * 5 + (1, 0) * 5 + (0,) * 5
                MSTEPS = 4
                mfill_at = [0]
                for steps_ in mplaces:
                    mfill_at.append(mfill_at[-1] + steps_)
                qunits = [(h, q) for h in range(H) for q in range(NT)]
                LAG = 2

                def mfill_dest(f):
                    kind, i = mfills[f]
                    if kind == "k":
                        return kmT[:, 2 * i:2 * i + 2, :].rearrange("p a m -> p (a m)")
                    return vm[:, i % MT, (i // MT) * 512:(i // MT + 1) * 512]

                with nc.Block() as block:
                    @block.sync
                    def _(sp):
                        sp.dma_start(memtm, mem[0].rearrange("(t p) d -> p t d", p=P)).then_inc(mem_here, 16)
                        load_group(sp, GKV + 3, (mfill_full, 2))
                        load_group(sp, GO, (mfill_full, 4))
                        load_group(sp, GO + 1, (mfill_full, 6))
                        load_group(sp, GQ, (mfill_full, 8))

                    @block.gpsimd
                    def _(pool):
                        link(pool, pool.iota(dist[:, :], pattern=[[1, 512]], base=-384, channel_multiplier=-1,
                                             allow_small_or_imprecise_dtypes=True))
                        pool.affine_select(out=dist[:, :], in_=dist[:, :], compare_op=ALU.is_ge, fill=NEG,
                                           base=384, pattern=[[-1, 512]], channel_multiplier=1)\
                            .then_inc(dist_done, 1)

                    @block.tensor
                    def _(pe):
                        def mfill(place):
                            for step in range(mfill_at[place], mfill_at[place + 1]):
                                f, part = divmod(step, MSTEPS)
                                kind, i = mfills[f]
                                dst = bank[6]
                                if part == 0 and f:
                                    pe.wait_ge(mfill_read, f)
                                if kind == "k":
                                    a, k0 = divmod(part, 2)
                                    g, ks = GKV + i // 2, range(4 * k0, 4 * k0 + 4)
                                    ct = (2 * i + a) % 4
                                else:
                                    g, ks = GKV + 2 + i // MT, range(2 * part, 2 * part + 2)
                                    t = i % MT
                                if part == 0:
                                    group_here(pe, g)
                                w = slot(g, 512)
                                for k in ks:
                                    if kind == "k":
                                        last = nc.tensor.matmul(dst[:, a * MEM:(a + 1) * MEM],
                                                                w[:, k, ct * P:(ct + 1) * P], memT[:, k, :],
                                                                start=(k == 0), stop=(k == KT - 1))
                                    else:
                                        last = nc.tensor.matmul(dst[:, :], memT[:, k, t * P:(t + 1) * P], w[:, k, :],
                                                                start=(k == 0), stop=(k == KT - 1))
                                if part == MSTEPS - 1:
                                    last.then_inc(mfill_full, 1)

                        for j in range(NJ):
                            nc.tensor.matmul(bank[j][:, :], blkones[:, :], bt[:, j, :], start=True, stop=True)\
                                .then_inc(mu_full, 1)
                        pe.wait_ge(mem_here, 16)
                        for b in range(4):
                            t, hf = divmod(b, 2)
                            for k in range(4):
                                c = 4 * hf + k
                                last = nc.tensor.transpose(bank[4 + b][:, k * P:(k + 1) * P],
                                                           memtm[:, t, c:D:KT], ident[:, :])
                            last.then_inc(mt_full, 1)
                        pe.wait_ge(mt_read, 4)
                        mfill(0)
                        for j in range(NJ):
                            pe.wait_ge(ysq_done, j + 1)
                            nc.tensor.matmul(bank[j][:, :], blkones[:, :], ysq[:, j % 2, :], start=True, stop=True)\
                                .then_inc(var_full, 1)
                        mfill(1)
                        for j in range(NJ):
                            if j:
                                pe.wait_ge(bon_read, j)
                                pe.wait_ge(gate_read, j)
                            nc.tensor.matmul(bank[4][:, :], blkones[:, :], rf[:, j, :], start=True, stop=True)\
                                .then_inc(bon_full, 1)
                            nc.tensor.matmul(bank[5][:, :], wg[:, j * P:(j + 1) * P], sgz[:, :], start=True, stop=True)\
                                .then_inc(gate_full, 1)
                            mfill(2 + j)

                        def scores(n):
                            h, q = qunits[n]
                            j, r = h // 2, slice((h % 2) * HD, (h % 2) * HD + HD)
                            if n < 3:
                                pe.wait_ge(var_read, n + 1)
                            else:
                                pe.wait_ge(s_read, n - 2)
                            nk = (q + 1) * P
                            nc.tensor.matmul(bank[n % 3][:, 0:nk], qT[r, j, q * P:(q + 1) * P], kT[r, j, 0:nk],
                                             start=True, stop=True).then_inc(s_full, 1)

                        def values(n):
                            h, q = qunits[n]
                            j = h // 2
                            pe.wait_ge(p_norm, n + 1)
                            b = 3 + n % 2
                            if n < 2:
                                pe.wait_ge(var_read, 4) if n == 0 else pe.wait_ge(bon_read, NJ)
                            else:
                                pe.wait_ge(pt_read, n - 1)
                            for k in range(q + 1):
                                last = nc.tensor.transpose(bank[b][:, k * P:(k + 1) * P],
                                                           pr[:, n % 3, k * P:(k + 1) * P], ident[:, :])
                            last.then_inc(pt_full, 1)

                        def product(n):
                            h, q = qunits[n]
                            j = h // 2
                            pe.wait_ge(pt_read, n + 1)
                            if q == 0:
                                if h >= 2:
                                    pe.wait_ge(o_read, h - 1)
                                else:
                                    pe.wait_ge(gate_read, NJ)
                            o = q * HD
                            for k in range(q + 1):
                                last = nc.tensor.matmul(bank[5 + 2 * (h % 2)][:, o:o + HD], prT[:, n % 3, k * P:(k + 1) * P],
                                                        av[:, k, h * HD:(h + 1) * HD], start=(k == 0), stop=(k == q))
                            last.then_inc(o_full, 1)

                        pe.wait_ge(dist_done, 1)
                        for n in range(len(qunits) + LAG + 1):
                            if n < len(qunits):
                                scores(n)
                            if LAG <= n < len(qunits) + LAG:
                                values(n - LAG)
                            if n > LAG:
                                product(n - LAG - 1)
                            mfill(6 + n)
                        pe.wait_ge(on_done, 1)
                        for j in range(NJ):
                            for t in range(NT):
                                last = nc.tensor.transpose(bank[j][:, t * P:(t + 1) * P],
                                                           oa[:, t, 2 * j:2 * j + 2, :].rearrange("p h d -> p (h d)"),
                                                           ident[:, :])
                            last.then_inc(ot_full, 1)

                    @block.scalar
                    def _(act):
                        mfills_read = [0]

                        def mfill(place):
                            while mfills_read[0] < mfill_at[place + 1] // MSTEPS:
                                f = mfills_read[0]
                                act.wait_ge(mfill_full, f + 1)
                                nc.scalar.activation(mfill_dest(f), bank[6][:, :], ACT.Copy)\
                                    .then_inc(mfill_read, 1)
                                mfills_read[0] += 1

                        for b in range(4):
                            t, hf = divmod(b, 2)
                            act.wait_ge(mt_full, b + 1)
                            nc.scalar.activation(memT[:, 4 * hf:4 * hf + 4, t * P:(t + 1) * P],
                                                 bank[4 + b][:, :].rearrange("p (k s) -> p k s", k=4),
                                                 ACT.Copy).then_inc(mt_read, 1)
                        for j in range(NJ):
                            act.wait_ge(yc_done, j + 1)
                            if j >= 2:
                                act.wait_ge(var_full, j - 1)
                            nc.scalar.activation(ysq[:, j % 2, :], bt[:, j, :], ACT.Square).then_inc(ysq_done, 1)
                        mfill(0)
                        for j in range(NJ):
                            act.wait_ge(var_read, j + 1)
                            nc.scalar.activation(kt_[:, j, :], kt_[:, j, :], ACT.Sqrt).then_inc(rstd_root, 1)
                        for place in range(1, 6):
                            mfill(place)

                        def exps(n):
                            h, q = qunits[n]
                            nk = (q + 1) * P
                            act.wait_ge(s_max, n + 1)
                            if n >= 3:
                                act.wait_ge(pt_full, n - 2)
                            nc.scalar.activation(pr[:, n % 3, 0:nk], sc[:, n % 3, 0:nk], ACT.Exp,
                                                 bias=nmx[:, h, q:q + 1], scale=HD ** -0.5,
                                                 accum_out=rs[:, h, q:q + 1]).then_inc(p_done, 1)

                        def transposed(n):
                            h, q = qunits[n]
                            nk = (q + 1) * P
                            act.wait_ge(pt_full, n + 1)
                            if n >= 3:
                                act.wait_ge(o_full, n - 2)
                            nc.scalar.activation(prT[:, n % 3, 0:nk], bank[3 + n % 2][:, 0:nk], ACT.Copy)\
                                .then_inc(pt_read, 1)

                        for n in range(len(qunits) + LAG):
                            if n < len(qunits):
                                exps(n)
                            if n >= LAG:
                                transposed(n - LAG)
                            mfill(6 + n)
                        mfill(6 + len(qunits) + LAG)
                        act.wait_ge(o_read, H)
                        nc.scalar.activation(osq[:, :, :, :].rearrange("p t h d -> p (t h d)"),
                                             oa[:, :, :, :].rearrange("p t h d -> p (t h d)"), ACT.Square)\
                            .then_inc(osq_done, 1)
                        act.wait_ge(oms_done, 1)
                        nc.scalar.activation(oss[:, :, :], oss[:, :, :], ACT.Sqrt).then_inc(ort_done, 1)
                        for j in range(NJ):
                            act.wait_ge(ot_full, j + 1)
                            nc.scalar.activation(mixT[:, j, :], bank[j][:, :], ACT.Copy,
                                                 scale=col("attn_out_g", j)).then_inc(ot_read, 1)

                    @block.vector
                    def _(dve):
                        for j in range(NJ):
                            dve.wait_ge(mu_full, j + 1)
                            nc.vector.scalar_tensor_tensor(bt[:, j, :], bank[j][:, :], -1.0 / HD, bt[:, j, :],
                                                           ALU.mult, ALU.add).then_inc(yc_done, 1)
                        for j in range(NJ):
                            dve.wait_ge(var_full, j + 1)
                            nc.vector.tensor_scalar(kt_[:, j, :], bank[j][:, :], 1.0 / HD, GN_EPS, ALU.mult,
                                                    ALU.add).then_inc(var_read, 1)
                        for j in range(NJ):
                            y = bt[:, j, :]
                            dve.wait_ge(bon_full, j + 1)
                            nc.vector.tensor_tensor(vf[:, j, :], bank[4][:, :], vf[:, j, :], ALU.mult)\
                                .then_inc(bon_read, 1)
                            dve.wait_ge(rstd_root, j + 1)
                            link(dve, nc.vector.reciprocal(kt_[:, j, :], kt_[:, j, :]))
                            link(dve, nc.vector.tensor_tensor(y, y, kt_[:, j, :], ALU.mult))
                            link(dve, nc.vector.tensor_scalar(y, y, col("lnx_g", j), col("lnx_b", j), ALU.mult,
                                                              ALU.add))
                            link(dve, nc.vector.tensor_tensor(y, y, vf[:, j, :], ALU.add))
                            dve.wait_ge(gate_full, j + 1)
                            nc.vector.tensor_tensor(rf[:, j, :], bank[5][:, :], y, ALU.mult).then_inc(gate_read, 1)
                        dve.wait_ge(dist_done, 1)

                        def biased(n):
                            h, q = qunits[n]
                            nk = (q + 1) * P
                            slope = 2.0 ** (-8.0 * (h + 1) / H)
                            dve.wait_ge(s_full, n + 1)
                            if n >= 3:
                                dve.wait_ge(p_done, n - 2)
                            nc.vector.scalar_tensor_tensor(sc[:, n % 3, 0:nk], dist[:, 384 - q * P:512],
                                                           slope * HD ** 0.5, bank[n % 3][:, 0:nk],
                                                           ALU.mult, ALU.add).then_inc(s_read, 1)
                            dve.wait_ge(s_read, n + 1)
                            link(dve, nc.vector.tensor_reduce(mx[:, h, q:q + 1], sc[:, n % 3, 0:nk], AX_X, ALU.max))
                            nc.vector.tensor_scalar(nmx[:, h, q:q + 1], mx[:, h, q:q + 1], -HD ** -0.5, None,
                                                    ALU.mult).then_inc(s_max, 1)

                        def normalised(n):
                            h, q = qunits[n]
                            nk = (q + 1) * P
                            dve.wait_ge(p_done, n + 1)
                            link(dve, nc.vector.reciprocal(ri[:, h, q:q + 1], rs[:, h, q:q + 1]))
                            nc.vector.tensor_scalar(pr[:, n % 3, 0:nk], pr[:, n % 3, 0:nk], ri[:, h, q:q + 1], None,
                                                    ALU.mult).then_inc(p_norm, 1)

                        def head_out(h):
                            dve.wait_ge(o_full, NT * (h + 1))
                            nc.vector.tensor_copy(oa[:, :, h, :], bank[5 + 2 * (h % 2)][:, 0:NT * HD]
                                                  .rearrange("p (t c) -> p t c", t=NT)).then_inc(o_read, 1)

                        for n in range(len(qunits)):
                            biased(n)
                            if n >= 1:
                                normalised(n - 1)
                            if n % NT == NT - 1 and n > NT:
                                head_out(n // NT - 1)
                        normalised(len(qunits) - 1)
                        head_out(H - 1)
                        dve.wait_ge(osq_done, 1)
                        link(dve, nc.vector.tensor_reduce(oss[:, :, :], osq[:, :, :, :], AX_X, ALU.add))
                        nc.vector.tensor_scalar(oss[:, :, :], oss[:, :, :], 1.0 / HD, RMS_EPS, ALU.mult, ALU.add)\
                            .then_inc(oms_done, 1)
                        dve.wait_ge(ort_done, 1)
                        link(dve, nc.vector.reciprocal(oss[:, :, :], oss[:, :, :]))
                        nc.vector.tensor_tensor(oa[:, :, :, :].rearrange("p t h d -> p (t h) d"),
                                                oa[:, :, :, :].rearrange("p t h d -> p (t h) d"),
                                                oss[:, :, :].rearrange("p t h -> p (t h)").unsqueeze(2)
                                                .to_broadcast([P, NT * H, HD]), ALU.mult).then_inc(on_done, 1)
                        for j in range(NJ):
                            nc.vector.tensor_copy(mixT[:, NJ + j, :], rf[:, j, :])
            if stop == 3:
                return finish_early(mixT[:, 0, :])

        nc.clear_and_free_semaphores(part_sems)
        nc.all_engine_barrier()

        x1 = sb("x1", [P, NT, D])
        ln_gb = sb("ln_gb", [P, 2, D])
        ring2 = sb("ring2", [P, 3 * SLOT])
        stats = sb("stats", [P, NT, 2, 6])
        mv = sb("mv", [P, NT, 2])
        rstd = sb("rstd", [P, NT])
        counts = sb("counts", [P, NE])
        most_f = sb("most_f", [P, 1])
        thresholds = sb("thresholds", [P, S // CAP - 1])
        blk_f = sb("blk_f", [P, S // CAP - 1])
        more_i = sb("more_i", [P, 1], I32)
        gate_here = [sem(f"gate_here{i}") for i in range(2)]
        up_in = [sem(f"up_in{i}") for i in range(2)]
        down_here = [sem(f"down_here{i}") for i in range(2)]

        def expert_slot(s, i):
            return (ring2, ring)[s][:, i * SLOT:(i + 1) * SLOT]

        expert_w = (w_exp_gate[0].rearrange("e (p k) n -> e p (k n)", k=KT),
                    w_exp_up[0].rearrange("e (p k) n -> e p (k n)", k=KT),
                    w_exp_down[0].rearrange("e (p k) n -> e p (k n)", k=FT))
        expert_sem = (gate_here, up_in, down_here)

        def load_expert(eng, e, s, i):
            eng.dma_start(expert_slot(s, i), expert_w[i][e]).then_inc(expert_sem[i][s], 16)

        class Norm:

            def __init__(self, i):
                self.i = i
                self.here, self.added, self.var_done, self.rooted, self.scaled, self.shifted = (
                    sem(f"ln{i}_{n}") for n in ("here", "added", "var_done", "rooted", "scaled", "shifted"))
                self.aggr = sem(f"ln{i}_aggr")

            def load(self, eng):
                for h, src in enumerate((ln_g, ln_b)):
                    eng.dma_start(ln_gb[:, h, :], src[0, self.i:self.i + 1, :].to_broadcast([P, D]))\
                        .then_inc(self.here, 16)

            def statistics(self, dve, t):
                dve.wait_ge(self.added, 2 * t + 2)
                for hf in range(2):
                    ins = nc.vector.bn_stats(stats[:, t, hf, :], x1[:, t, hf * 512:(hf + 1) * 512])
                link(dve, ins)
                link(dve, nc.vector.bn_aggr(mv[:, t, :], stats[:, t, :, :].rearrange("p a b -> p (a b)")))
                nc.vector.tensor_scalar(rstd[:, t:t + 1], mv[:, t, 1:2], LN_EPS, None, ALU.add)\
                    .then_inc(self.var_done, 1)

            def root(self, act, t):
                act.wait_ge(self.var_done, t + 1)
                nc.scalar.activation(rstd[:, t:t + 1], rstd[:, t:t + 1], ACT.Sqrt).then_inc(self.rooted, 1)

            def scale(self, dve, t):
                dve.wait_ge(self.rooted, t + 1)
                link(dve, nc.vector.reciprocal(rstd[:, t:t + 1], rstd[:, t:t + 1]))
                link(dve, nc.vector.tensor_scalar(x1[:, t, :], x1[:, t, :], mv[:, t, 0:1], rstd[:, t:t + 1],
                                                  ALU.subtract, ALU.mult))
                if t == 0:
                    dve.wait_ge(self.here, 32)
                link(dve, nc.vector.tensor_tensor(x1[:, t, :], x1[:, t, :], ln_gb[:, 0, :], ALU.mult))
                nc.vector.tensor_tensor(x1[:, t, :], x1[:, t, :], ln_gb[:, 1, :], ALU.add)\
                    .then_inc(self.shifted, 1)

        B = ExitStack()
        with B:
            def sB(name, shape, dt=F32):
                return B.enter_context(nc.sbuf_tensor(name, shape, dt))

            x1T, qmT = xT, mixT
            n1 = Norm(0)
            x_back = sem("x_back")
            wo_full = sem("wo_full")
            t1_full, t1_act, t1_dve = sem("t1_full"), sem("t1_act"), sem("t1_dve")
            qm_full, qm_read = sem("qm_full"), sem("qm_read")

            with nc.Block() as block:
                @block.sync
                def _(sp):
                    for t in range(NT):
                        sp.dma_start(x1[:, t, :], x[0, t * P:(t + 1) * P, :]).then_inc(x_back, 16)
                    n1.load(sp)
                    for i in range(3):
                        load_expert(sp, 0, 0, i)
                    load_group(sp, GQ + 1, (wo_full, 8))
                    load_group(sp, GMO, (wo_full, 8))
                    load_group(sp, GMO + 1, (qm_full, 4))

                @block.tensor
                def _(pe):
                    group_here(pe, GO)
                    group_here(pe, GO + 1)
                    for t in range(NT):
                        for hf in range(2):
                            w = slot(GO + hf, 512)
                            for k in range(2 * NJ):
                                last = nc.tensor.matmul(bank[2 * t + hf][:, :], mixT[:, k, t * P:(t + 1) * P],
                                                        w[:, k, :], start=(k == 0), stop=(k == 2 * NJ - 1))
                            last.then_inc(wo_full, 1)
                    for t in range(NT):
                        pe.wait_ge(n1.shifted, t + 1)
                        for hf in range(2):
                            for k in range(4):
                                c = 4 * hf + k
                                last = nc.tensor.transpose(bank[2 * t + hf][:, k * P:(k + 1) * P],
                                                           x1[:, t, c:D:KT], ident[:, :])
                            last.then_inc(t1_full, 1)
                    pe.wait_ge(t1_act, 4)
                    pe.wait_ge(t1_dve, 4)
                    for i in range(KT):
                        w = slot(GQ + i // 4, 512)
                        group_here(pe, GQ + i // 4)
                        for k in range(KT):
                            last = nc.tensor.matmul(bank[i][:, :], w[:, k, (i % 4) * P:(i % 4 + 1) * P], x1T[:, k, :],
                                                    start=(k == 0), stop=(k == KT - 1))
                        last.then_inc(qm_full, 1)

                @block.scalar
                def _(act):
                    for t in range(NT):
                        n1.root(act, t)
                    for t in range(NT):
                        act.wait_ge(t1_full, 2 * t + 1)
                        nc.scalar.activation(x1T[:, 0:4, t * P:(t + 1) * P],
                                             bank[2 * t][:, :].rearrange("p (k s) -> p k s", k=4),
                                             ACT.Copy).then_inc(t1_act, 1)
                    for i in range(KT):
                        act.wait_ge(qm_full, i + 1)
                        nc.scalar.activation(qmT[:, i, :], bank[i][:, :], ACT.Copy).then_inc(qm_read, 1)

                @block.vector
                def _(dve):
                    dve.wait_ge(x_back, 64)
                    for t in range(NT):
                        for hf in range(2):
                            dve.wait_ge(wo_full, 2 * t + hf + 1)
                            v = x1[:, t, hf * 512:(hf + 1) * 512]
                            nc.vector.scalar_tensor_tensor(v, v, ALPHA, bank[2 * t + hf][:, :], ALU.mult, ALU.add)\
                                .then_inc(n1.added, 1)
                        n1.statistics(dve, t)
                        if t:
                            n1.scale(dve, t - 1)
                    n1.scale(dve, NT - 1)
                    for t in range(NT):
                        dve.wait_ge(t1_full, 2 * t + 2)
                        nc.vector.tensor_copy(x1T[:, 4:8, t * P:(t + 1) * P],
                                              bank[2 * t + 1][:, :].rearrange("p (k s) -> p k s", k=4))\
                            .then_inc(t1_dve, 1)

            omT = xT
            sm = sB("sm", [P, 3, MEM])
            pm = sB("pm", [P, 3, MEM])
            pmT = sB("pmT", [P, 2, MT, S])
            mmx = sB("mmx", [P, MH, NT])
            mnm = sB("mnm", [P, MH, NT])
            mrs = sB("mrs", [P, MH, NT])
            ms_full, ms_max, mp_done, mp_norm = sem("ms_full"), sem("ms_max"), sem("mp_done"), sem("mp_norm")
            mpt_full, mpt_read, mo_full, mo_read = sem("mpt_full"), sem("mpt_read"), sem("mo_full"), sem("mo_read")
            mu_ = [(h, t) for h in range(MH) for t in range(NT)]
            with nc.Block() as block:
                @block.tensor
                def _(pe):
                    def scores(n):
                        h, t = mu_[n]
                        if n >= 3:
                            pe.wait_ge(mp_done, n - 2)
                        for k in range(2):
                            last = nc.tensor.matmul(bank[n % 3][:, 0:MEM], qmT[:, 2 * h + k, t * P:(t + 1) * P],
                                                    kmT[:, 2 * h + k, :], start=(k == 0), stop=(k == 1))
                        last.then_inc(ms_full, 1)

                    def transposed(n):
                        h, t = mu_[n]
                        pe.wait_ge(mp_norm, n + 1)
                        if t == 0 and h:
                            pe.wait_ge(mpt_read, 2 * h)
                        for m in range(MT):
                            last = nc.tensor.transpose(bank[3 + m][:, t * P:(t + 1) * P],
                                                       pm[:, n % 3, m * P:(m + 1) * P], ident[:, :])
                        last.then_inc(mpt_full, 1)

                    def product(h):
                        pe.wait_ge(mpt_read, 2 * h + 2)
                        for i in range(2):
                            if h:
                                pe.wait_ge(mo_read, 2 * h + i - 1)
                            for m in range(MT):
                                c = 2 * h + i
                                last = nc.tensor.matmul(bank[5 + i][:, :], vm[:, m, c * P:(c + 1) * P],
                                                        pmT[:, h % 2, m, :], start=(m == 0), stop=(m == MT - 1))
                            last.then_inc(mo_full, 1)

                    for n in range(len(mu_) + 5):
                        if n < len(mu_):
                            scores(n)
                        if 2 <= n < len(mu_) + 2:
                            transposed(n - 2)
                        if n >= 8 and n % NT == 0:
                            product(n // NT - 2)

                @block.scalar
                def _(act):
                    def out(h):
                        for i in range(2):
                            act.wait_ge(mo_full, 2 * h + i + 1)
                            nc.scalar.activation(omT[:, 2 * h + i, :], bank[5 + i][:, :], ACT.Copy)\
                                .then_inc(mo_read, 1)

                    for n in range(len(mu_) + 3):
                        if n < len(mu_):
                            h, t = mu_[n]
                            act.wait_ge(ms_max, n + 1)
                            if n >= 3:
                                act.wait_ge(mpt_full, n - 2)
                            nc.scalar.activation(pm[:, n % 3, :], bank[n % 3][:, 0:MEM], ACT.Exp,
                                                 bias=mnm[:, h, t:t + 1], scale=MHD ** -0.5,
                                                 accum_out=mrs[:, h, t:t + 1]).then_inc(mp_done, 1)
                        if n >= NT + 2 and (n - NT - 2) % NT == 0:
                            h = (n - NT - 2) // NT
                            for m in range(MT):
                                act.wait_ge(mpt_full, NT * (h + 1))
                                if h >= 2:
                                    act.wait_ge(mo_full, 2 * (h - 1))
                                nc.scalar.activation(pmT[:, h % 2, m, :], bank[3 + m][:, :], ACT.Copy)\
                                    .then_inc(mpt_read, 1)
                            if h:
                                out(h - 1)
                    out(MH - 1)

                @block.vector
                def _(dve):
                    def normalised(n):
                        h, t = mu_[n]
                        dve.wait_ge(mp_done, n + 1)
                        link(dve, nc.vector.reciprocal(mrs[:, h, t:t + 1], mrs[:, h, t:t + 1]))
                        nc.vector.tensor_scalar(pm[:, n % 3, :], pm[:, n % 3, :], mrs[:, h, t:t + 1], None,
                                                ALU.mult).then_inc(mp_norm, 1)

                    for n, (h, t) in enumerate(mu_):
                        dve.wait_ge(ms_full, n + 1)
                        link(dve, nc.vector.tensor_reduce(mmx[:, h, t:t + 1], bank[n % 3][:, 0:MEM], AX_X, ALU.max))
                        nc.vector.tensor_scalar(mnm[:, h, t:t + 1], mmx[:, h, t:t + 1], -MHD ** -0.5, None,
                                                ALU.mult).then_inc(ms_max, 1)
                        if n:
                            normalised(n - 1)
                    normalised(len(mu_) - 1)
            if stop == 4:
                return finish_early(omT[:, 0, :])

            x2T = mixT
            wr = sB("wr", [P, KT, NE])
            brb = sB("brb", [P, NE])
            lg = sB("lg", [NE, S])
            aff = sB("aff", [P, NT, NE])
            sel = sB("sel", [P, NT, NE])
            pair = sB("pair", [P, NT, NGRP, 6])
            g8 = sB("g8", [P, 3, NT, NGRP])
            t1c = sB("t1c", [P, 4, NT])
            oh = sB("oh", [P, 3, NT, NE])
            sc3 = sB("sc3", [P, 3, NT, NE])
            rank = sB("rank", [P, NT, NE])
            wsel = sB("wsel", [P, 3, NT])
            dst_f = sB("dst_f", [P, NT, TOP_K])
            dst_i = sB("dst_i", [P, NT, TOP_K], I32)
            ent = sB("ent", [P, NT, TOP_K, 4], I32)
            void = sB("void", [P, S * NE * 4 // P], I32)
            from_last = sB("from_last", [P, NE])
            eidx = sB("eidx", [P, NE])
            before = sB("before", [P, P])
            ones = sB("ones", [P, P])
            xs_rows = nc.dram_tensor("xs_rows", (S, D), F32, kind="Internal").ap()
            table = nc.dram_tensor("table", (S * NE, 4), I32, kind="Internal").ap()
            n2 = Norm(1)
            mo2_full = sem("mo2_full")
            void_done, void_out = sem("void_done"), sem("void_out")
            router_here, xs_out = sem("router_here"), sem("xs_out")
            t2_full, t2_act, t2_dve = sem("t2_full"), sem("t2_act"), sem("t2_dve")
            lg_full, lg_read, lt_full, aff_done = sem("lg_full"), sem("lg_read"), sem("lt_full"), sem("aff_done")
            oh_done, rk_full, ent_done, ent_out = sem("oh_done"), sem("rk_full"), sem("ent_done"), sem("ent_out")
            rk_read = sem("rk_read")
            flat = "p a b -> p (a b)"
            with nc.Block() as block:
                @block.sync
                def _(sp):
                    n2.load(sp)
                    sp.dma_start(wr[:, :, :], w_router.rearrange("(p k) n -> p k n", k=KT)).then_inc(router_here, 16)
                    sp.dma_start(brb[:, :], b_router.rearrange("(a n) -> a n", a=1).to_broadcast([P, NE]))\
                        .then_inc(router_here, 16)
                    sp.wait_ge(void_done, 1)
                    sp.dma_start(table.rearrange("(p r) f -> p (r f)", p=P), void[:, :]).then_inc(void_out, 16)
                    for i in range(3):
                        if i == 0:
                            sp.wait_ge(mo2_full, 8)
                        load_expert(sp, 1, 1, i)
                    for t in range(NT):
                        sp.wait_ge(n2.shifted, t + 1)
                        sp.dma_start(xs_rows[t * P:(t + 1) * P, :], x1[:, t, :]).then_inc(xs_out, 16)
                    sp.wait_ge(xs_out, 64)

                @block.gpsimd
                def _(pool):
                    link(pool, pool.iota(ent[:, :, :, 0], pattern=[[P, NT], [0, TOP_K]], base=0,
                                         channel_multiplier=1))
                    link(pool, pool.iota(ent[:, :, :, 1], pattern=[[P, NT], [S, TOP_K]], base=0,
                                         channel_multiplier=1))
                    link(pool, pool.memset(ent[:, :, :, 2:4], 0))
                    link(pool, pool.iota(from_last[:, :], pattern=[[-1, NE]], base=NE, channel_multiplier=0,
                                         allow_small_or_imprecise_dtypes=True))
                    link(pool, pool.iota(eidx[:, :], pattern=[[1, NE]], base=0, channel_multiplier=0,
                                         allow_small_or_imprecise_dtypes=True))
                    link(pool, pool.iota(thresholds[:, :], pattern=[[CAP, S // CAP - 1]], base=CAP,
                                         channel_multiplier=0, allow_small_or_imprecise_dtypes=True))
                    link(pool, pool.memset(ones[:, :], 1.0))
                    link(pool, pool.affine_select(out=before[:, :], in_=ones[:, :], compare_op=ALU.is_gt,
                                                  fill=0.0, base=0, pattern=[[1, P]], channel_multiplier=-1))
                    pool.memset(void[:, :], OFF).then_inc(void_done, 1)
                    pool.wait_ge(void_done, 1)
                    pool.wait_ge(void_out, 16)
                    pool.wait_ge(ent_done, 1)
                    for t in range(NT):
                        for k in range(TOP_K):
                            pool.indirect_dma_start(table[:, :],
                                                    bass.IndirectOffsetOnAxis(dst_i[:, t, k:k + 1].bitcast(U32), 0),
                                                    ent[:, t, k, :], None).then_inc(ent_out, 16)
                    pool.wait_ge(ent_out, 16 * NT * TOP_K)

                @block.tensor
                def _(pe):
                    group_here(pe, GMO)
                    group_here(pe, GMO + 1)
                    for t in range(NT):
                        for hf in range(2):
                            w = slot(GMO + hf, 512)
                            for k in range(KT):
                                last = nc.tensor.matmul(bank[2 * t + hf][:, :], omT[:, k, t * P:(t + 1) * P],
                                                        w[:, k, :], start=(k == 0), stop=(k == KT - 1))
                            last.then_inc(mo2_full, 1)
                    for t in range(NT):
                        pe.wait_ge(n2.shifted, t + 1)
                        for hf in range(2):
                            for k in range(4):
                                c = 4 * hf + k
                                last = nc.tensor.transpose(bank[2 * t + hf][:, k * P:(k + 1) * P],
                                                           x1[:, t, c:D:KT], ident[:, :])
                            last.then_inc(t2_full, 1)
                    pe.wait_ge(router_here, 32)
                    for t in range(NT):
                        pe.wait_ge(t2_act, t + 1)
                        pe.wait_ge(t2_dve, t + 1)
                        for k in range(KT):
                            last = nc.tensor.matmul(bank[0][0:NE, t * P:(t + 1) * P], wr[:, k, :],
                                                    x2T[:, k, t * P:(t + 1) * P], start=(k == 0), stop=(k == KT - 1))
                    last.then_inc(lg_full, 1)
                    pe.wait_ge(lg_read, 1)
                    for t in range(NT):
                        last = nc.tensor.transpose(bank[1][:, t * NE:(t + 1) * NE], lg[:, t * P:(t + 1) * P],
                                                   ident[0:NE, 0:NE])
                    last.then_inc(lt_full, 1)
                    pe.wait_ge(oh_done, 1)
                    nc.tensor.matmul(bank[2][:, 0:P], before[:, :], oh[:, 2, :, :], start=True, stop=True)
                    nc.tensor.matmul(bank[2][:, P:2 * P], ones[:, :], oh[:, 2, :, :], start=True, stop=True)\
                        .then_inc(rk_full, 1)

                @block.scalar
                def _(act):
                    for t in range(NT):
                        n2.root(act, t)
                    for t in range(NT):
                        act.wait_ge(t2_full, 2 * t + 1)
                        nc.scalar.activation(x2T[:, 0:4, t * P:(t + 1) * P],
                                             bank[2 * t][:, :].rearrange("p (k s) -> p k s", k=4),
                                             ACT.Copy).then_inc(t2_act, 1)
                    act.wait_ge(lt_full, 1)
                    nc.scalar.activation(aff[:, :, :], bank[1][:, 0:NT * NE].rearrange("p (t e) -> p t e", t=NT),
                                         ACT.Sigmoid).then_inc(aff_done, 1)

                @block.vector
                def _(dve):
                    for t in range(NT):
                        for hf in range(2):
                            dve.wait_ge(mo2_full, 2 * t + hf + 1)
                            v = x1[:, t, hf * 512:(hf + 1) * 512]
                            nc.vector.scalar_tensor_tensor(v, v, ALPHA, bank[2 * t + hf][:, :], ALU.mult, ALU.add)\
                                .then_inc(n2.added, 1)
                        n2.statistics(dve, t)
                        if t:
                            n2.scale(dve, t - 1)
                    n2.scale(dve, NT - 1)
                    for t in range(NT):
                        dve.wait_ge(t2_full, 2 * t + 2)
                        nc.vector.tensor_copy(x2T[:, 4:8, t * P:(t + 1) * P],
                                              bank[2 * t + 1][:, :].rearrange("p (k s) -> p k s", k=4))\
                            .then_inc(t2_dve, 1)
                    dve.wait_ge(lg_full, 1)
                    nc.vector.tensor_copy(lg[:, :], bank[0][0:NE, :]).then_inc(lg_read, 1)
                    dve.wait_ge(aff_done, 1)
                    dve.wait_ge(void_done, 1)
                    V = nc.vector
                    link(dve, V.tensor_tensor(sel[:, :, :], aff[:, :, :], brb[:, :].unsqueeze(1)
                                              .to_broadcast([P, NT, NE]), ALU.add))
                    s4 = sel[:, :, :].rearrange("p t (g i) -> p (t g) i", i=EPG)
                    pr6 = pair[:, :, :, :].rearrange("p t g i -> p (t g) i")
                    V.tensor_tensor(pr6[:, :, 0:3], s4[:, :, 0:3], s4[:, :, 1:4], ALU.add)
                    V.tensor_tensor(pr6[:, :, 3:5], s4[:, :, 0:2], s4[:, :, 2:4], ALU.add)
                    link(dve, V.tensor_tensor(pr6[:, :, 5:6], s4[:, :, 0:1], s4[:, :, 3:4], ALU.add))
                    grp, geq, gsel = (g8[:, i, :, :] for i in range(3))
                    link(dve, V.tensor_reduce(grp, pair[:, :, :, :], AX_X, ALU.max))

                    def first_largest(values, n, tmp_, onehot, wts, m):
                        shape = [P, NT, n]
                        link(dve, V.tensor_reduce(m, values, AX_X, ALU.max))
                        link(dve, V.tensor_tensor(tmp_, values, m.unsqueeze(2).to_broadcast(shape), ALU.is_equal))
                        link(dve, V.tensor_tensor(tmp_, tmp_, wts.unsqueeze(1).to_broadcast(shape), ALU.mult))
                        link(dve, V.tensor_reduce(m, tmp_, AX_X, ALU.max))
                        link(dve, V.tensor_tensor(onehot, tmp_, m.unsqueeze(2).to_broadcast(shape), ALU.is_equal))

                    first_largest(grp, NGRP, geq, gsel, from_last[:, NE - NGRP:NE], t1c[:, 0, :])
                    out_, masked, tmp_ = (sc3[:, i, :, :] for i in range(3))
                    gb = gsel.rearrange("p t g -> p (t g)").unsqueeze(2).to_broadcast([P, NT * NGRP, EPG])
                    as4 = lambda v: v.rearrange("p t (g i) -> p (t g) i", i=EPG)
                    link(dve, V.tensor_scalar(as4(out_), gb, 1.0, -NEG, ALU.subtract, ALU.mult))
                    link(dve, V.tensor_tensor(as4(masked), as4(sel[:, :, :]), gb, ALU.mult))
                    link(dve, V.tensor_tensor(masked, masked, out_, ALU.add))
                    first_largest(masked, NE, tmp_, oh[:, 0, :, :], from_last[:, :], t1c[:, 1, :])
                    link(dve, V.scalar_tensor_tensor(masked, oh[:, 0, :, :], 3 * NEG, masked, ALU.mult, ALU.add))
                    first_largest(masked, NE, tmp_, oh[:, 1, :, :], from_last[:, :], t1c[:, 2, :])
                    V.tensor_tensor(oh[:, 2, :, :], oh[:, 0, :, :], oh[:, 1, :, :], ALU.add).then_inc(oh_done, 1)
                    for k in range(TOP_K):
                        link(dve, V.tensor_tensor(tmp_, oh[:, k, :, :], aff[:, :, :], ALU.mult))
                        link(dve, V.tensor_reduce(wsel[:, k, :], tmp_, AX_X, ALU.add))
                    link(dve, V.tensor_tensor(wsel[:, 2, :], wsel[:, 0, :], wsel[:, 1, :], ALU.add))
                    link(dve, V.reciprocal(wsel[:, 2, :], wsel[:, 2, :]))
                    for k in range(TOP_K):
                        V.tensor_tensor(ent[:, :, k, 2].bitcast(F32), wsel[:, k, :], wsel[:, 2, :], ALU.mult)
                    dve.wait_ge(rk_full, 1)
                    cum = bank[2][:, 0:P].rearrange("p (t e) -> p t e", t=NT)
                    tot = bank[2][:, P:2 * P].rearrange("p (t e) -> p t e", t=NT)
                    offs = sc3[:, 0, :, :]
                    link(dve, V.memset(offs[:, 0, :], 0.0))
                    for t in range(1, NT):
                        link(dve, V.tensor_tensor(offs[:, t, :], tot[:, t - 1, :], offs[:, t - 1, :], ALU.add))
                    link(dve, V.tensor_tensor(counts[:, :], tot[:, NT - 1, :], offs[:, NT - 1, :], ALU.add))
                    link(dve, V.tensor_tensor(rank[:, :, :], cum, offs, ALU.add))
                    link(dve, V.tensor_reduce(most_f[:, :], counts[:, :], AX_X, ALU.max))
                    link(dve, V.tensor_scalar(blk_f[:, :], thresholds[:, :], most_f[:, 0:1], None, ALU.is_lt))
                    link(dve, V.tensor_reduce(most_f[:, :], blk_f[:, :], AX_X, ALU.add))
                    link(dve, V.tensor_copy(more_i[:, :], most_f[:, :]))
                    link(dve, V.tensor_scalar(rank[:, :, :], rank[:, :, :], float(NE), None, ALU.mult))
                    link(dve, V.tensor_tensor(rank[:, :, :], rank[:, :, :], eidx[:, :].unsqueeze(1)
                                              .to_broadcast([P, NT, NE]), ALU.add))
                    for k in range(TOP_K):
                        link(dve, V.tensor_tensor(tmp_, oh[:, k, :, :], rank[:, :, :], ALU.mult))
                        link(dve, V.tensor_reduce(dst_f[:, :, k:k + 1], tmp_, AX_X, ALU.add))
                    V.tensor_copy(dst_i[:, :, :], dst_f[:, :, :]).then_inc(ent_done, 1)
            if stop == 5:
                return finish_early(xT[:, 0, :])

        NR = NE // 2
        tabs = sb("tabs", [P, NE, 4], I32)
        halfp = sb("halfp", [P, 3])
        tokc = sb("tokc", [P, 2, 1], I32)
        rowc = sb("rowc", [P, 2, 1], I32)
        gatec = sb("gatec", [P, 2, 1])
        xg = sb("xg", [CAP, 2, D])
        xgT = sb("xgT", [P, 2, KT, CAP])
        sil = sb("sil", [CAP, 2, DE])
        hb = sb("hb", [CAP, 2, DE])
        hT = sb("hT", [P, 2, FT, CAP])
        ye = sb("ye", [P, 2, DE])
        y_rows = nc.dram_tensor("y_rows", (TOP_K * S * 2, D // 2), F32, kind="Internal").ap()
        table_v = table.rearrange("(r e) f -> r e f", e=NE)
        n3 = Norm(2)
        tabs_here, tabs_done, xg_zero = sem("tabs_here"), sem("tabs_done"), sem("xg_zero")
        y_read = [sem(f"y_read{i}") for i in range(NT)]
        out_done = sem("out_done")

        def side_sems(name):
            return [sem(f"{name}{s}") for s in range(2)]

        xg_here, xgt_full, xgt_read = side_sems("xg_here"), side_sems("xgt_full"), side_sems("xgt_read")
        gu_full, sil_done, h_done = side_sems("gu_full"), side_sems("sil_done"), side_sems("h_done")
        ht_full, ht_read, y_full = side_sems("ht_full"), side_sems("ht_read"), side_sems("y_full")
        y_scaled, y_out = side_sems("y_scaled"), side_sems("y_out")
        gate_col, tokc_done, rowc_done = side_sems("gate_col"), side_sems("tokc_done"), side_sems("rowc_done")
        both = (0, 1)

        def further_blocks(eng, body):
            n = eng.value_load(more_i[0:1, 0:1], min_val=0, max_val=S // CAP - 1)
            with eng.If(n > 0):
                with eng.Fori(1, n + 1) as blk:
                    body(blk)

        with nc.Block() as block:
            @block.sync
            def _(sp):
                n3.load(sp)

                def table_in(blk):
                    for h in both:
                        sp.dma_start(tabs[h * CAP:(h + 1) * CAP, :, :], table_v[bass.ds(blk * CAP, CAP), :, :]
                                     ).then_inc(tabs_here, 16)

                def weights(r, i):
                    for s in both:
                        sp.wait_ge(gu_full[s], i)
                        load_expert(sp, 2 * r + s, s, 0)
                        load_expert(sp, 2 * r + s, s, 1)
                        sp.wait_ge(y_full[s], i)
                        load_expert(sp, 2 * r + s, s, 2)

                table_in(0)
                with sp.Fori(1, NR) as r:
                    weights(r, r)

                def block_(blk):
                    for s in both:
                        sp.wait_ge(y_out[s], 16 * NR * blk)
                    table_in(blk)
                    with sp.Fori(0, NR) as r:
                        weights(r, blk * NR + r)

                further_blocks(sp, block_)

            @block.gpsimd
            def _(pool):
                link(pool, pool.memset(halfp[0:CAP, 0:2], 0.0))
                link(pool, pool.memset(halfp[CAP:P, 0:1], 1.0))
                link(pool, pool.memset(halfp[CAP:P, 1:2], 0.0))
                link(pool, pool.memset(halfp[:, 2:3], 1.0))
                pool.memset(xg[:, :, :], 0.0).then_inc(xg_zero, 1)
                zero_i, one_f = halfp[:, 1:2].bitcast(I32), halfp[:, 2:3]
                limit = pool.alloc_register(name="limit")
                limits = pool.alloc_register(name="limits")
                pool.reg_mov(limits, 0)

                def below(rows):
                    pool.reg_add(limit, limits, rows - 1)
                    return limit

                pool.wait_ge(xg_zero, 1)

                def gather(r, i, s, start=False):
                    if not start:
                        pool.wait_ge(xgt_full[s], i)
                    pool.tensor_tensor(tokc[:, s, :], tabs[:, 2 * r + s, 0:1], zero_i, ALU.add).then_inc(tokc_done[s], 1)
                    pool.wait_ge(tokc_done[s], i + 1)
                    pool.indirect_dma_start(xg[:, s, :], None, xs_rows[:, :],
                                            bass.IndirectOffsetOnAxis(tokc[0:CAP, s, :].bitcast(U32), 0),
                                            bounds_check=below(S), oob_is_err=False).then_inc(xg_here[s], 16)

                def scatter(r, i, s, start=False):
                    if not start:
                        pool.wait_ge(y_out[s], 16 * i)
                    pool.tensor_tensor(rowc[:, s, :], tabs[:, 2 * r + s, 1:2], zero_i, ALU.add).then_inc(rowc_done[s], 1)
                    pool.wait_ge(rowc_done[s], i + 1)
                    pool.tensor_tensor(gatec[:, s, :], tabs[:, 2 * r + s, 2:3].bitcast(F32), one_f, ALU.mult).then_inc(gate_col[s], 1)
                    pool.wait_ge(y_scaled[s], i + 1)
                    pool.indirect_dma_start(y_rows[:, :], bass.IndirectOffsetOnAxis(rowc[:, s, :].bitcast(U32), 0),
                                            ye[:, s, :], None, bounds_check=below(TOP_K * S * 2), oob_is_err=False)\
                        .then_inc(y_out[s], 16)

                def rounds(first, start=False):
                    for s in both:
                        gather(0, first, s, start)
                    for s in both:
                        gather(1, first + 1, s)
                    for s in both:
                        scatter(0, first, s, start)
                    with pool.Fori(1, NR - 1) as r:
                        for s in both:
                            gather(r + 1, first + r + 1, s)
                        for s in both:
                            scatter(r, first + r, s)
                    for s in both:
                        scatter(NR - 1, first + NR - 1, s)

                pool.wait_ge(tabs_done, 1)
                rounds(0, start=True)

                def block_(blk):
                    pool.wait_ge(xg_zero, 1)
                    pool.wait_ge(tabs_done, blk + 1)
                    rounds(blk * NR)

                further_blocks(pool, block_)
                for s in both:
                    pool.wait_ge(y_out[s], 16 * NR)

            @block.tensor
            def _(pe):
                def turn(dst, src, first):
                    if first:
                        return nc.tensor.matmul(dst, src, ident[0:CAP, 0:CAP], start=True, stop=True)
                    return nc.tensor.transpose(dst, src, ident[0:CAP, 0:CAP])

                def round_(i, start=False):
                    for s in both:
                        pe.wait_ge(xg_here[s], 16 * (i + 1))
                        for k in range(KT):
                            last = turn(bank[s][:, k * CAP:(k + 1) * CAP], xg[:, s, k:D:KT], k == 0)
                        last.then_inc(xgt_full[s], 1)
                    for s in both:
                        pe.wait_ge(xgt_read[s], i + 1)
                        pe.wait_ge(gate_here[s], 16 * (i + 1))
                        pe.wait_ge(up_in[s], 16 * (i + 1))
                        for k in range(KT):
                            for m in both:
                                last = nc.tensor.matmul(bank[2 + s][m * CAP:(m + 1) * CAP, :], xgT[:, s, k, :],
                                                        expert_slot(s, m)[:, k * DE:(k + 1) * DE],
                                                        start=(k == 0), stop=(k == KT - 1))
                        last.then_inc(gu_full[s], 1)
                        pe.wait_ge(h_done[s], i + 1)
                        for k in range(FT):
                            last = turn(bank[4 + s][:, k * CAP:(k + 1) * CAP], hb[:, s, k:DE:FT], k == 0)
                        last.then_inc(ht_full[s], 1)
                        pe.wait_ge(ht_read[s], i + 1)
                        pe.wait_ge(down_here[s], 16 * (i + 1))
                        if not start:
                            pe.wait_ge(y_scaled[s], i)
                        for k in range(FT):
                            for m in both:
                                o = k * D + m * 512
                                last = nc.tensor.matmul(bank[6 + s][m * CAP:(m + 1) * CAP, :], hT[:, s, k, :],
                                                        expert_slot(s, 2)[:, o:o + 512],
                                                        start=(k == 0), stop=(k == FT - 1))
                        last.then_inc(y_full[s], 1)

                round_(0, start=True)
                with pe.Fori(1, NR) as r:
                    round_(r)

                def block_(blk):
                    with pe.Fori(0, NR) as r:
                        round_(blk * NR + r)

                further_blocks(pe, block_)

            @block.scalar
            def _(act):
                def round_(i):
                    for s in both:
                        act.wait_ge(xgt_full[s], i + 1)
                        nc.scalar.activation(xgT[:, s, :, :].rearrange("p k c -> p (k c)"), bank[s][:, :], ACT.Copy)\
                            .then_inc(xgt_read[s], 1)
                    for s in both:
                        act.wait_ge(gu_full[s], i + 1)
                        nc.scalar.activation(sil[:, s, :], bank[2 + s][0:CAP, :], ACT.Silu).then_inc(sil_done[s], 1)
                        act.wait_ge(y_full[s], i + 1)
                        act.wait_ge(gate_col[s], i + 1)
                        nc.scalar.activation(ye[:, s, :], bank[6 + s][:, :], ACT.Copy, scale=gatec[:, s, :])\
                            .then_inc(y_scaled[s], 1)

                with act.Fori(0, NR) as r:
                    round_(r)

                def block_(blk):
                    with act.Fori(0, NR) as r:
                        round_(blk * NR + r)

                further_blocks(act, block_)

            @block.vector
            def _(dve):
                def rows_of(blk):
                    dve.wait_ge(tabs_here, 32 * (blk + 1))
                    nc.vector.tensor_scalar(tabs[:, :, 1], tabs[:, :, 1], 2.0, halfp[:, 0:1], ALU.mult, ALU.add)\
                        .then_inc(tabs_done, 1)

                def round_(i):
                    for s in both:
                        dve.wait_ge(sil_done[s], i + 1)
                        nc.vector.tensor_tensor(hb[:, s, :], bank[2 + s][CAP:P, :], sil[:, s, :], ALU.mult)\
                            .then_inc(h_done[s], 1)
                        dve.wait_ge(ht_full[s], i + 1)
                        nc.vector.tensor_copy(hT[:, s, :, :].rearrange("p k c -> p (k c)"),
                                              bank[4 + s][:, 0:FT * CAP]).then_inc(ht_read[s], 1)

                dve.wait_ge(xg_zero, 1)
                rows_of(0)
                with dve.Fori(0, NR) as r:
                    round_(r)

                def block_(blk):
                    rows_of(blk)
                    with dve.Fori(0, NR) as r:
                        round_(blk * NR + r)

                further_blocks(dve, block_)

        yb = ring[:, 0:NT * 2 * D].rearrange("p (t k d) -> p t k d", t=NT, k=TOP_K)
        y_v = y_rows.rearrange("(k t h) c -> t k (h c)", k=TOP_K, h=2)
        with nc.Block() as block:
            @block.sync
            def _(sp):
                for t in range(NT):
                    sp.dma_start(yb[:, t, :, :], y_v[t * P:(t + 1) * P, :, :]).then_inc(y_read[t], 16)
                for t in range(NT):
                    sp.wait_ge(n3.shifted, t + 1)
                    sp.dma_start(out[0, t * P:(t + 1) * P, :], x1[:, t, :]).then_inc(out_done, 16)
                sp.wait_ge(out_done, 16 * NT)

            @block.scalar
            def _(act):
                for t in range(NT):
                    n3.root(act, t)

            @block.vector
            def _(dve):
                for t in range(NT):
                    dve.wait_ge(y_read[t], 16)
                    link(dve, nc.vector.tensor_tensor(yb[:, t, 0, :], yb[:, t, 0, :], yb[:, t, 1, :], ALU.add))
                    for hf in range(2):
                        v = slice(hf * 512, (hf + 1) * 512)
                        nc.vector.scalar_tensor_tensor(x1[:, t, v], x1[:, t, v], ALPHA, yb[:, t, 0, v],
                                                       ALU.mult, ALU.add).then_inc(n3.added, 1)
                    n3.statistics(dve, t)
                    if t:
                        n3.scale(dve, t - 1)
                n3.scale(dve, NT - 1)


_INS = ["x", "mem", "w_in", "mu_shift", "w0", "w_decay_up", "a0", "w_iclr_up", "w_gate_up", "k_k", "k_a", "r_k",
        "lnx_g", "lnx_b", "attn_out_g", "w_out", "w_mem_q", "w_mem_kv", "w_mem_o", "w_router", "b_router",
        "w_exp_gate", "w_exp_up", "w_exp_down", "ln_g", "ln_b"]


def kernel(**inputs):
    import numpy as np
    import concourse.bacc as bacc
    from concourse.bass_utils import run_bass_kernel_spmd

    nc = bacc.Bacc("TRN2", target_bir_lowering=False, num_devices=1)
    arrays, args = {}, []
    for name in _INS:
        a = np.ascontiguousarray(inputs[name])
        arrays[f"in_{name}"] = a
        args.append(nc.dram_tensor(f"in_{name}", a.shape, mybir.dt.from_np(a.dtype), kind="ExternalInput").ap())
    out = nc.dram_tensor("out_0", (1, S, D), F32, kind="ExternalOutput").ap()
    hybrid_decoder_trunk(nc, *args, out)
    result = run_bass_kernel_spmd(nc, [arrays], core_ids=[0])
    return result.results[0]["out_0"]
```

```python
from contextlib import ExitStack

import concourse.bass as bass
from concourse import mybir

ALU = mybir.AluOpType
ACT = mybir.ActivationFunctionType
F32 = mybir.dt.float32
I32 = mybir.dt.int32
U32 = mybir.dt.uint32
AX_X = mybir.AxisListType.X

P = 128
S = 512
D = 1024
KT = D // P
NT = S // P
MEM = 256
MT = MEM // P
H = 8
HD = 64
W = H * HD
NJ = W // P
CH = 64
NC = S // CH
MH = 4
MHD = D // MH
NE = 32
NGRP = 8
EPG = NE // NGRP
DE = 512
FT = DE // P
CAP = 64
TOP_K = 2
OFF = 1 << 20
NEG = -1e30
LN_EPS = 1e-5
RMS_EPS = 1e-6
GN_EPS = 64e-5
ALPHA = 2.0 ** 0.25
DECAY = 0.6065306597126334
ATT0 = 3 * W
SLOT = KT * 512

ROWS = {}
_n = 0
for _name, _k in (("mu", 14), ("w0", 4), ("a0", 4), ("k_k", 4), ("k_a", 4), ("r_k", 4),
                  ("lnx_g", 4), ("lnx_b", 4), ("attn_out_g", 4)):
    ROWS[_name] = (_n, _k)
    _n += _k
NROWS = _n


def hybrid_decoder_trunk(nc, x, mem, w_in, mu_shift, w0, w_decay_up, a0, w_iclr_up, w_gate_up, k_k, k_a,
                         r_k, lnx_g, lnx_b, attn_out_g, w_out, w_mem_q, w_mem_kv, w_mem_o, w_router,
                         b_router, w_exp_gate, w_exp_up, w_exp_down, ln_g, ln_b, out):
    ctx = ExitStack()
    with ctx:
        def sb(name, shape, dt=F32):
            return ctx.enter_context(nc.sbuf_tensor(name, shape, dt))

        def sem(name):
            return ctx.enter_context(nc.semaphore(name))

        part_sems = []

        def part_sem(name):
            part_sems.append(nc.alloc_semaphore(name=name))
            return part_sems[-1]

        dve_step, act_step, pool_step = sem("dve_step"), sem("act_step"), sem("pool_step")
        steps = {"dve": 0, "act": 0, "pool": 0}

        def link(eng, ins):
            name, step = {id(nc.vector): ("dve", dve_step), id(nc.scalar): ("act", act_step),
                          id(nc.gpsimd): ("pool", pool_step)}[id(eng)]
            steps[name] += 1
            ins.then_inc(step, 1)
            eng.wait_ge(step, steps[name])

        bank = [ctx.enter_context(nc.psum_tensor(f"bank{i}", [P, 512], F32)) for i in range(8)]

        ident = sb("ident", [P, P])
        blkones = sb("blkones", [P, P])
        cols = sb("cols", [P, NROWS])
        omm = sb("omm", [P, 14])
        xT = sb("xT", [P, KT, S])
        mixT = sb("mixT", [P, 2 * NJ, S])
        ring = sb("ring", [P, 3 * SLOT])
        ar = sb("ar", [P, 2, NJ, S])
        kmT = ar[:, 0, :, :].rearrange("p j s -> p (j s)").rearrange("p (k m) -> p k m", k=KT)
        vm = ar[:, 1, :, :].rearrange("p j s -> p (j s)").rearrange("p (t d) -> p t d", t=MT)

        def col(name, i):
            return cols[:, ROWS[name][0] + i:ROWS[name][0] + i + 1]

        def slot(g, width):
            o = (g % 3) * SLOT
            return ring[:, o:o + KT * width].rearrange("p (k n) -> p k n", k=KT)

        wv = w_in[0].rearrange("(p k) n -> p k n", k=KT)
        kvv = w_mem_kv[0].rearrange("(p k) n -> p k n", k=KT)
        outv = w_out[0].rearrange("(k p) n -> p k n", p=P)
        qv = w_mem_q[0].rearrange("(p k) n -> p k n", k=KT)
        ov = w_mem_o[0].rearrange("(k p) n -> p k n", p=P)
        groups = ([wv[:, :, ATT0 + 3 * W:ATT0 + 3 * W + 2 * P]]
                  + [wv[:, :, c:c + W] for c in (ATT0 + W, ATT0, ATT0 + 2 * W, 2 * W, 0, W)]
                  + [kvv[:, :, c:c + 512] for c in range(0, 2 * D, 512)]
                  + [v[:, :, c:c + 512] for v in (outv, qv, ov) for c in (0, 512)])
        GL, GK, GR, GV, GAV, GAQ, GAK, GKV, GO, GQ, GMO = 0, 1, 2, 3, 4, 5, 6, 7, 11, 13, 15
        w_here = [sem(f"w_here{i}") for i in range(3)]

        def load_group(eng, g, held=None):
            if held:
                eng.wait_ge(*held)
            n = groups[g].shape[2]
            eng.dma_start(slot(g, n), groups[g]).then_inc(w_here[g % 3], 16)

        def group_here(eng, g):
            eng.wait_ge(w_here[g % 3], 16 * (g // 3 + 1))

        A = ExitStack()
        with A:
            def sa(name, shape, dt=F32):
                return A.enter_context(nc.sbuf_tensor(name, shape, dt))

            bt = sa("bt", [P, NJ, S])
            kt_ = sa("kt_", [P, NJ, S])
            vf = sa("vf", [P, NJ, S])
            rf = sa("rf", [P, NJ, S])
            sgz = sa("sgz", [P, S])
            wc = sa("wc", [P, NJ, NC])
            wg = sa("wg", [P, W])
            av = sa("av", [P, NT, W])
            mask = sa("mask", [P, 2, 2, 2, CH])
            maskT = sa("maskT", [P, 4, CH])
            id64 = sa("id64", [P, CH])

            A1 = ExitStack()
            with A1:
                def s1(name, shape, dt=F32):
                    return A1.enter_context(nc.sbuf_tensor(name, shape, dt))

                kf = s1("kf", [P, NJ, S])
                af = s1("af", [P, NJ, S])
                wf = s1("wf", [P, NJ, S])
                lf = s1("lf", [P, S])
                sq = s1("sq", [P, NJ, S])
                tmp = s1("tmp", [P, 4, S])
                zb = s1("zb", [P, 2, S + 1])
                wup = s1("wup", [P, W])
                rows = s1("rows", [NROWS, P])
                starts = s1("starts", [P, S])
                xtm = mixT[:, :, :].rearrange("p a s -> p (a s)").rearrange("p (t d) -> p t d", t=NT)

                x_here = [part_sem(f"x_here{i}") for i in range(NT)]
                rows_here, up_here = part_sem("rows_here"), part_sem("up_here")
                ident_done, consts_done = part_sem("ident_done"), part_sem("consts_done")
                xt_full, xt_dve, xt_act = part_sem("xt_full"), part_sem("xt_dve"), part_sem("xt_act")
                cols_full, cols_done, omm_done = part_sem("cols_full"), part_sem("cols_done"), part_sem("omm_done")
                job_full = part_sem("job_full")
                z_read, dec_read = part_sem("z_read"), part_sem("dec_read")
                icl_read, nrm_read = part_sem("icl_read"), part_sem("nrm_read")
                shifted, tanh_done = part_sem("shifted"), part_sem("tanh_done")
                sgz_done, w_done = part_sem("sgz_done"), part_sem("w_done")
                sq_done, rt_done, scanned = part_sem("sq_done"), part_sem("rt_done"), part_sem("scanned")

                AV_EARLY = 2
                jobs = [("L", 0), ("L", 1), ("K", 0), ("K", 1)]
                for j in range(NJ):
                    jobs += [("dec", j), ("icl", j)]
                jobs += [("K", 2), ("K", 3), ("R", 0)] + [("nrm", j) for j in range(NJ)]
                jobs += [("R", j) for j in range(1, NJ)]
                jobs += [("V", j) for j in range(NJ)]
                jobs += [("AV", t) for t in range(AV_EARLY)]
                shift_order = [job for job in jobs if job[0] in ("L", "K", "R", "V")]
                mu_col = {"R": 0, "K": 4, "V": 8, "L": 12}

                def nth(job):
                    return shift_order.index(job) + 1

                def shift_dest(kind, j):
                    if kind == "L":
                        return (lf, sgz)[j][:, :]
                    return {"K": kf, "R": rf, "V": vf}[kind][:, j, :]

                def wait_bank_free(eng, n):
                    if n >= 8:
                        kind, j = jobs[n - 8]
                        if kind in ("L", "K", "R", "V"):
                            eng.wait_ge(z_read, nth((kind, j)))
                        else:
                            eng.wait_ge({"dec": dec_read, "icl": icl_read, "nrm": nrm_read}[kind], j + 1)

                with nc.Block() as block:
                    @block.sync
                    def _(sp):
                        for t in range(NT):
                            sp.dma_start(xtm[:, t, :], x[0, t * P:(t + 1) * P, :]).then_inc(x_here[t], 16)
                        load_group(sp, GL)
                        sp.wait_ge(rows_here, 16 * len(ROWS))
                        load_group(sp, GK)
                        load_group(sp, GR)
                        sp.dma_start(wup[0:64, :], w_decay_up[0]).then_inc(up_here, 16)
                        sp.dma_start(wup[64:128, :], w_iclr_up[0]).then_inc(up_here, 16)
                        sp.dma_start(wg[:, :], w_gate_up[0]).then_inc(up_here, 16)
                        for g, last in ((3, ("L", 1)), (4, ("K", 3)), (5, ("R", 3)), (6, ("V", 3))):
                            load_group(sp, g, (job_full, jobs.index(last) + 1))

                    @block.gpsimd
                    def _(pool):
                        link(pool, pool.memset(ident[:, :], 0.0))
                        pool.affine_select(out=ident[:, :], in_=ident[:, :], compare_op=ALU.not_equal,
                                           fill=1.0, base=0, pattern=[[-1, P]], channel_multiplier=1)\
                            .then_inc(ident_done, 1)
                        pool.wait_ge(ident_done, 1)
                        link(pool, pool.memset(id64[:, :], 0.0))
                        link(pool, pool.memset(blkones[:, :], 0.0))
                        link(pool, pool.memset(mask[:, :, :, :, :], 1.0))
                        link(pool, pool.memset(maskT[:, :, :], 1.0))
                        link(pool, pool.memset(starts[:, :], 0.0))
                        link(pool, pool.memset(zb[:, :, 0:1], 0.0))
                        for h in range(2):
                            rs = slice(64 * h, 64 * h + 64)
                            link(pool, pool.memset(blkones[rs, 64 * h:64 * h + 64], 1.0))
                            link(pool, pool.affine_select(out=id64[rs, :], in_=id64[rs, :],
                                                          compare_op=ALU.not_equal, fill=1.0, base=0,
                                                          pattern=[[-1, CH]], channel_multiplier=1))
                            m = mask[rs, :, :, :, :].rearrange("p u b a t -> p (u b) a t")
                            link(pool, pool.affine_select(out=m, in_=m, compare_op=ALU.is_gt, fill=0.0, base=0,
                                                          pattern=[[0, 4], [1, 2], [1, CH]],
                                                          channel_multiplier=-1))
                            pool.affine_select(out=maskT[rs, :, :], in_=maskT[rs, :, :],
                                               compare_op=ALU.is_gt, fill=0.0, base=0,
                                               pattern=[[0, 4], [-1, CH]], channel_multiplier=1)\
                                .then_inc(consts_done, 1)
                            pool.wait_ge(consts_done, h + 1)

                    @block.tensor
                    def _(pe):
                        pe.wait_ge(ident_done, 1)
                        for t in range(NT):
                            pe.wait_ge(x_here[t], 16)
                            for hf in range(2):
                                for k in range(4):
                                    c = 4 * hf + k
                                    last = nc.tensor.transpose(bank[2 * t + hf][:, k * P:(k + 1) * P],
                                                               xtm[:, t, c:D:KT], ident[:, :])
                                last.then_inc(xt_full, 1)
                        pe.wait_ge(rows_here, 16 * len(ROWS))
                        pe.wait_ge(xt_dve, 1)
                        nc.tensor.transpose(bank[0][:, 0:NROWS], rows[:, :], ident[0:NROWS, 0:NROWS])\
                            .then_inc(cols_full, 1)
                        pe.wait_ge(xt_dve, 4)
                        pe.wait_ge(xt_act, 4)
                        pe.wait_ge(cols_done, 1)
                        for n, (kind, j) in enumerate(jobs):
                            dst = bank[n % 8]
                            wait_bank_free(pe, n)
                            if kind in ("L", "K", "R", "V"):
                                g = {"L": GL, "K": GK, "R": GR, "V": GV}[kind]
                                w = slot(g, 256 if kind == "L" else 512)
                                group_here(pe, g)
                                for k in range(KT):
                                    last = nc.tensor.matmul(dst[:, :], w[:, k, j * P:(j + 1) * P], xT[:, k, :],
                                                            start=(k == 0), stop=(k == KT - 1))
                                last.then_inc(job_full, 1)
                            elif kind == "AV":
                                group_here(pe, GAV)
                                for k in range(KT):
                                    last = nc.tensor.matmul(dst[:, :], xT[:, k, j * P:(j + 1) * P], slot(GAV, 512)[:, k, :],
                                                            start=(k == 0), stop=(k == KT - 1))
                                last.then_inc(job_full, 1)
                            elif kind == "dec":
                                pe.wait_ge(up_here, 48)
                                pe.wait_ge(tanh_done, 1)
                                nc.tensor.matmul(dst[:, :], wup[0:64, j * P:(j + 1) * P], lf[0:64, :],
                                                 start=True, stop=True).then_inc(job_full, 1)
                            elif kind == "icl":
                                pe.wait_ge(shifted, 1)
                                nc.tensor.matmul(dst[:, :], wup[64:128, j * P:(j + 1) * P], lf[64:128, :],
                                                 start=True, stop=True).then_inc(job_full, 1)
                            else:
                                pe.wait_ge(consts_done, 2)
                                pe.wait_ge(sq_done, j + 1)
                                nc.tensor.matmul(dst[:, :], blkones[:, :], sq[:, j, :],
                                                 start=True, stop=True).then_inc(job_full, 1)

                    @block.scalar
                    def _(act):
                        for name, src in (("mu", mu_shift[0]), ("w0", w0[0]), ("a0", a0[0]), ("k_k", k_k[0]),
                                          ("k_a", k_a[0]), ("r_k", r_k[0].rearrange("h d -> (h d)")),
                                          ("lnx_g", lnx_g[0]), ("lnx_b", lnx_b[0]),
                                          ("attn_out_g", attn_out_g[0])):
                            r, k = ROWS[name]
                            act.dma_start(rows[r:r + k, :], src.rearrange("(c p) -> c p", p=P))\
                                .then_inc(rows_here, 16)
                        for b in range(1, 8, 2):
                            act.wait_ge(xt_full, b + 1)
                            t, hf = divmod(b, 2)
                            nc.scalar.activation(xT[:, 4 * hf:4 * hf + 4, t * P:(t + 1) * P],
                                                 bank[b][:, :].rearrange("p (k s) -> p k s", k=4),
                                                 ACT.Copy).then_inc(xt_act, 1)
                        act.wait_ge(omm_done, 1)
                        act.wait_ge(consts_done, 2)
                        for n, (kind, j) in enumerate(jobs):
                            if kind in ("L", "K", "R", "V"):
                                i = mu_col[kind] + j
                                m = nth((kind, j))
                                act.wait_ge(job_full, n + 1)
                                if m > 2:
                                    act.wait_ge(shifted, m - 2)
                                nc.scalar.activation(zb[:, (m - 1) % 2, 1:S + 1], bank[n % 8][:, :], ACT.Copy)
                                nc.scalar.activation(shift_dest(kind, j), bank[n % 8][:, :], ACT.Copy,
                                                     scale=omm[:, i:i + 1]).then_inc(z_read, 1)
                            if kind == "AV":
                                act.wait_ge(job_full, n + 1)
                                nc.scalar.activation(av[:, j, :], bank[n % 8][:, :], ACT.Copy)
                            if (kind, j) == ("L", 1):
                                act.wait_ge(shifted, 1)
                                nc.scalar.activation(lf[0:64, :], lf[0:64, :], ACT.Tanh).then_inc(tanh_done, 1)
                                act.wait_ge(shifted, 2)
                                nc.scalar.activation(sgz[:, :], sgz[:, :], ACT.Sigmoid).then_inc(sgz_done, 1)
                            if kind == "dec":
                                act.wait_ge(job_full, n + 1)
                                nc.scalar.activation(wf[:, j, :], bank[n % 8][:, :], ACT.Sigmoid,
                                                     bias=col("w0", j)).then_inc(dec_read, 1)
                            if kind == "icl":
                                act.wait_ge(job_full, n + 1)
                                nc.scalar.activation(af[:, j, :], bank[n % 8][:, :], ACT.Sigmoid,
                                                     bias=col("a0", j)).then_inc(icl_read, 1)
                            if (kind, j) == ("K", 3):
                                for q in range(NJ):
                                    act.wait_ge(dec_read, q + 1)
                                    nc.scalar.activation(wf[:, q, :], wf[:, q, :], ACT.Exp, scale=-DECAY)\
                                        .then_inc(w_done, 1)
                                for q in range(NJ):
                                    act.wait_ge(shifted, nth(("K", q)))
                                    nc.scalar.activation(sq[:, q, :], kf[:, q, :], ACT.Square,
                                                         scale=col("k_k", q)).then_inc(sq_done, 1)
                            if kind == "nrm":
                                act.wait_ge(nrm_read, j + 1)
                                nc.scalar.activation(sq[:, j, :], sq[:, j, :], ACT.Sqrt).then_inc(rt_done, 1)

                    @block.vector
                    def _(dve):
                        for b in range(0, 8, 2):
                            dve.wait_ge(xt_full, b + 1)
                            t, hf = divmod(b, 2)
                            nc.vector.tensor_copy(xT[:, 4 * hf:4 * hf + 4, t * P:(t + 1) * P],
                                                  bank[b][:, :].rearrange("p (k s) -> p k s", k=4))\
                                .then_inc(xt_dve, 1)
                        dve.wait_ge(cols_full, 1)
                        nc.vector.tensor_copy(cols[:, :], bank[0][:, 0:NROWS]).then_inc(cols_done, 1)
                        dve.wait_ge(cols_done, 1)
                        nc.vector.tensor_scalar(omm[:, :], cols[:, 0:14], -1.0, 1.0, ALU.mult, ALU.add)\
                            .then_inc(omm_done, 1)
                        dve.wait_ge(consts_done, 2)

                        def decay_products(j):
                            dve.wait_ge(w_done, j + 1)
                            if j > 0:
                                dve.wait_ge(scanned, j)
                            link(dve, nc.vector.tensor_copy(starts[:, 0:S:CH], wf[:, j, 0:S:CH]))
                            link(dve, nc.vector.memset(wf[:, j, 0:S:CH], 0.0))
                            nc.vector.tensor_tensor_scan(wf[:, j, :], wf[:, j, :], starts[:, :], 0.0,
                                                         ALU.mult, ALU.add).then_inc(scanned, 1)

                        def key_side(j):
                            dve.wait_ge(rt_done, j + 1)
                            dve.wait_ge(scanned, j + 1)
                            dve.wait_ge(icl_read, j + 1)
                            rn, kk, b, rw, am = sq[:, j, :], tmp[:, 0, :], tmp[:, 1, :], tmp[:, 2, :], tmp[:, 3, :]
                            nc.vector.reciprocal(rw, wf[:, j, :])
                            nc.vector.tensor_copy(wc[:, j, :], wf[:, j, CH - 1:S:CH])
                            link(dve, nc.vector.reciprocal(rn, rn))
                            nc.vector.tensor_scalar(am, af[:, j, :], -1.0, col("k_a", j), ALU.add, ALU.mult)
                            link(dve, nc.vector.scalar_tensor_tensor(kk, kf[:, j, :], col("k_k", j), rn,
                                                                     ALU.mult, ALU.mult))
                            kkc, wfc = (v.rearrange("p (c t) -> p c t", t=CH) for v in (kk, wf[:, j, :]))
                            at = ar[:, 0, j, :].rearrange("p (c t) -> p c t", t=CH)
                            nc.vector.scalar_tensor_tensor(at[:, :, 1:CH], kkc[:, :, 1:CH], -1.0,
                                                           wfc[:, :, 0:CH - 1], ALU.mult, ALU.mult)
                            nc.vector.tensor_scalar(at[:, :, 0:1], kkc[:, :, 0:1], -1.0, None, ALU.mult)
                            nc.vector.tensor_tensor(b, kk, af[:, j, :], ALU.mult)
                            link(dve, nc.vector.scalar_tensor_tensor(kf[:, j, :], am, 1.0, kf[:, j, :],
                                                                     ALU.add, ALU.mult))
                            nc.vector.tensor_tensor(bt[:, j, :], b, rw, ALU.mult)
                            link(dve, nc.vector.tensor_tensor(kt_[:, j, :], kf[:, j, :], rw, ALU.mult))

                        def receptance_side(j):
                            dve.wait_ge(shifted, nth(("R", j)))
                            nc.vector.tensor_tensor(ar[:, 1, j, :], rf[:, j, :], wf[:, j, :], ALU.mult)
                            nc.vector.scalar_tensor_tensor(rf[:, j, :], rf[:, j, :], col("r_k", j), kf[:, j, :],
                                                           ALU.mult, ALU.mult)

                        for n, (kind, j) in enumerate(jobs):
                            if kind in ("L", "K", "R", "V"):
                                m = nth((kind, j))
                                i = mu_col[kind] + j
                                d = shift_dest(kind, j)
                                dve.wait_ge(z_read, m)
                                nc.vector.scalar_tensor_tensor(d, zb[:, (m - 1) % 2, 0:S], cols[:, i:i + 1], d,
                                                               ALU.mult, ALU.add).then_inc(shifted, 1)
                            if (kind, j) == ("R", 0):
                                for q in range(NJ):
                                    decay_products(q)
                            if kind == "nrm":
                                dve.wait_ge(job_full, n + 1)
                                nc.vector.tensor_scalar(sq[:, j, :], bank[n % 8][:, :], 1e-24, None, ALU.max)\
                                    .then_inc(nrm_read, 1)
                            if kind == "R" and j > 0:
                                key_side(j - 1)
                            if (kind, j) == ("V", 0):
                                key_side(NJ - 1)
                            if kind == "V":
                                receptance_side(j)

            qT = sa("qT", [P, NJ, S])
            kT = sa("kT", [P, NJ, S])
            memtm = mixT[:, 0:NJ, :].rearrange("p a s -> p (a s)").rearrange("p (t d) -> p t d", t=MT)
            mem_here = part_sem("mem_here")
            A2 = ExitStack()
            with A2:
                def s2(name, shape, dt=F32):
                    return A2.enter_context(nc.sbuf_tensor(name, shape, dt))

                NG = (NC // 2) * 2
                tm = s2("tm", [P, 2, 2, 3, P])
                gg = s2("gg", [P, 2, 2, 2, 2, 2, CH])
                ntb = s2("ntb", [P, 2, 2, 2, CH])
                pw = s2("pw", [P, 2, 2, 4, CH])
                pd = s2("pd", [P, 2, 2, 4, 2, CH])
                ux = s2("ux", [P, 2, 4, 2, CH])
                rr = s2("rr", [P, 2, 2, CH])
                ft = s2("ft", [P, 2, 2, CH])
                hs = s2("hs", [P, 2, 2, CH])
                yi = s2("yi", [P, 2, 2, CH])
                st = s2("st", [P, NJ, 2, CH])

                tm_full, tm_read = part_sem("tm_full"), part_sem("tm_read")
                g_full, g_masked = part_sem("g_full"), part_sem("g_masked")
                nt_full, nt_masked = part_sem("nt_full"), part_sem("nt_masked")
                akv_full, akv_read = part_sem("akv_full"), part_sem("akv_read")
                sq_full, sq_act, sq_dve = part_sem("sq_full"), part_sem("sq_act"), part_sem("sq_dve")
                ax_full, ax_added = part_sem("ax_full"), part_sem("ax_added")
                re_full, re_read = part_sem("re_full"), part_sem("re_read")
                sy_full, st_done, y_done = part_sem("sy_full"), part_sem("st_done"), part_sem("y_done")
                st_zero = part_sem("st_zero")
                fill_full, fill_read = part_sem("fill_full"), part_sem("fill_read")
                half = [slice(0, 64), slice(64, 128)]

                fills = ([(GAV, t, av[:, t, :]) for t in range(AV_EARLY, NT)]
                         + [(GAQ, j, qT[:, j, :]) for j in range(NJ)] + [(GAK, j, kT[:, j, :]) for j in range(NJ)])
                STEPS = 4
                share = (0, 1, 0, 0, 0, 0, 0, 1, 1, 1, 1, 0)
                fill_at = [0]
                for place in range(NG * len(share)):
                    fill_at.append(min(STEPS * len(fills), fill_at[-1] + share[place % len(share)]))
                fill_at[-1] = STEPS * len(fills)

                def scalar_copy(dst, src):
                    return nc.scalar.activation(dst, src, ACT.Copy)

                def first_powers(copy, cp):
                    src = bank[cp][half[cp], :].rearrange("p (w u c) -> p w u c", w=2, u=4)
                    copy(pw[half[cp], 0, :, :, :], src)
                    return copy(pd[half[cp], 0, :, :, cp, :], src)

                def powers(copy, m, which):
                    src = bank[which][:, 0:4 * CH].rearrange("p (u c) -> p u c", u=4)
                    if m < 4 - which:
                        copy(pw[:, m % 2, which, :, :], src)
                    copy(pd[half[0], m % 2, which, :, 0, :], src[half[0]])
                    return copy(pd[half[1], m % 2, which, :, 1, :], src[half[1]])

                with nc.Block() as block:
                    @block.sync
                    def _(sp):
                        sp.dma_start(memtm, mem[0].rearrange("(t p) d -> p t d", p=P)).then_inc(mem_here, 16)
                        for i in range(3):
                            load_group(sp, GKV + i, (fill_full, 4 * (i + 1) - AV_EARLY))

                    @block.gpsimd
                    def _(pool):
                        pool.memset(pd[:, :, :, :, :, :], 0.0).then_inc(st_zero, 1)
                        pool.wait_ge(st_zero, 1)
                        pool.memset(st[:, :, 0, :], 0.0).then_inc(st_zero, 1)

                    @block.tensor
                    def _(pe):
                        def fill(n, place):
                            place += n * len(share)
                            for step in range(fill_at[place], fill_at[place + 1]):
                                f, part = divmod(step, STEPS)
                                g, i, _ = fills[f]
                                if part == 0:
                                    group_here(pe, g)
                                    if f >= 2:
                                        pe.wait_ge(fill_read, f - 1)
                                w = slot(g, 512)
                                for k in range(2 * part, 2 * part + 2):
                                    sl = slice(i * P, (i + 1) * P)
                                    lhs, rhs = (xT[:, k, sl], w[:, k, :]) if g == GAV else (w[:, k, sl], xT[:, k, :])
                                    last = nc.tensor.matmul(bank[6 + f % 2][:, :], lhs, rhs, start=(k == 0),
                                                            stop=(k == KT - 1))
                                if part == STEPS - 1:
                                    last.then_inc(fill_full, 1)

                        pe.wait_ge(st_zero, 2)
                        for n in range(NG):
                            cpair, quad = divmod(n, 2)
                            b = n % 2
                            units = [(p, hp) for p in range(2) for hp in range(2)]
                            ts = slice(cpair * P, (cpair + 1) * P)
                            fill(n, 0)
                            if n:
                                pe.wait_ge(y_done, 2 * n - 1)
                            for p in range(2):
                                j = 2 * quad + p
                                srcs = (ar[:, 0, j, ts], bt[:, j, ts], kt_[:, j, ts],
                                        vf[:, j, ts])
                                for i, src in enumerate(srcs):
                                    last = nc.tensor.transpose(bank[4 + p][:, i * P:(i + 1) * P], src, ident[:, :])
                                last.then_inc(tm_full, 1)
                            if n:
                                pe.wait_ge(re_read, 2 * n)
                            for p in range(2):
                                for cp in range(2):
                                    c = 2 * cpair + cp
                                    cs = slice(c * CH, (c + 1) * CH)
                                    for i, left in enumerate((bt, kt_)):
                                        for hp in range(2):
                                            j = 2 * quad + p
                                            o = (2 * p + i) * 2 * CH
                                            ins = nc.tensor.matmul(bank[hp][half[cp], o:o + 2 * CH],
                                                                   left[half[hp], j, cs], ar[half[hp], :, j, cs],
                                                                   start=True, stop=True)
                                            if (p, cp, i) == (1, 1, 1):
                                                ins.then_inc(g_full, 1)
                            if n:
                                pe.wait_ge(y_done, 2 * n)
                            for p in range(2):
                                for cp in range(2):
                                    c = 2 * cpair + cp
                                    cs = slice(c * CH, (c + 1) * CH)
                                    for hp in range(2):
                                        j = 2 * quad + p
                                        ins = nc.tensor.matmul(bank[2 + hp][half[cp], p * CH:(p + 1) * CH],
                                                               ar[half[hp], 0, j, cs], bt[half[hp], j, cs],
                                                               start=True, stop=True)
                                        if (p, cp) == (1, 1):
                                            ins.then_inc(nt_full, 1)
                            fill(n, 1)
                            pe.wait_ge(tm_read, 2 * n + 2)
                            pe.wait_ge(g_masked, 2 * n + 2)
                            for u, (p, hp) in enumerate(units):
                                for cp in range(2):
                                    ins = nc.tensor.matmul(bank[4 + cp][half[cp], u * CH:(u + 1) * CH],
                                                           gg[half[cp], b, hp, p, 1, 0, :],
                                                           tm[half[cp], b, p, 2, hp * CH:(hp + 1) * CH],
                                                           start=True, stop=True)
                                    if u == 3:
                                        ins.then_inc(akv_full, 1)
                            fill(n, 2)
                            pe.wait_ge(nt_masked, 2 * n + 2)
                            for which in range(2):
                                for u, (p, hp) in enumerate(units):
                                    for cp in range(2):
                                        at, a = gg[half[cp], b, hp, p, 0, 0, :], ntb[half[cp], b, hp, p, :]
                                        o = (4 * which + u) * CH
                                        ins = nc.tensor.matmul(bank[cp][half[cp], o:o + CH], (a, at)[which],
                                                               (at, a)[which], start=True, stop=True)
                                        if (which, u) == (1, 3):
                                            ins.then_inc(sq_full, 1)
                            pe.wait_ge(akv_read, 2 * n + 2)
                            for u, (p, hp) in enumerate(units):
                                for cp in range(2):
                                    ins = nc.tensor.matmul(bank[2 + cp][half[cp], 2 * u * CH:2 * (u + 1) * CH],
                                                           gg[half[cp], b, hp, p, 0, 0, :],
                                                           ux[half[cp], b, u, :, :], start=True, stop=True)
                                    if u == 3:
                                        ins.then_inc(ax_full, 1)
                            for m in range(1, 6):
                                fill(n, 2 + m)
                                q = (m - 1) % 2
                                pe.wait_ge(sq_act, 5 * n + m)
                                if m < 5:
                                    pe.wait_ge(sq_dve, 4 * n + m)
                                    for which in ((0, 1) if m < 4 else (0,)):
                                        for u in range(4):
                                            last = nc.tensor.matmul(bank[which][:, u * CH:(u + 1) * CH],
                                                                    pd[:, q, 1 - which, u, :, :]
                                                                    .rearrange("p c t -> p (c t)"),
                                                                    pw[:, q, which, u, :], start=True, stop=True)
                                        last.then_inc(sq_full, 1)
                                pe.wait_ge(ax_added, 7 * n + (2 if m == 1 else m + 1))
                                for u in range(4):
                                    last = nc.tensor.matmul(bank[2][:, 2 * u * CH:2 * (u + 1) * CH],
                                                            pd[:, q, 0, u, :, :].rearrange("p c t -> p (c t)"),
                                                            ux[:, b, u, :, :].rearrange("p w c -> p (w c)"),
                                                            start=True, stop=True)
                                last.then_inc(ax_full, 1)
                            fill(n, 8)
                            pe.wait_ge(ax_added, 7 * n + 7)
                            for u, (p, hp) in enumerate(units):
                                hs_ = slice(hp * CH, (hp + 1) * CH)
                                for kind in range(4):
                                    for cp in range(2):
                                        r, o = half[cp], (4 * p + kind) * CH
                                        dst = bank[cp][half[hp], o:o + CH]
                                        M, U = ux[r, b, u, 0, :], ux[r, b, u, 1, :]
                                        bm, km, vm = (tm[r, b, p, i, hs_] for i in range(3))
                                        br, kr = gg[r, b, hp, p, 0, 1, :], gg[r, b, hp, p, 1, 1, :]
                                        terms = (((M, br),), ((M, bm),), ((bm, U), (km, vm)), ((U, br), (vm, kr)))[kind]
                                        for i, (lhs, rhs) in enumerate(terms):
                                            ins = nc.tensor.matmul(dst, lhs, rhs, start=(i == 0),
                                                                   stop=(i == len(terms) - 1))
                                        if u == 3 and kind == 3:
                                            ins.then_inc(re_full, 1)
                            for cp in range(2):
                                c = 2 * cpair + cp
                                fill(n, 9 + cp)
                                pe.wait_ge(re_read, 2 * n + cp + 1)
                                pe.wait_ge(st_done, 2 * n + cp) if 2 * n + cp else None
                                base = 4 if cp == 0 else 2
                                for p in range(2):
                                    for hp in range(2):
                                        j = 2 * quad + p
                                        s_in = st[half[hp], j, c % 2, :]
                                        nc.tensor.matmul(bank[base + hp][half[hp], p * CH:(p + 1) * CH],
                                                         ft[half[hp], cp, p, :], s_in, start=True, stop=True)
                                for p in range(2):
                                    for hp in range(2):
                                        j = 2 * quad + p
                                        s_in = st[half[hp], j, c % 2, :]
                                        ins = nc.tensor.matmul(bank[base + hp][half[hp], (2 + p) * CH:(3 + p) * CH],
                                                               s_in, rr[half[hp], cp, p, :], start=True, stop=True)
                                ins.then_inc(sy_full, 1)
                            fill(n, 11)

                    @block.scalar
                    def _(act):
                        done = [0]

                        def fill(n, place):
                            place += n * len(share)
                            while done[0] < fill_at[place + 1] // STEPS:
                                f = done[0]
                                act.wait_ge(fill_full, f + 1)
                                nc.scalar.activation(fills[f][2], bank[6 + f % 2][:, :], ACT.Copy)\
                                    .then_inc(fill_read, 1)
                                done[0] += 1

                        for n in range(NG):
                            b = n % 2
                            for p in range(2):
                                act.wait_ge(tm_full, 2 * n + p + 1)
                                if n >= 2 and p == 0:
                                    act.wait_ge(sy_full, 2 * n - 2)
                                nc.scalar.activation(ux[:, b, 2 * p:2 * p + 2, 0, :],
                                                     bank[4 + p][:, 0:P].rearrange("p (h c) -> p h c", h=2), ACT.Copy)
                                nc.scalar.activation(tm[:, b, p, :, :],
                                                     bank[4 + p][:, P:4 * P].rearrange("p (k c) -> p k c", k=3),
                                                     ACT.Copy).then_inc(tm_read, 1)
                            fill(n, 1)
                            act.wait_ge(sq_full, 9 * n + 1)
                            first_powers(scalar_copy, 0).then_inc(sq_act, 1)
                            for m in range(1, 5):
                                act.wait_ge(sq_full, 9 * n + 2 * m + 1)
                                powers(scalar_copy, m, 0).then_inc(sq_act, 1)
                            fill(n, 7)
                            fill(n, 11)

                    @block.vector
                    def _(dve):
                        for n in range(NG):
                            cpair, quad = divmod(n, 2)
                            b = n % 2
                            if n >= 2:
                                dve.wait_ge(sy_full, 2 * n - 2)
                            for hp in range(2):
                                dve.wait_ge(g_full, 2 * n + hp + 1)
                                nc.vector.tensor_tensor(gg[:, b, hp, :, :, :, :].rearrange("p a b c t -> p (a b c t)"),
                                                        bank[hp][:, :],
                                                        mask[:, :, :, :, :].rearrange("p a b c t -> p (a b c t)"),
                                                        ALU.mult).then_inc(g_masked, 1)
                            for hp in range(2):
                                dve.wait_ge(nt_full, 2 * n + hp + 1)
                                nc.vector.tensor_tensor(ntb[:, b, hp, :, :], bank[2 + hp][:, 0:2 * CH]
                                                        .rearrange("p (a t) -> p a t", a=2), maskT[:, 0:2, :],
                                                        ALU.mult).then_inc(nt_masked, 1)
                            for cp in range(2):
                                dve.wait_ge(akv_full, 2 * n + cp + 1)
                                nc.vector.tensor_copy(ux[half[cp], b, :, 1, :],
                                                      bank[4 + cp][half[cp], 0:4 * CH]
                                                      .rearrange("p (u c) -> p u c", u=4)).then_inc(akv_read, 1)
                            dve.wait_ge(sq_full, 9 * n + 2)
                            first_powers(nc.vector.tensor_copy, 1).then_inc(sq_dve, 1)
                            for cp in range(2):
                                dve.wait_ge(ax_full, 7 * n + cp + 1)
                                v = ux[half[cp], b, :, :, :].rearrange("p u w c -> p (u w c)")
                                nc.vector.tensor_tensor(v, bank[2 + cp][half[cp], :], v, ALU.add)\
                                    .then_inc(ax_added, 1)
                            for m in range(1, 6):
                                if m < 4:
                                    dve.wait_ge(sq_full, 9 * n + 2 * m + 2)
                                    powers(nc.vector.tensor_copy, m, 1).then_inc(sq_dve, 1)
                                dve.wait_ge(ax_full, 7 * n + m + 2)
                                v = ux[:, b, :, :, :].rearrange("p u w c -> p (u w c)")
                                nc.vector.tensor_tensor(v, bank[2][:, :], v, ALU.add).then_inc(ax_added, 1)
                            js = slice(2 * quad, 2 * quad + 2)
                            for cp in range(2):
                                c = 2 * cpair + cp
                                dve.wait_ge(re_full, 2 * n + cp + 1)
                                if n:
                                    dve.wait_ge(sy_full, 2 * n)
                                    dve.wait_ge(st_done, 2 * n)
                                    dve.wait_ge(y_done, 2 * n)
                                src = bank[cp][:, :].rearrange("p (a k t) -> p a k t", a=2, k=4)
                                nc.vector.tensor_tensor(rr[:, cp, :, :], src[:, :, 0, :], ar[:, 1, js, c * CH:(c + 1) * CH],
                                                        ALU.add)
                                nc.vector.tensor_tensor(ft[:, cp, :, :], src[:, :, 1, :],
                                                        id64[:, :].unsqueeze(1).to_broadcast([P, 2, CH]), ALU.add)
                                nc.vector.tensor_tensor(hs[:, cp, :, :], src[:, :, 2, :],
                                                        wc[:, js, c:c + 1].to_broadcast([P, 2, CH]), ALU.mult)
                                nc.vector.tensor_copy(yi[:, cp, :, :], src[:, :, 3, :]).then_inc(re_read, 1)
                            for cp in range(2):
                                c = 2 * cpair + cp
                                base = 4 if cp == 0 else 2
                                dve.wait_ge(sy_full, 2 * n + cp + 1)
                                dve.wait_ge(re_read, 2 * n + cp + 1)
                                for p in range(2):
                                    for hp in range(2):
                                        j = 2 * quad + p
                                        ins = nc.vector.scalar_tensor_tensor(
                                            st[half[hp], j, (c + 1) % 2, :],
                                            bank[base + hp][half[hp], p * CH:(p + 1) * CH], wc[half[hp], j, c:c + 1],
                                            hs[half[hp], cp, p, :], ALU.mult, ALU.add)
                                ins.then_inc(st_done, 1)
                                for hp in range(2):
                                    ins = nc.vector.tensor_tensor(
                                        bt[half[hp], js, c * CH:(c + 1) * CH],
                                        bank[base + hp][half[hp], 2 * CH:4 * CH].rearrange("p (a t) -> p a t", a=2),
                                        yi[half[hp], cp, :, :], ALU.add)
                                ins.then_inc(y_done, 1)

            A3 = ExitStack()
            with A3:
                def s3(name, shape, dt=F32):
                    return A3.enter_context(nc.sbuf_tensor(name, shape, dt))

                dist = s3("dist", [P, 512])
                ysq = s3("ysq", [P, 2, S])
                sc = s3("sc", [P, 3, S])
                pr = s3("pr", [P, 3, S])
                prT = s3("prT", [P, 3, S])
                mx = s3("mx", [P, H, NT])
                nmx = s3("nmx", [P, H, NT])
                rs = s3("rs", [P, H, NT])
                ri = s3("ri", [P, H, NT])
                oa = s3("oa", [P, NT, H, HD])
                osq = s3("osq", [P, NT, H, HD])
                oss = s3("oss", [P, NT, H])
                v8 = s3("v8", [H, S])
                to_heads = s3("to_heads", [P, NJ, H])
                from_heads = s3("from_heads", [H, NJ, P])
                memT = mixT[:, NJ:2 * NJ, :].rearrange("p a s -> p (a s)").rearrange("p (k s) -> p k s", k=KT)

                dist_done = part_sem("dist_done")
                mt_full, mt_read = part_sem("mt_full"), part_sem("mt_read")
                mu_full, yc_done, ysq_done = part_sem("mu_full"), part_sem("yc_done"), part_sem("ysq_done")
                var_full, var_read, rstd_root = part_sem("var_full"), part_sem("var_read"), part_sem("rstd_root")
                heads_done, rstd_done, rb_full = part_sem("heads_done"), part_sem("rstd_done"), part_sem("rb_full")
                yn_done, ya_done = part_sem("yn_done"), part_sem("ya_done")
                bon_full, gate_full = part_sem("bon_full"), part_sem("gate_full")
                bon_read, gate_read = part_sem("bon_read"), part_sem("gate_read")
                mfill_full, mfill_read = part_sem("mfill_full"), part_sem("mfill_read")
                s_full, s_read = part_sem("s_full"), part_sem("s_read")
                s_max, p_done, p_norm = part_sem("s_max"), part_sem("p_done"), part_sem("p_norm")
                pt_full, pt_read = part_sem("pt_full"), part_sem("pt_read")
                o_full, o_read = part_sem("o_full"), part_sem("o_read")
                osq_done, oms_done = part_sem("osq_done"), part_sem("oms_done")
                ort_done, on_done = part_sem("ort_done"), part_sem("on_done")
                ot_full, ot_read = part_sem("ot_full"), part_sem("ot_read")

                mfills = [("k", i) for i in range(KT // 2)] + [("v", i) for i in range(2 * MT)]
                mplaces = (0, 4, 1, 1, 1, 1) + (0, 1, 1, 1) * 8 + (0, 0, 0)
                MSTEPS = 4
                mfill_at = [0]
                for steps_ in mplaces:
                    mfill_at.append(mfill_at[-1] + steps_)
                qunits = [(h, q) for h in range(H) for q in range(NT)]
                LAG = 2

                def mfill_dest(f):
                    kind, i = mfills[f]
                    if kind == "k":
                        return kmT[:, 2 * i:2 * i + 2, :].rearrange("p a m -> p (a m)")
                    return vm[:, i % MT, (i // MT) * 512:(i // MT + 1) * 512]

                with nc.Block() as block:
                    @block.sync
                    def _(sp):
                        load_group(sp, GKV + 3, (mfill_full, 2))
                        load_group(sp, GO, (mfill_full, 4))
                        load_group(sp, GO + 1, (mfill_full, 6))
                        load_group(sp, GQ, (mfill_full, 8))

                    @block.gpsimd
                    def _(pool):
                        link(pool, pool.memset(to_heads[:, :, :], 0.0))
                        for h in range(H):
                            link(pool, pool.memset(to_heads[half[h % 2], h // 2, h:h + 1], 1.0))
                        ch = from_heads[:, :, :].rearrange("h j p -> h (j p)")
                        link(pool, pool.memset(ch, 1.0))
                        link(pool, pool.affine_select(out=ch, in_=ch, compare_op=ALU.is_ge, fill=0.0, base=0,
                                                      pattern=[[1, S]], channel_multiplier=-HD))
                        pool.affine_select(out=ch, in_=ch, compare_op=ALU.is_ge, fill=0.0, base=HD - 1,
                                           pattern=[[-1, S]], channel_multiplier=HD).then_inc(heads_done, 1)
                        pool.wait_ge(heads_done, 1)
                        link(pool, pool.iota(dist[:, :], pattern=[[1, 512]], base=-384, channel_multiplier=-1,
                                             allow_small_or_imprecise_dtypes=True))
                        pool.affine_select(out=dist[:, :], in_=dist[:, :], compare_op=ALU.is_ge, fill=NEG,
                                           base=384, pattern=[[-1, 512]], channel_multiplier=1)\
                            .then_inc(dist_done, 1)

                    @block.tensor
                    def _(pe):
                        def mfill(place):
                            for step in range(mfill_at[place], mfill_at[place + 1]):
                                f, part = divmod(step, MSTEPS)
                                kind, i = mfills[f]
                                dst = bank[6]
                                if part == 0 and f:
                                    pe.wait_ge(mfill_read, f)
                                if kind == "k":
                                    a, k0 = divmod(part, 2)
                                    g, ks = GKV + i // 2, range(4 * k0, 4 * k0 + 4)
                                    ct = (2 * i + a) % 4
                                else:
                                    g, ks = GKV + 2 + i // MT, range(2 * part, 2 * part + 2)
                                    t = i % MT
                                if part == 0:
                                    group_here(pe, g)
                                w = slot(g, 512)
                                for k in ks:
                                    if kind == "k":
                                        last = nc.tensor.matmul(dst[:, a * MEM:(a + 1) * MEM],
                                                                w[:, k, ct * P:(ct + 1) * P], memT[:, k, :],
                                                                start=(k == 0), stop=(k == KT - 1))
                                    else:
                                        last = nc.tensor.matmul(dst[:, :], memT[:, k, t * P:(t + 1) * P], w[:, k, :],
                                                                start=(k == 0), stop=(k == KT - 1))
                                if part == MSTEPS - 1:
                                    last.then_inc(mfill_full, 1)

                        for j in range(NJ):
                            nc.tensor.matmul(bank[j][:, :], blkones[:, :], bt[:, j, :], start=True, stop=True)\
                                .then_inc(mu_full, 1)
                        pe.wait_ge(mem_here, 16)
                        for b in range(4):
                            t, hf = divmod(b, 2)
                            for k in range(4):
                                c = 4 * hf + k
                                last = nc.tensor.transpose(bank[4 + b][:, k * P:(k + 1) * P],
                                                           memtm[:, t, c:D:KT], ident[:, :])
                            last.then_inc(mt_full, 1)
                        pe.wait_ge(mt_read, 4)
                        mfill(0)
                        pe.wait_ge(heads_done, 1)
                        for j in range(NJ):
                            pe.wait_ge(ysq_done, j + 1)
                            nc.tensor.matmul(bank[0][0:H, :], to_heads[:, j, :], ysq[:, j % 2, :], start=(j == 0),
                                             stop=(j == NJ - 1)).then_inc(var_full, 1)
                        mfill(1)
                        pe.wait_ge(rstd_done, 1)
                        for j in range(NJ):
                            nc.tensor.matmul(bank[j][:, :], from_heads[:, j, :], v8[:, :], start=True, stop=True)\
                                .then_inc(rb_full, 1)
                        for j in range(NJ):
                            if j:
                                pe.wait_ge(bon_read, j)
                                pe.wait_ge(gate_read, j)
                            nc.tensor.matmul(bank[4][:, :], blkones[:, :], rf[:, j, :], start=True, stop=True)\
                                .then_inc(bon_full, 1)
                            nc.tensor.matmul(bank[5][:, :], wg[:, j * P:(j + 1) * P], sgz[:, :], start=True, stop=True)\
                                .then_inc(gate_full, 1)
                            mfill(2 + j)

                        def scores(n):
                            h, q = qunits[n]
                            j, r = h // 2, slice((h % 2) * HD, (h % 2) * HD + HD)
                            if n < 3:
                                pe.wait_ge(yn_done, n + 1)
                            else:
                                pe.wait_ge(s_read, n - 2)
                            nk = (q + 1) * P
                            nc.tensor.matmul(bank[n % 3][:, 0:nk], qT[r, j, q * P:(q + 1) * P], kT[r, j, 0:nk],
                                             start=True, stop=True).then_inc(s_full, 1)

                        def values(n):
                            h, q = qunits[n]
                            j = h // 2
                            pe.wait_ge(p_norm, n + 1)
                            b = 3 + n % 2
                            if n < 2:
                                pe.wait_ge(yn_done, NJ) if n == 0 else pe.wait_ge(bon_read, NJ)
                            else:
                                pe.wait_ge(pt_read, n - 1)
                            for k in range(q + 1):
                                last = nc.tensor.transpose(bank[b][:, k * P:(k + 1) * P],
                                                           pr[:, n % 3, k * P:(k + 1) * P], ident[:, :])
                            last.then_inc(pt_full, 1)

                        def product(n):
                            h, q = qunits[n]
                            j = h // 2
                            pe.wait_ge(pt_read, n + 1)
                            if q == 0:
                                if h >= 2:
                                    pe.wait_ge(o_read, h - 1)
                                else:
                                    pe.wait_ge(gate_read, NJ)
                            o = q * HD
                            for k in range(q + 1):
                                last = nc.tensor.matmul(bank[5 + 2 * (h % 2)][:, o:o + HD], prT[:, n % 3, k * P:(k + 1) * P],
                                                        av[:, k, h * HD:(h + 1) * HD], start=(k == 0), stop=(k == q))
                            last.then_inc(o_full, 1)

                        pe.wait_ge(dist_done, 1)
                        for n in range(len(qunits) + LAG + 1):
                            if n < len(qunits):
                                scores(n)
                            if LAG <= n < len(qunits) + LAG:
                                values(n - LAG)
                            if n > LAG:
                                product(n - LAG - 1)
                            mfill(6 + n)
                        for j in range(NJ):
                            pe.wait_ge(on_done, 1 if j < NJ - 1 else 2)
                            for t in range(NT):
                                last = nc.tensor.transpose(bank[j][:, t * P:(t + 1) * P],
                                                           oa[:, t, 2 * j:2 * j + 2, :].rearrange("p h d -> p (h d)"),
                                                           ident[:, :])
                            last.then_inc(ot_full, 1)

                    @block.scalar
                    def _(act):
                        mfills_read = [0]

                        def mfill(place):
                            while mfills_read[0] < mfill_at[place + 1] // MSTEPS:
                                f = mfills_read[0]
                                act.wait_ge(mfill_full, f + 1)
                                nc.scalar.activation(mfill_dest(f), bank[6][:, :], ACT.Copy)\
                                    .then_inc(mfill_read, 1)
                                mfills_read[0] += 1

                        for b in range(4):
                            t, hf = divmod(b, 2)
                            act.wait_ge(mt_full, b + 1)
                            nc.scalar.activation(memT[:, 4 * hf:4 * hf + 4, t * P:(t + 1) * P],
                                                 bank[4 + b][:, :].rearrange("p (k s) -> p k s", k=4),
                                                 ACT.Copy).then_inc(mt_read, 1)
                        for j in range(NJ):
                            act.wait_ge(yc_done, j + 1)
                            if j >= 2:
                                act.wait_ge(var_full, j - 1)
                            nc.scalar.activation(ysq[:, j % 2, :], bt[:, j, :], ACT.Square).then_inc(ysq_done, 1)
                        mfill(0)
                        act.wait_ge(var_read, 1)
                        nc.scalar.activation(v8[:, :], v8[:, :], ACT.Sqrt).then_inc(rstd_root, 1)
                        for j in range(NJ):
                            act.wait_ge(yn_done, j + 1)
                            nc.scalar.activation(bt[:, j, :], bt[:, j, :], ACT.Identity, bias=col("lnx_b", j),
                                                 scale=col("lnx_g", j)).then_inc(ya_done, 1)
                        for place in range(1, 6):
                            mfill(place)

                        def exps(n):
                            h, q = qunits[n]
                            nk = (q + 1) * P
                            act.wait_ge(s_max, n + 1)
                            if n >= 3:
                                act.wait_ge(pt_full, n - 2)
                            nc.scalar.activation(pr[:, n % 3, 0:nk], sc[:, n % 3, 0:nk], ACT.Exp,
                                                 bias=nmx[:, h, q:q + 1], scale=HD ** -0.5,
                                                 accum_out=rs[:, h, q:q + 1]).then_inc(p_done, 1)

                        def squares(j):
                            act.wait_ge(o_read, 2 * j + 2)
                            nc.scalar.activation(osq[:, :, 2 * j:2 * j + 2, :], oa[:, :, 2 * j:2 * j + 2, :],
                                                 ACT.Square).then_inc(osq_done, 1)

                        def transposed(n):
                            h, q = qunits[n]
                            nk = (q + 1) * P
                            act.wait_ge(pt_full, n + 1)
                            if n >= 3:
                                act.wait_ge(o_full, n - 2)
                            nc.scalar.activation(prT[:, n % 3, 0:nk], bank[3 + n % 2][:, 0:nk], ACT.Copy)\
                                .then_inc(pt_read, 1)

                        for n in range(len(qunits) + LAG):
                            if n < len(qunits):
                                exps(n)
                            if n >= LAG:
                                transposed(n - LAG)
                            if n >= 3 * NT and n % (2 * NT) == NT and n < len(qunits):
                                squares(n // (2 * NT) - 1)
                            mfill(6 + n)
                        mfill(6 + len(qunits) + LAG)
                        act.wait_ge(oms_done, NJ - 1)
                        nc.scalar.activation(oss[:, :, 0:H - 2], oss[:, :, 0:H - 2], ACT.Sqrt).then_inc(ort_done, 1)
                        squares(NJ - 1)
                        act.wait_ge(oms_done, NJ)
                        nc.scalar.activation(oss[:, :, H - 2:H], oss[:, :, H - 2:H], ACT.Sqrt).then_inc(ort_done, 1)
                        for j in range(NJ):
                            act.wait_ge(ot_full, j + 1)
                            nc.scalar.activation(mixT[:, j, :], bank[j][:, :], ACT.Copy,
                                                 scale=col("attn_out_g", j)).then_inc(ot_read, 1)

                    @block.vector
                    def _(dve):
                        for j in range(NJ):
                            dve.wait_ge(mu_full, j + 1)
                            nc.vector.scalar_tensor_tensor(bt[:, j, :], bank[j][:, :], -1.0 / HD, bt[:, j, :],
                                                           ALU.mult, ALU.add).then_inc(yc_done, 1)
                        dve.wait_ge(var_full, NJ)
                        nc.vector.tensor_scalar(v8[:, :], bank[0][0:H, :], 1.0 / HD, GN_EPS, ALU.mult, ALU.add)\
                            .then_inc(var_read, 1)
                        dve.wait_ge(rstd_root, 1)
                        nc.vector.reciprocal(v8[:, :], v8[:, :]).then_inc(rstd_done, 1)
                        for j in range(NJ):
                            dve.wait_ge(rb_full, j + 1)
                            nc.vector.tensor_tensor(bt[:, j, :], bank[j][:, :], bt[:, j, :], ALU.mult)\
                                .then_inc(yn_done, 1)
                        for j in range(NJ):
                            dve.wait_ge(bon_full, j + 1)
                            nc.vector.tensor_tensor(vf[:, j, :], bank[4][:, :], vf[:, j, :], ALU.mult)\
                                .then_inc(bon_read, 1)
                            dve.wait_ge(bon_read, j + 1)
                            dve.wait_ge(ya_done, j + 1)
                            link(dve, nc.vector.tensor_tensor(vf[:, j, :], vf[:, j, :], bt[:, j, :], ALU.add))
                            dve.wait_ge(gate_full, j + 1)
                            nc.vector.tensor_tensor(rf[:, j, :], bank[5][:, :], vf[:, j, :], ALU.mult)\
                                .then_inc(gate_read, 1)
                        dve.wait_ge(dist_done, 1)

                        def biased(n):
                            h, q = qunits[n]
                            nk = (q + 1) * P
                            slope = 2.0 ** (-8.0 * (h + 1) / H)
                            dve.wait_ge(s_full, n + 1)
                            if n >= 3:
                                dve.wait_ge(p_done, n - 2)
                            nc.vector.scalar_tensor_tensor(sc[:, n % 3, 0:nk], dist[:, 384 - q * P:512],
                                                           slope * HD ** 0.5, bank[n % 3][:, 0:nk],
                                                           ALU.mult, ALU.add).then_inc(s_read, 1)
                            dve.wait_ge(s_read, n + 1)
                            link(dve, nc.vector.tensor_reduce(mx[:, h, q:q + 1], sc[:, n % 3, 0:nk], AX_X, ALU.max))
                            nc.vector.tensor_scalar(nmx[:, h, q:q + 1], mx[:, h, q:q + 1], -HD ** -0.5, None,
                                                    ALU.mult).then_inc(s_max, 1)

                        def normalised(n):
                            h, q = qunits[n]
                            nk = (q + 1) * P
                            dve.wait_ge(p_done, n + 1)
                            link(dve, nc.vector.reciprocal(ri[:, h, q:q + 1], rs[:, h, q:q + 1]))
                            nc.vector.tensor_scalar(pr[:, n % 3, 0:nk], pr[:, n % 3, 0:nk], ri[:, h, q:q + 1], None,
                                                    ALU.mult).then_inc(p_norm, 1)

                        def head_out(h):
                            dve.wait_ge(o_full, NT * (h + 1))
                            nc.vector.tensor_copy(oa[:, :, h, :], bank[5 + 2 * (h % 2)][:, 0:NT * HD]
                                                  .rearrange("p (t c) -> p t c", t=NT)).then_inc(o_read, 1)

                        def mean_squares(j):
                            hs_ = slice(2 * j, 2 * j + 2)
                            dve.wait_ge(osq_done, j + 1)
                            link(dve, nc.vector.tensor_reduce(oss[:, :, hs_], osq[:, :, hs_, :], AX_X, ALU.add))
                            nc.vector.tensor_scalar(oss[:, :, hs_], oss[:, :, hs_], 1.0 / HD, RMS_EPS, ALU.mult,
                                                    ALU.add).then_inc(oms_done, 1)

                        def scaled_heads(hs_, roots):
                            n_heads = hs_.stop - hs_.start
                            dve.wait_ge(ort_done, roots)
                            link(dve, nc.vector.reciprocal(oss[:, :, hs_], oss[:, :, hs_]))
                            nc.vector.tensor_tensor(oa[:, :, hs_, :], oa[:, :, hs_, :], oss[:, :, hs_].unsqueeze(3)
                                                    .to_broadcast([P, NT, n_heads, HD]), ALU.mult).then_inc(on_done, 1)

                        for n in range(len(qunits)):
                            biased(n)
                            if n >= 1:
                                normalised(n - 1)
                            if n % NT == NT - 1 and n > NT:
                                head_out(n // NT - 1)
                            if n >= 3 * NT and n % (2 * NT) == NT + 1:
                                mean_squares(n // (2 * NT) - 1)
                        normalised(len(qunits) - 1)
                        head_out(H - 1)
                        scaled_heads(slice(0, H - 2), 1)
                        mean_squares(NJ - 1)
                        scaled_heads(slice(H - 2, H), 2)
                        for j in range(NJ):
                            nc.vector.tensor_copy(mixT[:, NJ + j, :], rf[:, j, :])

        nc.clear_and_free_semaphores(part_sems)
        nc.all_engine_barrier()

        x1 = sb("x1", [P, NT, D])
        ln_gb = sb("ln_gb", [P, 2, D])
        ring2 = sb("ring2", [P, 3 * SLOT])
        stats = sb("stats", [P, NT, 2, 6])
        mv = sb("mv", [P, NT, 2])
        rstd = sb("rstd", [P, NT])
        counts = sb("counts", [P, NE])
        most_f = sb("most_f", [P, 1])
        thresholds = sb("thresholds", [P, S // CAP - 1])
        blk_f = sb("blk_f", [P, S // CAP - 1])
        more_i = sb("more_i", [P, 1], I32)
        gate_here = [sem(f"gate_here{i}") for i in range(3)]
        up_in = [sem(f"up_in{i}") for i in range(3)]
        down_here = [sem(f"down_here{i}") for i in range(3)]

        def expert_slot(s, i):
            if s == 2:
                return (ar[:, :, :, :].rearrange("p a j s -> p (a j s)"), xT[:, :, :].rearrange("p k s -> p (k s)"),
                        mixT[:, :, :].rearrange("p j s -> p (j s)"))[i]
            return (ring2, ring)[s][:, i * SLOT:(i + 1) * SLOT]

        expert_w = (w_exp_gate[0].rearrange("e (p k) n -> e p (k n)", k=KT),
                    w_exp_up[0].rearrange("e (p k) n -> e p (k n)", k=KT),
                    w_exp_down[0].rearrange("e (p k) n -> e p (k n)", k=FT))
        expert_sem = (gate_here, up_in, down_here)

        def load_expert(eng, e, s, i):
            eng.dma_start(expert_slot(s, i), expert_w[i][e]).then_inc(expert_sem[i][s], 16)

        class Norm:

            def __init__(self, i):
                self.i = i
                self.here, self.added, self.var_done, self.rooted, self.centred, self.shifted = (
                    sem(f"ln{i}_{n}") for n in ("here", "added", "var_done", "rooted", "centred", "shifted"))

            def load(self, eng):
                for h, src in enumerate((ln_g, ln_b)):
                    eng.dma_start(ln_gb[:, h, :], src[0, self.i:self.i + 1, :].to_broadcast([P, D]))\
                        .then_inc(self.here, 16)

            def statistics(self, dve, t):
                dve.wait_ge(self.added, 2 * t + 2)
                for hf in range(2):
                    ins = nc.vector.bn_stats(stats[:, t, hf, :], x1[:, t, hf * 512:(hf + 1) * 512])
                link(dve, ins)
                link(dve, nc.vector.bn_aggr(mv[:, t, :], stats[:, t, :, :].rearrange("p a b -> p (a b)")))
                nc.vector.tensor_scalar(rstd[:, t:t + 1], mv[:, t, 1:2], LN_EPS, None, ALU.add)\
                    .then_inc(self.var_done, 1)
                if t == 0:
                    dve.wait_ge(self.here, 32)
                nc.vector.scalar_tensor_tensor(x1[:, t, :], x1[:, t, :], mv[:, t, 0:1], ln_gb[:, 0, :],
                                               ALU.subtract, ALU.mult).then_inc(self.centred, 1)

            def root(self, act, t):
                act.wait_ge(self.var_done, t + 1)
                nc.scalar.activation(rstd[:, t:t + 1], rstd[:, t:t + 1], ACT.Sqrt).then_inc(self.rooted, 1)

            def scale(self, dve, t):
                dve.wait_ge(self.rooted, t + 1)
                link(dve, nc.vector.reciprocal(rstd[:, t:t + 1], rstd[:, t:t + 1]))
                dve.wait_ge(self.centred, t + 1)
                nc.vector.scalar_tensor_tensor(x1[:, t, :], x1[:, t, :], rstd[:, t:t + 1], ln_gb[:, 1, :],
                                               ALU.mult, ALU.add).then_inc(self.shifted, 1)

        B = ExitStack()
        with B:
            def sB(name, shape, dt=F32):
                return B.enter_context(nc.sbuf_tensor(name, shape, dt))

            x1T, qmT = xT, mixT
            n1 = Norm(0)
            x_back = sem("x_back")
            wo_full = sem("wo_full")
            t1_full, t1_act, t1_dve = sem("t1_full"), sem("t1_act"), sem("t1_dve")
            qm_full, qm_read = sem("qm_full"), sem("qm_read")
            q_order = [6, 7, 0, 1, 2, 3, 4, 5]

            with nc.Block() as block:
                @block.sync
                def _(sp):
                    for t in range(NT):
                        sp.dma_start(x1[:, t, :], x[0, t * P:(t + 1) * P, :]).then_inc(x_back, 16)
                    n1.load(sp)
                    for i in range(3):
                        load_expert(sp, 0, 0, i)
                    load_group(sp, GQ + 1, (wo_full, 8))
                    load_group(sp, GMO, (wo_full, 8))
                    load_group(sp, GMO + 1, (qm_full, 6))

                @block.tensor
                def _(pe):
                    def tokens(t):
                        pe.wait_ge(n1.shifted, t + 1)
                        for hf in range(2):
                            for k in range(4):
                                c = 4 * hf + k
                                last = nc.tensor.transpose(bank[2 * t + hf][:, k * P:(k + 1) * P],
                                                           x1[:, t, c:D:KT], ident[:, :])
                            last.then_inc(t1_full, 1)

                    group_here(pe, GO)
                    group_here(pe, GO + 1)
                    for t in range(NT):
                        for hf in range(2):
                            w = slot(GO + hf, 512)
                            for k in range(2 * NJ):
                                last = nc.tensor.matmul(bank[2 * t + hf][:, :], mixT[:, k, t * P:(t + 1) * P],
                                                        w[:, k, :], start=(k == 0), stop=(k == 2 * NJ - 1))
                            last.then_inc(wo_full, 1)
                        if t >= 2:
                            tokens(t - 2)
                    def queries(i, cs):
                        w = slot(GQ + i // 4, 512)
                        group_here(pe, GQ + i // 4)
                        for k in range(KT):
                            last = nc.tensor.matmul(bank[i][:, cs], w[:, k, (i % 4) * P:(i % 4 + 1) * P], x1T[:, k, cs],
                                                    start=(k == 0), stop=(k == KT - 1))
                        return last

                    early = slice(0, (NT - 1) * P)
                    tokens(NT - 2)
                    pe.wait_ge(t1_act, 2 * (NT - 1))
                    for i in range(2 * (NT - 1)):
                        queries(i, early)
                    tokens(NT - 1)
                    pe.wait_ge(t1_act, 2 * NT - 1)
                    pe.wait_ge(t1_dve, 1)
                    for i in q_order:
                        queries(i, slice(0, S) if i >= 2 * (NT - 1) else slice((NT - 1) * P, S)).then_inc(qm_full, 1)

                @block.scalar
                def _(act):
                    def tokens(b):
                        t, hf = divmod(b, 2)
                        act.wait_ge(t1_full, b + 1)
                        nc.scalar.activation(x1T[:, 4 * hf:4 * hf + 4, t * P:(t + 1) * P],
                                             bank[b][:, :].rearrange("p (k s) -> p k s", k=4),
                                             ACT.Copy).then_inc(t1_act, 1)

                    for t in range(NT - 1):
                        n1.root(act, t)
                        if t == 2:
                            tokens(0)
                            tokens(1)
                    for b in range(2, 2 * (NT - 1)):
                        tokens(b)
                    n1.root(act, NT - 1)
                    tokens(2 * (NT - 1))
                    for n, i in enumerate(q_order):
                        act.wait_ge(qm_full, n + 1)
                        nc.scalar.activation(qmT[:, i, :], bank[i][:, :], ACT.Copy).then_inc(qm_read, 1)

                @block.vector
                def _(dve):
                    dve.wait_ge(x_back, 64)
                    for t in range(NT):
                        for hf in range(2):
                            dve.wait_ge(wo_full, 2 * t + hf + 1)
                            v = x1[:, t, hf * 512:(hf + 1) * 512]
                            nc.vector.scalar_tensor_tensor(v, v, ALPHA, bank[2 * t + hf][:, :], ALU.mult, ALU.add)\
                                .then_inc(n1.added, 1)
                        n1.statistics(dve, t)
                        n1.scale(dve, t)
                    dve.wait_ge(t1_full, 2 * NT)
                    nc.vector.tensor_copy(x1T[:, 4:8, (NT - 1) * P:S],
                                          bank[2 * NT - 1][:, :].rearrange("p (k s) -> p k s", k=4))\
                        .then_inc(t1_dve, 1)

            omT = xT
            sm = sB("sm", [P, 3, MEM])
            pm = sB("pm", [P, 3, MEM])
            pmT = sB("pmT", [P, 2, MT, S])
            mmx = sB("mmx", [P, MH, NT])
            mnm = sB("mnm", [P, MH, NT])
            mrs = sB("mrs", [P, MH, NT])
            ms_full, ms_max, mp_done, mp_norm = sem("ms_full"), sem("ms_max"), sem("mp_done"), sem("mp_norm")
            mpt_full, mpt_read, mo_full, mo_read = sem("mpt_full"), sem("mpt_read"), sem("mo_full"), sem("mo_read")
            mu_ = [(h, t) for h in range(MH) for t in range(NT)]
            turned = ((bank[2], bank[3]), (bank[4], bank[7]))
            with nc.Block() as block:
                @block.tensor
                def _(pe):
                    def scores(n):
                        h, t = mu_[n]
                        if n >= 2:
                            pe.wait_ge(mp_done, n - 1)
                        for k in range(2):
                            last = nc.tensor.matmul(bank[n % 2][:, 0:MEM], qmT[:, 2 * h + k, t * P:(t + 1) * P],
                                                    kmT[:, 2 * h + k, :], start=(k == 0), stop=(k == 1))
                        last.then_inc(ms_full, 1)

                    def transposed(n):
                        h, t = mu_[n]
                        pe.wait_ge(mp_norm, n + 1)
                        if t == 0 and h >= 2:
                            pe.wait_ge(mpt_read, 2 * h - 2)
                        for m in range(MT):
                            last = nc.tensor.transpose(turned[h % 2][m][:, t * P:(t + 1) * P],
                                                       pm[:, n % 3, m * P:(m + 1) * P], ident[:, :])
                        last.then_inc(mpt_full, 1)

                    def product(h):
                        pe.wait_ge(mpt_read, 2 * h + 2)
                        for i in range(2):
                            if h:
                                pe.wait_ge(mo_read, 2 * h + i - 1)
                            for m in range(MT):
                                c = 2 * h + i
                                last = nc.tensor.matmul(bank[5 + i][:, :], vm[:, m, c * P:(c + 1) * P],
                                                        pmT[:, h % 2, m, :], start=(m == 0), stop=(m == MT - 1))
                            last.then_inc(mo_full, 1)

                    for n in range(len(mu_) + 5):
                        if n < len(mu_):
                            scores(n)
                        if 2 <= n < len(mu_) + 2:
                            transposed(n - 2)
                        if n >= 8 and n % NT == 0:
                            product(n // NT - 2)

                @block.scalar
                def _(act):
                    def out(h):
                        for i in range(2):
                            act.wait_ge(mo_full, 2 * h + i + 1)
                            nc.scalar.activation(omT[:, 2 * h + i, :], bank[5 + i][:, :], ACT.Copy)\
                                .then_inc(mo_read, 1)

                    for n in range(len(mu_) + 3):
                        if n < len(mu_):
                            h, t = mu_[n]
                            act.wait_ge(ms_max, n + 1)
                            if n >= 3:
                                act.wait_ge(mpt_full, n - 2)
                            nc.scalar.activation(pm[:, n % 3, :], bank[n % 2][:, 0:MEM], ACT.Exp,
                                                 bias=mnm[:, h, t:t + 1], scale=MHD ** -0.5,
                                                 accum_out=mrs[:, h, t:t + 1]).then_inc(mp_done, 1)
                        if n >= NT + 2 and (n - NT - 2) % NT == 0:
                            h = (n - NT - 2) // NT
                            for m in range(MT):
                                act.wait_ge(mpt_full, NT * (h + 1))
                                if h >= 2:
                                    act.wait_ge(mo_full, 2 * (h - 1))
                                nc.scalar.activation(pmT[:, h % 2, m, :], turned[h % 2][m][:, :], ACT.Copy)\
                                    .then_inc(mpt_read, 1)
                            if h:
                                out(h - 1)
                    out(MH - 1)

                @block.vector
                def _(dve):
                    def normalised(n):
                        h, t = mu_[n]
                        dve.wait_ge(mp_done, n + 1)
                        link(dve, nc.vector.reciprocal(mrs[:, h, t:t + 1], mrs[:, h, t:t + 1]))
                        nc.vector.tensor_scalar(pm[:, n % 3, :], pm[:, n % 3, :], mrs[:, h, t:t + 1], None,
                                                ALU.mult).then_inc(mp_norm, 1)

                    for n, (h, t) in enumerate(mu_):
                        dve.wait_ge(ms_full, n + 1)
                        link(dve, nc.vector.tensor_reduce(mmx[:, h, t:t + 1], bank[n % 2][:, 0:MEM], AX_X, ALU.max))
                        nc.vector.tensor_scalar(mnm[:, h, t:t + 1], mmx[:, h, t:t + 1], -MHD ** -0.5, None,
                                                ALU.mult).then_inc(ms_max, 1)
                        if n:
                            normalised(n - 1)
                    normalised(len(mu_) - 1)

            x2T = mixT
            wr = sB("wr", [P, KT, NE])
            brb = sB("brb", [P, NE])
            lg = sB("lg", [NE, S])
            aff = sB("aff", [P, NT, NE])
            sel = sB("sel", [P, NT, NE])
            pair = sB("pair", [P, NT, NGRP, 6])
            g8 = sB("g8", [P, 3, NT, NGRP])
            t1c = sB("t1c", [P, 4, NT])
            oh = sB("oh", [P, 3, NT, NE])
            sc3 = sB("sc3", [P, 3, NT, NE])
            rank = sB("rank", [P, NT, NE])
            wsel = sB("wsel", [P, 3, NT])
            dst_f = sB("dst_f", [P, NT, TOP_K])
            dst_i = sB("dst_i", [P, NT, TOP_K], I32)
            ent = sB("ent", [P, NT, TOP_K, 4], I32)
            void = sB("void", [P, S * NE * 4 // P], I32)
            from_last = sB("from_last", [P, NE])
            eidx = sB("eidx", [P, NE])
            before = sB("before", [P, P])
            ones = sB("ones", [P, P])
            xs_rows = nc.dram_tensor("xs_rows", (S, D), F32, kind="Internal").ap()
            table = nc.dram_tensor("table", (S * NE, 4), I32, kind="Internal").ap()
            n2 = Norm(1)
            mo2_full = sem("mo2_full")
            void_done, void_out = sem("void_done"), sem("void_out")
            router_here, xs_out = sem("router_here"), sem("xs_out")
            t2_full, t2_act, t2_dve = sem("t2_full"), sem("t2_act"), sem("t2_dve")
            lg_full, lg_read, lt_full, aff_done = sem("lg_full"), sem("lg_read"), sem("lt_full"), sem("aff_done")
            oh_done, rk_full, ent_done, ent_out = sem("oh_done"), sem("rk_full"), sem("ent_done"), sem("ent_out")
            flat = "p a b -> p (a b)"
            with nc.Block() as block:
                @block.sync
                def _(sp):
                    n2.load(sp)
                    sp.dma_start(wr[:, :, :], w_router.rearrange("(p k) n -> p k n", k=KT)).then_inc(router_here, 16)
                    sp.dma_start(brb[:, :], b_router.rearrange("(a n) -> a n", a=1).to_broadcast([P, NE]))\
                        .then_inc(router_here, 16)
                    sp.wait_ge(void_done, 1)
                    sp.dma_start(table.rearrange("(p r) f -> p (r f)", p=P), void[:, :]).then_inc(void_out, 16)
                    load_expert(sp, 2, 2, 0)
                    load_expert(sp, 1, 1, 2)
                    sp.wait_ge(mo2_full, 8)
                    load_expert(sp, 1, 1, 0)
                    load_expert(sp, 1, 1, 1)
                    for t in range(NT):
                        sp.wait_ge(n2.shifted, t + 1)
                        sp.dma_start(xs_rows[t * P:(t + 1) * P, :], x1[:, t, :]).then_inc(xs_out, 16)
                    load_expert(sp, 2, 2, 1)
                    sp.wait_ge(lg_full, 1)
                    load_expert(sp, 2, 2, 2)
                    sp.wait_ge(xs_out, 64)

                @block.gpsimd
                def _(pool):
                    link(pool, pool.iota(ent[:, :, :, 0], pattern=[[P, NT], [0, TOP_K]], base=0,
                                         channel_multiplier=1))
                    link(pool, pool.iota(ent[:, :, :, 1], pattern=[[P, NT], [S, TOP_K]], base=0,
                                         channel_multiplier=1))
                    link(pool, pool.memset(ent[:, :, :, 2:4], 0))
                    link(pool, pool.iota(from_last[:, :], pattern=[[-1, NE]], base=NE, channel_multiplier=0,
                                         allow_small_or_imprecise_dtypes=True))
                    link(pool, pool.iota(eidx[:, :], pattern=[[1, NE]], base=0, channel_multiplier=0,
                                         allow_small_or_imprecise_dtypes=True))
                    link(pool, pool.iota(thresholds[:, :], pattern=[[CAP, S // CAP - 1]], base=CAP,
                                         channel_multiplier=0, allow_small_or_imprecise_dtypes=True))
                    link(pool, pool.memset(ones[:, :], 1.0))
                    link(pool, pool.affine_select(out=before[:, :], in_=ones[:, :], compare_op=ALU.is_gt,
                                                  fill=0.0, base=0, pattern=[[1, P]], channel_multiplier=-1))
                    pool.memset(void[:, :], OFF).then_inc(void_done, 1)
                    pool.wait_ge(void_done, 1)
                    pool.wait_ge(void_out, 16)
                    pool.wait_ge(ent_done, 1)
                    for t in range(NT):
                        for k in range(TOP_K):
                            pool.indirect_dma_start(table[:, :],
                                                    bass.IndirectOffsetOnAxis(dst_i[:, t, k:k + 1].bitcast(U32), 0),
                                                    ent[:, t, k, :], None).then_inc(ent_out, 16)
                    pool.wait_ge(ent_out, 16 * NT * TOP_K)

                @block.tensor
                def _(pe):
                    def tokens(t):
                        pe.wait_ge(n2.shifted, t + 1)
                        for hf in range(2):
                            for k in range(4):
                                c = 4 * hf + k
                                last = nc.tensor.transpose(bank[2 * t + hf][:, k * P:(k + 1) * P],
                                                           x1[:, t, c:D:KT], ident[:, :])
                            last.then_inc(t2_full, 1)

                    def logits(t):
                        for k in range(KT):
                            last = nc.tensor.matmul(bank[0][0:NE, t * P:(t + 1) * P], wr[:, k, :],
                                                    x2T[:, k, t * P:(t + 1) * P], start=(k == 0), stop=(k == KT - 1))
                        return last

                    group_here(pe, GMO)
                    group_here(pe, GMO + 1)
                    for t in range(NT):
                        for hf in range(2):
                            w = slot(GMO + hf, 512)
                            for k in range(KT):
                                last = nc.tensor.matmul(bank[2 * t + hf][:, :], omT[:, k, t * P:(t + 1) * P],
                                                        w[:, k, :], start=(k == 0), stop=(k == KT - 1))
                            last.then_inc(mo2_full, 1)
                        if t >= 2:
                            tokens(t - 2)
                    tokens(NT - 2)
                    pe.wait_ge(router_here, 32)
                    for t in range(NT - 1):
                        pe.wait_ge(t2_act, 2 * t + 2)
                        logits(t)
                    tokens(NT - 1)
                    pe.wait_ge(t2_act, 2 * NT - 1)
                    pe.wait_ge(t2_dve, 1)
                    last = logits(NT - 1)
                    last.then_inc(lg_full, 1)
                    pe.wait_ge(lg_read, 1)
                    for t in range(NT):
                        last = nc.tensor.transpose(bank[1][:, t * NE:(t + 1) * NE], lg[:, t * P:(t + 1) * P],
                                                   ident[0:NE, 0:NE])
                    last.then_inc(lt_full, 1)
                    pe.wait_ge(oh_done, 1)
                    nc.tensor.matmul(bank[2][:, 0:P], before[:, :], oh[:, 2, :, :], start=True, stop=True)
                    nc.tensor.matmul(bank[2][:, P:2 * P], ones[:, :], oh[:, 2, :, :], start=True, stop=True)\
                        .then_inc(rk_full, 1)

                @block.scalar
                def _(act):
                    def tokens(b):
                        t, hf = divmod(b, 2)
                        act.wait_ge(t2_full, b + 1)
                        nc.scalar.activation(x2T[:, 4 * hf:4 * hf + 4, t * P:(t + 1) * P],
                                             bank[b][:, :].rearrange("p (k s) -> p k s", k=4),
                                             ACT.Copy).then_inc(t2_act, 1)

                    for t in range(NT - 1):
                        n2.root(act, t)
                        if t == 2:
                            tokens(0)
                            tokens(1)
                    for b in range(2, 2 * (NT - 1)):
                        tokens(b)
                    n2.root(act, NT - 1)
                    tokens(2 * (NT - 1))
                    act.wait_ge(lt_full, 1)
                    nc.scalar.activation(aff[:, :, :], bank[1][:, 0:NT * NE].rearrange("p (t e) -> p t e", t=NT),
                                         ACT.Sigmoid).then_inc(aff_done, 1)

                @block.vector
                def _(dve):
                    for t in range(NT):
                        for hf in range(2):
                            dve.wait_ge(mo2_full, 2 * t + hf + 1)
                            v = x1[:, t, hf * 512:(hf + 1) * 512]
                            nc.vector.scalar_tensor_tensor(v, v, ALPHA, bank[2 * t + hf][:, :], ALU.mult, ALU.add)\
                                .then_inc(n2.added, 1)
                        n2.statistics(dve, t)
                        n2.scale(dve, t)
                    dve.wait_ge(t2_full, 2 * NT)
                    nc.vector.tensor_copy(x2T[:, 4:8, (NT - 1) * P:S],
                                          bank[2 * NT - 1][:, :].rearrange("p (k s) -> p k s", k=4))\
                        .then_inc(t2_dve, 1)
                    dve.wait_ge(lg_full, 1)
                    nc.vector.tensor_copy(lg[:, :], bank[0][0:NE, :]).then_inc(lg_read, 1)
                    dve.wait_ge(aff_done, 1)
                    dve.wait_ge(void_done, 1)
                    V = nc.vector
                    link(dve, V.tensor_tensor(sel[:, :, :], aff[:, :, :], brb[:, :].unsqueeze(1)
                                              .to_broadcast([P, NT, NE]), ALU.add))
                    s4 = sel[:, :, :].rearrange("p t (g i) -> p (t g) i", i=EPG)
                    pr6 = pair[:, :, :, :].rearrange("p t g i -> p (t g) i")
                    V.tensor_tensor(pr6[:, :, 0:3], s4[:, :, 0:3], s4[:, :, 1:4], ALU.add)
                    V.tensor_tensor(pr6[:, :, 3:5], s4[:, :, 0:2], s4[:, :, 2:4], ALU.add)
                    link(dve, V.tensor_tensor(pr6[:, :, 5:6], s4[:, :, 0:1], s4[:, :, 3:4], ALU.add))
                    grp, geq, gsel = (g8[:, i, :, :] for i in range(3))
                    link(dve, V.tensor_reduce(grp, pair[:, :, :, :], AX_X, ALU.max))

                    def first_largest(values, n, tmp_, onehot, wts, m):
                        shape = [P, NT, n]
                        link(dve, V.tensor_reduce(m, values, AX_X, ALU.max))
                        link(dve, V.tensor_tensor(tmp_, values, m.unsqueeze(2).to_broadcast(shape), ALU.is_equal))
                        link(dve, V.tensor_tensor(tmp_, tmp_, wts.unsqueeze(1).to_broadcast(shape), ALU.mult))
                        link(dve, V.tensor_reduce(m, tmp_, AX_X, ALU.max))
                        link(dve, V.tensor_tensor(onehot, tmp_, m.unsqueeze(2).to_broadcast(shape), ALU.is_equal))

                    first_largest(grp, NGRP, geq, gsel, from_last[:, NE - NGRP:NE], t1c[:, 0, :])
                    out_, masked, tmp_ = (sc3[:, i, :, :] for i in range(3))
                    gb = gsel.rearrange("p t g -> p (t g)").unsqueeze(2).to_broadcast([P, NT * NGRP, EPG])
                    as4 = lambda v: v.rearrange("p t (g i) -> p (t g) i", i=EPG)
                    link(dve, V.tensor_scalar(as4(out_), gb, 1.0, -NEG, ALU.subtract, ALU.mult))
                    link(dve, V.tensor_tensor(as4(masked), as4(sel[:, :, :]), gb, ALU.mult))
                    link(dve, V.tensor_tensor(masked, masked, out_, ALU.add))
                    first_largest(masked, NE, tmp_, oh[:, 0, :, :], from_last[:, :], t1c[:, 1, :])
                    link(dve, V.scalar_tensor_tensor(masked, oh[:, 0, :, :], 3 * NEG, masked, ALU.mult, ALU.add))
                    first_largest(masked, NE, tmp_, oh[:, 1, :, :], from_last[:, :], t1c[:, 2, :])
                    V.tensor_tensor(oh[:, 2, :, :], oh[:, 0, :, :], oh[:, 1, :, :], ALU.add).then_inc(oh_done, 1)
                    for k in range(TOP_K):
                        link(dve, V.tensor_tensor(tmp_, oh[:, k, :, :], aff[:, :, :], ALU.mult))
                        link(dve, V.tensor_reduce(wsel[:, k, :], tmp_, AX_X, ALU.add))
                    link(dve, V.tensor_tensor(wsel[:, 2, :], wsel[:, 0, :], wsel[:, 1, :], ALU.add))
                    link(dve, V.reciprocal(wsel[:, 2, :], wsel[:, 2, :]))
                    for k in range(TOP_K):
                        V.tensor_tensor(ent[:, :, k, 2].bitcast(F32), wsel[:, k, :], wsel[:, 2, :], ALU.mult)
                    dve.wait_ge(rk_full, 1)
                    cum = bank[2][:, 0:P].rearrange("p (t e) -> p t e", t=NT)
                    tot = bank[2][:, P:2 * P].rearrange("p (t e) -> p t e", t=NT)
                    offs = sc3[:, 0, :, :]
                    link(dve, V.memset(offs[:, 0, :], 0.0))
                    for t in range(1, NT):
                        link(dve, V.tensor_tensor(offs[:, t, :], tot[:, t - 1, :], offs[:, t - 1, :], ALU.add))
                    link(dve, V.tensor_tensor(rank[:, :, :], cum, offs, ALU.add))
                    link(dve, V.tensor_scalar(rank[:, :, :], rank[:, :, :], float(NE), None, ALU.mult))
                    link(dve, V.tensor_tensor(rank[:, :, :], rank[:, :, :], eidx[:, :].unsqueeze(1)
                                              .to_broadcast([P, NT, NE]), ALU.add))
                    for k in range(TOP_K):
                        link(dve, V.tensor_tensor(tmp_, oh[:, k, :, :], rank[:, :, :], ALU.mult))
                        link(dve, V.tensor_reduce(dst_f[:, :, k:k + 1], tmp_, AX_X, ALU.add))
                    V.tensor_copy(dst_i[:, :, :], dst_f[:, :, :]).then_inc(ent_done, 1)
                    link(dve, V.tensor_tensor(counts[:, :], tot[:, NT - 1, :], offs[:, NT - 1, :], ALU.add))
                    link(dve, V.tensor_reduce(most_f[:, :], counts[:, :], AX_X, ALU.max))
                    link(dve, V.tensor_scalar(blk_f[:, :], thresholds[:, :], most_f[:, 0:1], None, ALU.is_lt))
                    link(dve, V.tensor_reduce(most_f[:, :], blk_f[:, :], AX_X, ALU.add))
                    link(dve, V.tensor_copy(more_i[:, :], most_f[:, :]))

        NR = (NE - 2) // 3
        USES = (NR + 1, NR + 1, NR)
        tabs = sb("tabs", [P, NE, 4], I32)
        halfp = sb("halfp", [P, 3])
        tokc = sb("tokc", [P, 3, 1], I32)
        rowc = sb("rowc", [P, 3, 1], I32)
        gatec = sb("gatec", [P, 3, 1])
        xg = sb("xg", [CAP, 3, D])
        xgT = sb("xgT", [P, KT, CAP])
        sil = sb("sil", [CAP, 3, DE])
        hb = sb("hb", [CAP, 3, DE])
        hT = sb("hT", [P, FT, CAP])
        ye = sb("ye", [P, 3, DE])
        y_rows = nc.dram_tensor("y_rows", (TOP_K * S * 2, D // 2), F32, kind="Internal").ap()
        table_v = table.rearrange("(r e) f -> r e f", e=NE)
        n3 = Norm(2)
        tabs_here, tabs_done, xg_zero = sem("tabs_here"), sem("tabs_done"), sem("xg_zero")
        y_read, y_sum = [sem(f"y_read{i}") for i in range(NT)], sem("y_sum")
        out_done = sem("out_done")
        xg_here = [sem(f"xg_here{s}") for s in range(3)]
        y_out = [sem(f"y_out{s}") for s in range(3)]
        xgt_full, xgt_read = sem("xgt_full"), sem("xgt_read")
        gu_full, sil_done, h_done = sem("gu_full"), sem("sil_done"), sem("h_done")
        ht_full, ht_read, y_full, y_scaled = sem("ht_full"), sem("ht_read"), sem("y_full"), sem("y_scaled")
        gate_col, tokc_done, rowc_done = sem("gate_col"), sem("tokc_done"), sem("rowc_done")
        both = (0, 1)

        def at(blk, r, k):
            if isinstance(r, int) and not 0 <= 2 + 3 * r + k < NE:
                return None
            s = (2, 0, 1)[k % 3]
            e = 3 * r + (2 + k)
            return e, blk * NE + e, s, blk * USES[s] + r + (k // 3 + (k % 3 > 0))

        def for_steps(eng, blk, step, peeled=0):
            step(0, -2)
            step(0, -1)
            for r in range(peeled):
                for k in range(3):
                    step(r, k)
            with eng.Fori(peeled, NR - 1) as r:
                for k in range(3):
                    step(r, k)
            for k in range(3):
                step(NR - 1, k)

        def further_blocks(eng, body):
            n = eng.value_load(more_i[0:1, 0:1], min_val=0, max_val=S // CAP - 1)
            with eng.If(n > 0):
                with eng.Fori(1, n + 1) as blk:
                    body(blk)

        with nc.Block() as block:
            @block.sync
            def _(sp):
                def table_in(blk):
                    for h in both:
                        sp.dma_start(tabs[h * CAP:(h + 1) * CAP, :, :], table_v[bass.ds(blk * CAP, CAP), :, :]
                                     ).then_inc(tabs_here, 16)

                def weights(now, before=None, used=2):
                    e, n, s, c = now
                    sp.wait_ge(gu_full, n - used)
                    if before:
                        sp.wait_ge(up_in[before[2]], 16 * (before[3] + 1))
                    load_expert(sp, e, s, 0)
                    if before:
                        sp.wait_ge(down_here[before[2]], 16 * (before[3] + 1))
                    load_expert(sp, e, s, 1)
                    sp.wait_ge(y_full, n - used)
                    sp.wait_ge(gate_here[s], 16 * (c + 1))
                    load_expert(sp, e, s, 2)

                def later_weights(blk):
                    with sp.Fori(0, NR - 1) as r:
                        for k in (1, 2, 3):
                            weights(at(blk, r, k), at(blk, r, k - 1))
                    for k in (1, 2):
                        weights(at(blk, NR - 1, k), at(blk, NR - 1, k - 1))

                table_in(0)
                n3.load(sp)
                later_weights(0)

                def block_(blk):
                    sp.wait_ge(gate_col, NE * blk)
                    table_in(blk)
                    for k in (-2, -1, 0):
                        weights(at(blk, 0, k), used=0)
                    later_weights(blk)

                further_blocks(sp, block_)

            @block.gpsimd
            def _(pool):
                link(pool, pool.memset(halfp[0:CAP, 0:2], 0.0))
                link(pool, pool.memset(halfp[CAP:P, 0:1], 1.0))
                link(pool, pool.memset(halfp[CAP:P, 1:2], 0.0))
                link(pool, pool.memset(halfp[:, 2:3], 1.0))
                pool.memset(xg[:, :, :], 0.0).then_inc(xg_zero, 1)
                zero_i, one_f = halfp[:, 1:2].bitcast(I32), halfp[:, 2:3]
                limit = pool.alloc_register(name="limit")
                limits = pool.alloc_register(name="limits")
                pool.reg_mov(limits, 0)

                def below(rows):
                    pool.reg_add(limit, limits, rows - 1)
                    return limit

                pool.wait_ge(xg_zero, 1)

                def gather(e, n, s, c, used=2):
                    if not (isinstance(n, int) and n < 3):
                        pool.wait_ge(xgt_full, n - used)
                    pool.tensor_tensor(tokc[:, s, :], tabs[:, e, 0:1], zero_i, ALU.add).then_inc(tokc_done, 1)
                    pool.wait_ge(tokc_done, n + 1)
                    pool.indirect_dma_start(xg[:, s, :], None, xs_rows[:, :],
                                            bass.IndirectOffsetOnAxis(tokc[0:CAP, s, :].bitcast(U32), 0),
                                            bounds_check=below(S), oob_is_err=False).then_inc(xg_here[s], 16)

                def scatter(e, n, s, c):
                    if not (isinstance(c, int) and c == 0):
                        pool.wait_ge(y_out[s], 16 * c)
                    pool.tensor_tensor(rowc[:, s, :], tabs[:, e, 1:2], zero_i, ALU.add).then_inc(rowc_done, 1)
                    pool.wait_ge(rowc_done, n + 1)
                    pool.tensor_tensor(gatec[:, s, :], tabs[:, e, 2:3].bitcast(F32), one_f, ALU.mult)\
                        .then_inc(gate_col, 1)
                    pool.wait_ge(y_scaled, n + 1)
                    pool.indirect_dma_start(y_rows[:, :], bass.IndirectOffsetOnAxis(rowc[:, s, :].bitcast(U32), 0),
                                            ye[:, s, :], None, bounds_check=below(TOP_K * S * 2), oob_is_err=False)\
                        .then_inc(y_out[s], 16)

                def rows_through(blk, peeled=0):
                    gather(*at(blk, 0, -2), used=1)
                    gather(*at(blk, 0, -1), used=1)

                    def step(r, k):
                        if at(blk, r, k + 2):
                            gather(*at(blk, r, k + 2))
                        scatter(*at(blk, r, k))

                    for_steps(pool, blk, step, peeled)

                pool.wait_ge(tabs_done, 1)
                rows_through(0, peeled=1)

                def block_(blk):
                    pool.wait_ge(tabs_done, blk + 1)
                    rows_through(blk)

                further_blocks(pool, block_)
                for s in range(3):
                    pool.wait_ge(y_out[s], 16 * USES[s])

            @block.tensor
            def _(pe):
                def turn(dst, src, first):
                    if first:
                        return nc.tensor.matmul(dst, src, ident[0:CAP, 0:CAP], start=True, stop=True)
                    return nc.tensor.transpose(dst, src, ident[0:CAP, 0:CAP])

                def tokens(e, n, s, c):
                    pe.wait_ge(xg_here[s], 16 * (c + 1))
                    for k in range(KT):
                        last = turn(bank[0][:, k * CAP:(k + 1) * CAP], xg[:, s, k:D:KT], k == 0)
                    last.then_inc(xgt_full, 1)

                def gate_up(e, n, s, c):
                    pe.wait_ge(xgt_read, n + 1)
                    pe.wait_ge(gate_here[s], 16 * (c + 1))
                    pe.wait_ge(up_in[s], 16 * (c + 1))
                    for k in range(KT):
                        for m in both:
                            last = nc.tensor.matmul(bank[1 + s][m * CAP:(m + 1) * CAP, :], xgT[:, k, :],
                                                    expert_slot(s, m)[:, k * DE:(k + 1) * DE],
                                                    start=(k == 0), stop=(k == KT - 1))
                    last.then_inc(gu_full, 1)

                def down(e, n, s, c):
                    pe.wait_ge(h_done, n + 1)
                    for k in range(FT):
                        last = turn(bank[4][:, k * CAP:(k + 1) * CAP], hb[:, s, k:DE:FT], k == 0)
                    last.then_inc(ht_full, 1)
                    pe.wait_ge(ht_read, n + 1)
                    pe.wait_ge(down_here[s], 16 * (c + 1))
                    if not (isinstance(n, int) and n == 0):
                        pe.wait_ge(y_scaled, n)
                    for k in range(FT):
                        for m in both:
                            o = k * D + m * 512
                            last = nc.tensor.matmul(bank[5][m * CAP:(m + 1) * CAP, :], hT[:, k, :],
                                                    expert_slot(s, 2)[:, o:o + 512],
                                                    start=(k == 0), stop=(k == FT - 1))
                    last.then_inc(y_full, 1)

                def products(blk):
                    tokens(*at(blk, 0, -2))

                    def step(r, k):
                        gate_up(*at(blk, r, k))
                        if at(blk, r, k + 1):
                            tokens(*at(blk, r, k + 1))
                        down(*at(blk, r, k))

                    for_steps(pe, blk, step)

                products(0)
                further_blocks(pe, products)

            @block.scalar
            def _(act):
                def tokens(e, n, s, c):
                    act.wait_ge(xgt_full, n + 1)
                    nc.scalar.activation(xgT[:, :, :].rearrange("p k c -> p (k c)"), bank[0][:, :], ACT.Copy)\
                        .then_inc(xgt_read, 1)

                def silu(e, n, s, c):
                    act.wait_ge(gu_full, n + 1)
                    nc.scalar.activation(sil[:, s, :], bank[1 + s][0:CAP, :], ACT.Silu).then_inc(sil_done, 1)

                def scaled(e, n, s, c):
                    act.wait_ge(y_full, n + 1)
                    act.wait_ge(gate_col, n + 1)
                    nc.scalar.activation(ye[:, s, :], bank[5][:, :], ACT.Copy, scale=gatec[:, s, :])\
                        .then_inc(y_scaled, 1)

                def activations(blk):
                    tokens(*at(blk, 0, -2))

                    def step(r, k):
                        silu(*at(blk, r, k))
                        if at(blk, r, k + 1):
                            tokens(*at(blk, r, k + 1))
                        scaled(*at(blk, r, k))

                    for_steps(act, blk, step)

                activations(0)
                further_blocks(act, activations)

            @block.vector
            def _(dve):
                def rows_of(blk):
                    dve.wait_ge(tabs_here, 32 * (blk + 1))
                    nc.vector.tensor_scalar(tabs[:, :, 1], tabs[:, :, 1], 2.0, halfp[:, 0:1], ALU.mult, ALU.add)\
                        .then_inc(tabs_done, 1)

                def hidden(e, n, s, c):
                    dve.wait_ge(sil_done, n + 1)
                    nc.vector.tensor_tensor(hb[:, s, :], bank[1 + s][CAP:P, :], sil[:, s, :], ALU.mult)\
                        .then_inc(h_done, 1)

                def turned(e, n, s, c):
                    dve.wait_ge(ht_full, n + 1)
                    nc.vector.tensor_copy(hT[:, :, :].rearrange("p k c -> p (k c)"),
                                          bank[4][:, 0:FT * CAP]).then_inc(ht_read, 1)

                def hiddens(blk):
                    rows_of(blk)

                    def step(r, k):
                        hidden(*at(blk, r, k))
                        turned(*at(blk, r, k))

                    for_steps(dve, blk, step)

                dve.wait_ge(xg_zero, 1)
                hiddens(0)
                further_blocks(dve, hiddens)

        yb = ring[:, 0:NT * 2 * D].rearrange("p (t k d) -> p t k d", t=NT, k=TOP_K)
        y_v = y_rows.rearrange("(k t h) c -> t k (h c)", k=TOP_K, h=2)
        with nc.Block() as block:
            @block.sync
            def _(sp):
                for t in range(NT):
                    sp.dma_start(yb[:, t, :, :], y_v[t * P:(t + 1) * P, :, :]).then_inc(y_read[t], 16)
                for t in range(NT):
                    sp.wait_ge(n3.shifted, t + 1)
                    sp.dma_start(out[0, t * P:(t + 1) * P, :], x1[:, t, :]).then_inc(out_done, 16)
                sp.wait_ge(out_done, 16 * NT)

            @block.gpsimd
            def _(pool):
                for t in range(1, NT):
                    pool.wait_ge(y_read[t], 16)
                    pool.tensor_tensor(yb[:, t, 0, :], yb[:, t, 0, :], yb[:, t, 1, :], ALU.add).then_inc(y_sum, 1)
                    pool.wait_ge(y_sum, t)

            @block.scalar
            def _(act):
                for t in range(NT):
                    n3.root(act, t)

            @block.vector
            def _(dve):
                for t in range(NT):
                    if t:
                        dve.wait_ge(y_sum, t)
                    else:
                        dve.wait_ge(y_read[0], 16)
                        link(dve, nc.vector.tensor_tensor(yb[:, 0, 0, :], yb[:, 0, 0, :], yb[:, 0, 1, :], ALU.add))
                    for hf in range(2):
                        v = slice(hf * 512, (hf + 1) * 512)
                        nc.vector.scalar_tensor_tensor(x1[:, t, v], x1[:, t, v], ALPHA, yb[:, t, 0, v],
                                                       ALU.mult, ALU.add).then_inc(n3.added, 1)
                    n3.statistics(dve, t)
                    n3.scale(dve, t)


_INS = ["x", "mem", "w_in", "mu_shift", "w0", "w_decay_up", "a0", "w_iclr_up", "w_gate_up", "k_k", "k_a", "r_k",
        "lnx_g", "lnx_b", "attn_out_g", "w_out", "w_mem_q", "w_mem_kv", "w_mem_o", "w_router", "b_router",
        "w_exp_gate", "w_exp_up", "w_exp_down", "ln_g", "ln_b"]


def kernel(**inputs):
    import numpy as np
    import concourse.bacc as bacc
    from concourse.bass_utils import run_bass_kernel_spmd

    nc = bacc.Bacc("TRN2", target_bir_lowering=False, num_devices=1)
    arrays, args = {}, []
    for name in _INS:
        a = np.ascontiguousarray(inputs[name])
        arrays[f"in_{name}"] = a
        args.append(nc.dram_tensor(f"in_{name}", a.shape, mybir.dt.from_np(a.dtype), kind="ExternalInput").ap())
    out = nc.dram_tensor("out_0", (1, S, D), F32, kind="ExternalOutput").ap()
    hybrid_decoder_trunk(nc, *args, out)
    result = run_bass_kernel_spmd(nc, [arrays], core_ids=[0])
    return result.results[0]["out_0"]
```
